# Optimizing a Trainium2 kernel written in Bass

```python
import math
import jax
import jax.numpy as jnp
from jax import lax
import numpy as np

D_MODEL = 1024
BATCH = 1
SEQ = 512
DEPTH = 2

GRID_W = 64
CTX_LEN = 256
N_MIXERS = 4
RMS_EPS = 1e-6
D_FF = 4 * D_MODEL

GA_HEAD_DIM = 128
GA_N_HEADS = D_MODEL // GA_HEAD_DIM
GA_N_KV = 2
GA_GROUP = GA_N_HEADS // GA_N_KV
ROPE_THETA = 10000.0
Q_BLOCK = 128

HY_ORDER = 2
HY_SHORT = 3
HY_FILTER_HIDDEN = 64
HY_BANDS = 16
HY_EMB = 1 + 2 * HY_BANDS
HY_DECAY_SHORT = 0.3
HY_DECAY_LONG = 1.5
HY_TARGET = 1e-2

SSM_D_INNER = 2 * D_MODEL
SSM_HEAD_DIM = 64
SSM_N_HEADS = SSM_D_INNER // SSM_HEAD_DIM
SSM_GROUPS = 4
SSM_D_STATE = 128
SSM_CONV = 3
SSM_CHUNK = 128
SSM_GN = SSM_GROUPS * SSM_D_STATE
SSM_IN_DIM = 2 * SSM_D_INNER + 2 * SSM_GN + 2 * SSM_N_HEADS

NA_HEAD_DIM = 64
NA_N_HEADS = D_MODEL // NA_HEAD_DIM
NA_KH = 8
NA_KW = 16

kernel_name = 'hybrid_dit_interleaved_prefix_ctx'

def rmsnorm(x, g):
    xf = x.astype(jnp.float32)
    y = xf * lax.rsqrt(jnp.mean(xf * xf, axis=-1, keepdims=True) + RMS_EPS)
    return (y * g.astype(jnp.float32)).astype(x.dtype)

def modulate(h, shift, scale):
    return h * (1 + scale) + shift

def sq_relu_mlp(h, w1, w2):
    return jnp.square(jax.nn.relu(h @ w1)) @ w2

def dwconv_centred(u, w, b):
    k, ch = w.shape
    y = lax.conv_general_dilated(u, w[:, None, :].astype(u.dtype), window_strides=(1,),
                                 padding=[(k // 2, k // 2)],
                                 dimension_numbers=('NWC', 'WIO', 'NWC'), feature_group_count=ch)
    return y + b

def axial_rope_tables(n_tokens, head_dim):
    t = jnp.arange(n_tokens)
    row = (t // GRID_W).astype(jnp.float32)
    col = (t % GRID_W).astype(jnp.float32)
    nf = head_dim // 4
    inv = ROPE_THETA ** (-jnp.arange(nf, dtype=jnp.float32) / nf)
    ar = row[:, None] * inv[None, :]
    ac = col[:, None] * inv[None, :]
    cos = jnp.concatenate([jnp.cos(ar), jnp.cos(ar), jnp.cos(ac), jnp.cos(ac)], axis=-1)
    sin = jnp.concatenate([jnp.sin(ar), jnp.sin(ar), jnp.sin(ac), jnp.sin(ac)], axis=-1)
    return cos, sin

def apply_rope(x, cos, sin):
    shape = (x.shape[1],) + (1,) * (x.ndim - 3) + (x.shape[-1],)
    cos = cos.reshape(shape)
    sin = sin.reshape(shape)
    a, b, c, d = jnp.split(x, 4, axis=-1)
    rot = jnp.concatenate([-b, a, -d, c], axis=-1)
    return (x * cos + rot * sin).astype(x.dtype)

def gqa_attend(q, k, v):
    s = jnp.einsum('bqkgd,bskd->bkgqs', q, k).astype(jnp.float32) * (q.shape[-1] ** -0.5)
    p = jax.nn.softmax(s, axis=-1).astype(v.dtype)
    return jnp.einsum('bkgqs,bskd->bqkgd', p, v)

def mha(q, k, v):
    s = jnp.einsum('bqhd,bshd->bhqs', q, k).astype(jnp.float32) * (q.shape[-1] ** -0.5)
    p = jax.nn.softmax(s, axis=-1).astype(v.dtype)
    return jnp.einsum('bhqs,bshd->bqhd', p, v)

def mixer_gqa(h_lat, h_ctx, w_in, q_gain, k_gain, w_out, with_ctx_out):
    bsz, n_lat, _ = h_lat.shape
    hd = GA_HEAD_DIM

    def qkv(h):
        n = h.shape[1]
        q, k, v = jnp.split(h @ w_in, [GA_N_HEADS * hd, (GA_N_HEADS + GA_N_KV) * hd], axis=-1)
        q = rmsnorm(q.reshape(bsz, n, GA_N_KV, GA_GROUP, hd), q_gain)
        k = rmsnorm(k.reshape(bsz, n, GA_N_KV, hd), k_gain)
        return q, k, v.reshape(bsz, n, GA_N_KV, hd)

    q_l, k_l, v_l = qkv(h_lat)
    q_c, k_c, v_c = qkv(h_ctx)
    cos, sin = axial_rope_tables(n_lat, hd)
    q_l = apply_rope(q_l, cos, sin)
    k_l = apply_rope(k_l, cos, sin)
    k_all = jnp.concatenate([k_l, k_c], axis=1)
    v_all = jnp.concatenate([v_l, v_c], axis=1)
    nb = n_lat // Q_BLOCK
    qb = q_l.reshape(bsz, nb, Q_BLOCK, GA_N_KV, GA_GROUP, hd).swapaxes(0, 1)
    o = lax.map(lambda qblk: gqa_attend(qblk, k_all, v_all), qb)
    y_lat = o.swapaxes(0, 1).reshape(bsz, n_lat, GA_N_HEADS * hd) @ w_out
    y_ctx = None
    if with_ctx_out:
        y_ctx = gqa_attend(q_c, k_c, v_c).reshape(bsz, -1, GA_N_HEADS * hd) @ w_out
    return y_lat, y_ctx

def hyena_filters(n, w1, b1, w2, b2, w3, freq):
    t = jnp.linspace(0.0, 1.0, n, dtype=jnp.float32)[:, None]
    w = 2.0 * math.pi * jnp.arange(n, dtype=jnp.float32)[:, None] / n
    bands = jnp.linspace(1e-4, HY_BANDS - 1, HY_BANDS, dtype=jnp.float32)[None, :]
    feats = jnp.concatenate([t, jnp.cos(bands * w), -jnp.sin(bands * w)], axis=-1)
    h = jnp.sin(freq[0] * (feats @ w1 + b1))
    h = jnp.sin(freq[1] * (h @ w2 + b2))
    h = (h @ w3).astype(jnp.float32).reshape(n, 2 * HY_ORDER, D_MODEL)
    deltas = jnp.abs(jnp.linspace(math.log(HY_TARGET) / HY_DECAY_SHORT,
                                  math.log(HY_TARGET) / HY_DECAY_LONG, D_MODEL, dtype=jnp.float32))
    return h * jnp.exp(-t * deltas[None, :])[:, None, :]

def bidir_long_conv(z, h_fwd, h_bwd, skip):
    n = z.shape[1]
    filt_full = jnp.concatenate([h_fwd, jnp.zeros_like(h_fwd[:1]), h_bwd[:0:-1]], axis=0)
    zf = jnp.fft.rfft(z.astype(jnp.float32), n=2 * n, axis=1)
    ff = jnp.fft.rfft(filt_full, n=2 * n, axis=0)
    y = jnp.fft.irfft(zf * ff[None], n=2 * n, axis=1)[:, :n]
    return (y + z.astype(jnp.float32) * skip.astype(jnp.float32)).astype(z.dtype)

def mixer_hyena(h_lat, h_ctx, w_in, conv_w, conv_b, f_w1, f_b1, f_w2, f_b2, f_w3, f_freq, skip, w_out,
                with_ctx_out):
    def run(h):
        u = dwconv_centred(h @ w_in, conv_w, conv_b)
        v, x1, x2 = jnp.split(u, HY_ORDER + 1, axis=-1)
        filt = hyena_filters(h.shape[1], f_w1, f_b1, f_w2, f_b2, f_w3, f_freq)
        z = x1 * bidir_long_conv(v, filt[:, 0], filt[:, 1], skip[0])
        z = x2 * bidir_long_conv(z, filt[:, 2], filt[:, 3], skip[1])
        return z @ w_out

    y_ctx = run(h_ctx) if with_ctx_out else None
    return run(h_lat), y_ctx

def segsum_exp(a_cs):
    t = a_cs.shape[-1]
    diff = a_cs[..., :, None] - a_cs[..., None, :]
    return jnp.where(jnp.tril(jnp.ones((t, t), bool)), jnp.exp(jnp.minimum(diff, 0.0)), 0.0)

def ssd_scan(xs, dt, a, bm, cm, init_state):
    bsz, n, nh, p = xs.shape
    g, ns = bm.shape[2], bm.shape[3]
    e = nh // g
    nc = n // SSM_CHUNK
    x = (xs.astype(jnp.float32) * dt[..., None]).reshape(bsz, nc, SSM_CHUNK, g, e, p)
    da = (dt * a).reshape(bsz, nc, SSM_CHUNK, g, e).transpose(0, 3, 4, 1, 2)
    bc = bm.astype(jnp.float32).reshape(bsz, nc, SSM_CHUNK, g, ns)
    cc = cm.astype(jnp.float32).reshape(bsz, nc, SSM_CHUNK, g, ns)
    a_cs = jnp.cumsum(da, axis=-1)
    lmat = segsum_exp(a_cs)
    cb = jnp.einsum('bclgn,bcsgn->bgcls', cc, bc)
    y_diag = jnp.einsum('bgcls,bgecls,bcsgep->bclgep', cb, lmat, x)
    decay_states = jnp.exp(a_cs[..., -1:] - a_cs)
    states = jnp.einsum('bcsgn,bgecs,bcsgep->bcgepn', bc, decay_states, x)
    init = init_state.astype(jnp.float32).reshape(bsz, 1, g, e, p, ns)
    states = jnp.concatenate([init, states], axis=1)
    totals = jnp.pad(a_cs[..., -1], ((0, 0), (0, 0), (0, 0), (1, 0)))
    chunk_decay = segsum_exp(jnp.cumsum(totals, axis=-1))
    new_states = jnp.einsum('bgezc,bcgepn->bzgepn', chunk_decay, states)
    states, final = new_states[:, :-1], new_states[:, -1]
    y_off = jnp.einsum('bclgn,bcgepn,bgecl->bclgep', cc, states, jnp.exp(a_cs))
    y = (y_diag + y_off).reshape(bsz, n, nh, p)
    return y, final.reshape(bsz, nh, p, ns)

def mixer_ssd(h_lat, h_ctx, w_in, conv_w, conv_b, dt_bias, a_log, d_skip, norm_g, w_out, with_ctx_out):
    bsz = h_lat.shape[0]

    def prep(h):
        n = h.shape[1]
        z, xbc, dt = jnp.split(h @ w_in, [SSM_D_INNER, 2 * SSM_D_INNER + 2 * SSM_GN], axis=-1)
        xbc = jax.nn.silu(dwconv_centred(xbc, conv_w, conv_b))
        xs, bm, cm = jnp.split(xbc, [SSM_D_INNER, SSM_D_INNER + SSM_GN], axis=-1)
        xs = xs.reshape(bsz, n, SSM_N_HEADS, SSM_HEAD_DIM)
        bm = bm.reshape(bsz, n, SSM_GROUPS, SSM_D_STATE)
        cm = cm.reshape(bsz, n, SSM_GROUPS, SSM_D_STATE)
        dt = jax.nn.softplus(dt.astype(jnp.float32).reshape(bsz, n, 2, SSM_N_HEADS)
                             + dt_bias.astype(jnp.float32))
        return z, xs, bm, cm, dt

    a = -jnp.exp(a_log.astype(jnp.float32))

    def bidir(xs, bm, cm, dt, s_f, s_b):
        y_f, fin_f = ssd_scan(xs, dt[:, :, 0], a[0], bm, cm, s_f)
        y_b, fin_b = ssd_scan(xs[:, ::-1], dt[:, ::-1, 1], a[1], bm[:, ::-1], cm[:, ::-1], s_b)
        return y_f + y_b[:, ::-1], fin_f, fin_b

    def out(z, xs, y):
        n = xs.shape[1]
        y = (y + xs.astype(jnp.float32) * d_skip.astype(jnp.float32)[:, None]).reshape(bsz, n, SSM_D_INNER)
        y = rmsnorm(y * jax.nn.silu(z.astype(jnp.float32)), norm_g).astype(z.dtype)
        return y @ w_out

    zc, xc, bcm, ccm, dtc = prep(h_ctx)
    zero = jnp.zeros((bsz, SSM_N_HEADS, SSM_HEAD_DIM, SSM_D_STATE), jnp.float32)
    y_c, s_f, s_b = bidir(xc, bcm, ccm, dtc, zero, zero)
    zl, xl, blm, clm, dtl = prep(h_lat)
    y_l, _, _ = bidir(xl, blm, clm, dtl, s_f, s_b)
    y_ctx = out(zc, xc, y_c) if with_ctx_out else None
    return out(zl, xl, y_l), y_ctx

def mixer_na(h_lat, h_ctx, w_in, rpb, w_out, with_ctx_out):
    bsz, n_lat, _ = h_lat.shape
    rows = n_lat // GRID_W
    kh = min(NA_KH, rows)
    scale = NA_HEAD_DIM ** -0.5

    def qkv(h):
        q, k, v = jnp.split(h @ w_in, 3, axis=-1)
        shp = (bsz, h.shape[1], NA_N_HEADS, NA_HEAD_DIM)
        return q.reshape(shp), k.reshape(shp), v.reshape(shp)

    q_l, k_l, v_l = qkv(h_lat)
    q_c, k_c, v_c = qkv(h_ctx)
    grid = (bsz, rows, GRID_W, NA_N_HEADS, NA_HEAD_DIM)
    q_g = q_l.reshape(grid).swapaxes(0, 1)
    k_g = k_l.reshape(grid)
    v_g = v_l.reshape(grid)
    col = jnp.arange(GRID_W)
    c0 = jnp.clip(col - NA_KW // 2, 0, GRID_W - NA_KW)
    col_ok = (col[None, :] >= c0[:, None]) & (col[None, :] < c0[:, None] + NA_KW)
    dx_idx = jnp.clip(col[None, :] - col[:, None] + NA_KW - 1, 0, 2 * NA_KW - 2)
    rpb_cols = rpb.astype(jnp.float32)[:, :, dx_idx]

    def row_block(args):
        r, q_r = args
        r0 = jnp.clip(r - kh // 2, 0, rows - kh)
        k_band = lax.dynamic_slice_in_dim(k_g, r0, kh, axis=1)
        v_band = lax.dynamic_slice_in_dim(v_g, r0, kh, axis=1)
        dy_idx = r0 + jnp.arange(kh) - r + NA_KH - 1
        bias = rpb_cols[:, dy_idx].transpose(0, 2, 1, 3)
        s_lat = jnp.einsum('bqhd,byxhd->bhqyx', q_r, k_band).astype(jnp.float32) * scale + bias[None]
        s_lat = jnp.where(col_ok[:, None, :], s_lat, -jnp.inf)
        s_ctx = jnp.einsum('bqhd,bshd->bhqs', q_r, k_c).astype(jnp.float32) * scale
        s = jnp.concatenate([s_lat.reshape(bsz, NA_N_HEADS, GRID_W, kh * GRID_W), s_ctx], axis=-1)
        p = jax.nn.softmax(s, axis=-1).astype(v_band.dtype)
        p_lat = p[..., :kh * GRID_W].reshape(bsz, NA_N_HEADS, GRID_W, kh, GRID_W)
        p_ctx = p[..., kh * GRID_W:]
        return (jnp.einsum('bhqyx,byxhd->bqhd', p_lat, v_band)
                + jnp.einsum('bhqs,bshd->bqhd', p_ctx, v_c))

    o = lax.map(row_block, (jnp.arange(rows), q_g))
    y_lat = o.swapaxes(0, 1).reshape(bsz, n_lat, D_MODEL) @ w_out
    y_ctx = None
    if with_ctx_out:
        y_ctx = mha(q_c, k_c, v_c).reshape(bsz, -1, D_MODEL) @ w_out
    return y_lat, y_ctx

def sandwich_update(x, y_mix, mod, g, w1, w2):
    x = x + mod[2] * rmsnorm(y_mix, g[1])
    h = modulate(rmsnorm(x, g[2]), mod[3], mod[4])
    return x + mod[5] * rmsnorm(sq_relu_mlp(h, w1, w2), g[3])

def setup_inputs(seed: int = 0) -> dict:
    key = jax.random.key(seed)
    keys = iter(jax.random.split(key, 40))

    def nrm(shape, scale):
        return jax.random.normal(next(keys), shape, jnp.float32) * scale

    def unif(shape, lo, hi):
        return jax.random.uniform(next(keys), shape, jnp.float32, lo, hi)

    n_a, n_b, n_c, n_d = (len(range(m, DEPTH, N_MIXERS)) for m in range(N_MIXERS))
    d = D_MODEL
    dt0 = jnp.exp(unif((n_c, 2, SSM_N_HEADS), math.log(1e-3), math.log(1e-1)))
    return {
        'x': nrm((BATCH, SEQ, d), 1.0),
        'c': nrm((BATCH, d), 1.0),
        'ctx': nrm((BATCH, CTX_LEN, d), 1.0),
        'c_ctx': nrm((d,), 1.0),
        'ada_w': nrm((DEPTH, d, 6 * d), 0.5 * d ** -0.5),
        'ada_b': nrm((DEPTH, 6 * d), 0.02),
        'norm_g': 1.0 + nrm((DEPTH, 4, d), 0.02),
        'mlp_w1': nrm((DEPTH, d, D_FF), d ** -0.5),
        'mlp_w2': nrm((DEPTH, D_FF, d), D_FF ** -0.5),
        'ga_w_in': nrm((n_a, d, (GA_N_HEADS + 2 * GA_N_KV) * GA_HEAD_DIM), d ** -0.5),
        'ga_q_gain': 1.0 + nrm((n_a, GA_HEAD_DIM), 0.02),
        'ga_k_gain': 1.0 + nrm((n_a, GA_HEAD_DIM), 0.02),
        'ga_w_out': nrm((n_a, GA_N_HEADS * GA_HEAD_DIM, d), (GA_N_HEADS * GA_HEAD_DIM) ** -0.5),
        'hy_w_in': nrm((n_b, d, (HY_ORDER + 1) * d), d ** -0.5),
        'hy_conv_w': nrm((n_b, HY_SHORT, (HY_ORDER + 1) * d), HY_SHORT ** -0.5),
        'hy_conv_b': nrm((n_b, (HY_ORDER + 1) * d), 0.02),
        'hy_f_w1': nrm((n_b, HY_EMB, HY_FILTER_HIDDEN), HY_EMB ** -0.5),
        'hy_f_b1': nrm((n_b, HY_FILTER_HIDDEN), 0.02),
        'hy_f_w2': nrm((n_b, HY_FILTER_HIDDEN, HY_FILTER_HIDDEN), HY_FILTER_HIDDEN ** -0.5),
        'hy_f_b2': nrm((n_b, HY_FILTER_HIDDEN), 0.02),
        'hy_f_w3': nrm((n_b, HY_FILTER_HIDDEN, 2 * HY_ORDER * d), HY_FILTER_HIDDEN ** -0.5),
        'hy_f_freq': 1.0 + nrm((n_b, 2, HY_FILTER_HIDDEN), 0.02),
        'hy_skip': nrm((n_b, HY_ORDER, d), 0.5),
        'hy_w_out': nrm((n_b, d, d), d ** -0.5),
        'ssm_w_in': nrm((n_c, d, SSM_IN_DIM), d ** -0.5),
        'ssm_conv_w': nrm((n_c, SSM_CONV, SSM_D_INNER + 2 * SSM_GN), SSM_CONV ** -0.5),
        'ssm_conv_b': nrm((n_c, SSM_D_INNER + 2 * SSM_GN), 0.02),
        'ssm_dt_bias': dt0 + jnp.log(-jnp.expm1(-dt0)),
        'ssm_a_log': jnp.log(unif((n_c, 2, SSM_N_HEADS), 1.0, 16.0)),
        'ssm_d': 1.0 + nrm((n_c, SSM_N_HEADS), 0.02),
        'ssm_norm_g': 1.0 + nrm((n_c, SSM_D_INNER), 0.02),
        'ssm_w_out': nrm((n_c, SSM_D_INNER, d), SSM_D_INNER ** -0.5),
        'na_w_in': nrm((n_d, d, 3 * d), d ** -0.5),
        'na_rpb': nrm((n_d, NA_N_HEADS, 2 * NA_KH - 1, 2 * NA_KW - 1), 0.02),
        'na_w_out': nrm((n_d, d, d), d ** -0.5),
    }

def reference(x, c, ctx, c_ctx, ada_w, ada_b, norm_g, mlp_w1, mlp_w2,
              ga_w_in, ga_q_gain, ga_k_gain, ga_w_out,
              hy_w_in, hy_conv_w, hy_conv_b, hy_f_w1, hy_f_b1, hy_f_w2, hy_f_b2, hy_f_w3, hy_f_freq,
              hy_skip, hy_w_out,
              ssm_w_in, ssm_conv_w, ssm_conv_b, ssm_dt_bias, ssm_a_log, ssm_d, ssm_norm_g, ssm_w_out,
              na_w_in, na_rpb, na_w_out):
    sc = jax.nn.silu(c)
    scc = jax.nn.silu(c_ctx)
    x_lat, x_ctx = x, ctx
    for i in range(DEPTH):
        kind, j = i % N_MIXERS, i // N_MIXERS
        with_ctx = i < DEPTH - 1
        mod_l = jnp.split((sc @ ada_w[i] + ada_b[i])[:, None, :], 6, axis=-1)
        mod_c = jnp.split((scc @ ada_w[i] + ada_b[i])[None, None, :], 6, axis=-1)
        h_l = modulate(rmsnorm(x_lat, norm_g[i, 0]), mod_l[0], mod_l[1])
        h_c = modulate(rmsnorm(x_ctx, norm_g[i, 0]), mod_c[0], mod_c[1])
        if kind == 0:
            y_l, y_c = mixer_gqa(h_l, h_c, ga_w_in[j], ga_q_gain[j], ga_k_gain[j], ga_w_out[j], with_ctx)
        elif kind == 1:
            y_l, y_c = mixer_hyena(h_l, h_c, hy_w_in[j], hy_conv_w[j], hy_conv_b[j], hy_f_w1[j], hy_f_b1[j],
                                   hy_f_w2[j], hy_f_b2[j], hy_f_w3[j], hy_f_freq[j], hy_skip[j],
                                   hy_w_out[j], with_ctx)
        elif kind == 2:
            y_l, y_c = mixer_ssd(h_l, h_c, ssm_w_in[j], ssm_conv_w[j], ssm_conv_b[j], ssm_dt_bias[j],
                                 ssm_a_log[j], ssm_d[j], ssm_norm_g[j], ssm_w_out[j], with_ctx)
        else:
            y_l, y_c = mixer_na(h_l, h_c, na_w_in[j], na_rpb[j], na_w_out[j], with_ctx)
        x_lat = sandwich_update(x_lat, y_l, mod_l, norm_g[i], mlp_w1[i], mlp_w2[i])
        if with_ctx:
            x_ctx = sandwich_update(x_ctx, y_c, mod_c, norm_g[i], mlp_w1[i], mlp_w2[i])
    return x_lat


_drawn_inputs = setup_inputs


def setup_inputs(seed=0):
    import zlib

    import numpy as np

    out = dict(_drawn_inputs(seed))
    spreads = {}
    factors = {'norm_g': 3.101,
     'ga_q_gain': 8.0,
     'ga_k_gain': 8.0,
     'hy_conv_b': 8.585,
     'hy_f_freq': 5.367}
    for name, (base, spread) in spreads.items():
        noise = np.random.default_rng([zlib.crc32(name.encode()), seed]).standard_normal(out[name].shape)
        drawn = base * np.exp(spread * noise) if base else spread * noise
        out[name] = jnp.asarray(drawn.astype(out[name].dtype))
    for name, factor in factors.items():
        out[name] = (out[name] * factor).astype(out[name].dtype)
    return out
```

```python
import math
from contextlib import ExitStack

import concourse.bass as bass
import concourse.mybir as mybir
import numpy as np

F32 = mybir.dt.float32
F32R = mybir.dt.float32r
ALU = mybir.AluOpType
ACT = mybir.ActivationFunctionType
AX = mybir.AxisListType

P = 128
D = 1024
KC = D // P
NT = 512
NC = 256
NK = NT + NC
KT = NK // P
HD = 128
NH = 8
NKV = 2
GROUP = NH // NKV
QT = NT // P
EPS = 1e-6
FH = 64
NFEAT = 33
GRID_W = 64
QUARTERS = 4
QKV_UNITS = 12
OUT_UNITS = 8
MLP_UNITS = QUARTERS * 16
HY_UNITS = 24
U_QKV = 0
U_OUT0 = U_QKV + QKV_UNITS
U_MLP0 = U_OUT0 + OUT_UNITS
U_HY = U_MLP0 + MLP_UNITS
U_OUT1 = U_HY + HY_UNITS
U_MLP1 = U_OUT1 + OUT_UNITS
UNITS = U_MLP1 + MLP_UNITS
AHEAD = 3
ADA_BATCHES = [16, 32, 16, 24, 8]
ADA_START = [0, 16, 48, 64, 88]
C_G, C_AB, C_QG, C_KG = 0, 64, 160, 161
C_CW, C_CB, C_SK, C_F = 162, 234, 258, 274
NCOLS = 280
CE, CO, SE, SO, CEI, SEI = range(6)
TWO_PI_A = 6.28125
TWO_PI_B = float(np.float32(2 * math.pi - 6.28125))
TWO_PI_C = float(np.float32(2 * math.pi - 6.28125 - TWO_PI_B))
MAGIC = 12582912.0


def build(nc, xT, ctxT, cT, cols, wpack, apack, fw1, fw2, fw3, featsT, decay, tables, consts, ropes, fdram, out):
    with ExitStack() as ctx:
        def sb(name, shape, dt=F32, stack=ctx):
            return stack.enter_context(nc.sbuf_tensor(name, shape, dt))

        def sem(name):
            return ctx.enter_context(nc.semaphore(name))

        raw = sb("raw", [P, 2, D])
        whi = sb("whi", [P, 4, D], F32R)
        wlo = sb("wlo", [P, 4, D], F32R)
        araw = sb("araw", [P, 2, D])
        x = sb("x", [P, KC, NT])
        hhi = sb("hhi", [P, KC, NT], F32R)
        hlo = sb("hlo", [P, KC, NT], F32R)
        ghi = sb("ghi", [P, KC, NT], F32R)
        glo = sb("glo", [P, KC, NT], F32R)
        S = sb("scratch", [P, 12, NT])
        cst = sb("consts", [P, 3, P])
        col = sb("cols", [P, NCOLS])
        cs = sb("cs", [P, KC, 2])
        ce = sb("ce", [P, KC, 2])
        mods = sb("mods", [P, 2, 48, 2])
        gain = sb("gain", [P, 2, 4, KC])
        gainc = sb("gainc", [P, KC])
        nmax = sb("nmax", [P, 2])
        rsum = sb("rsum", [P, 2])
        rinv = sb("rinv", [P, 2])
        qg = sb("qg", [P, 1])
        epst = sb("eps", [P, 1])
        ident, ones, rotm = (cst[:, n, :] for n in range(3))
        y = S[:, 0:KC, :]
        with ExitStack() as area:
            thi = sb("thi", [P, 6, NT], F32R, area)
            tlo = sb("tlo", [P, 6, NT], F32R, area)
            fs = sb("fs", [P, 12, NT], F32, area)
        with ExitStack() as area:
            khi = sb("khi", [P, NKV, NK], F32R, area)
            klo = sb("klo", [P, NKV, NK], F32R, area)
            vhi = sb("vhi", [P, KT, NKV, HD], F32R, area)
            vlo = sb("vlo", [P, KT, NKV, HD], F32R, area)
            phi = sb("phi", [P, 2, KT, 2 * P], F32R, area)
            plo = sb("plo", [P, 2, KT, 2 * P], F32R, area)
        with ExitStack() as area:
            sb("below", [P, 4 * NKV * NK], F32, area)
            chi = sb("chi", [P, KC, NC], F32R, area)
            clo = sb("clo", [P, KC, NC], F32R, area)
            ctxs = sb("ctxs", [P, KC, NC], F32, area)
        with ExitStack() as area:
            t2hi = sb("t2hi", [P, 6, NT], F32R, area)
            t2lo = sb("t2lo", [P, 6, NT], F32R, area)
            zhi = sb("zhi", [P, 4, NT], F32R, area)
            zlo = sb("zlo", [P, 4, NT], F32R, area)
            es = sb("es", [P, 4, NT], F32, area)

        AB = ctx.enter_context(nc.psum_tensor("bank01", [P, 2, NT], F32))
        B2 = ctx.enter_context(nc.psum_tensor("bank2", [P, NT], F32))
        B3 = ctx.enter_context(nc.psum_tensor("bank3", [P, NT], F32))
        SC = ctx.enter_context(nc.psum_tensor("bank45", [P, 2, NT], F32))
        SD = ctx.enter_context(nc.psum_tensor("bank67", [P, 2, NT], F32))
        SCD = (SC, SD)

        small_in = sem("small_in")
        x_in = sem("x_in")
        table_in = sem("table_in")
        w3_in = sem("w3_in")
        decay_in = [sem(f"decay_in{n}") for n in range(2)]
        ctx_in = sem("ctx_in")
        rope_in = sem("rope_in")
        table2_in = sem("table2_in")
        filt_in = sem("filt_in")
        filt_out = sem("filt_out")
        raw_in = [sem(f"raw_in{n}") for n in range(2)]
        ada_in = [sem(f"ada_in{n}") for n in range(2)]
        x_out = sem("x_out")
        hi_done = sem("hi_done")
        lo_done = sem("lo_done")
        unit_done = sem("unit_done")
        evac_done = sem("evac_done")
        eps_set = sem("eps_set")
        silu_e = sem("silu_e")
        silu_done = sem("silu_done")
        ada_done = sem("ada_done")
        mod_done = sem("mod_done")
        sin_arg = sem("sin_arg")
        sin_done = sem("sin_done")
        fmlp_done = sem("fmlp_done")
        thi_done = sem("thi_done")
        tlo_done = sem("tlo_done")
        gen_done = sem("gen_done")
        gen_used = sem("gen_used")
        eo_full = sem("eo_full")
        eo_hi = sem("eo_hi")
        eo_lo = sem("eo_lo")
        fdft_done = sem("fdft_done")
        fodd_done = sem("fodd_done")
        fout_done = sem("fout_done")
        sq_done = sem("sq_done")
        ss_done = sem("ss_done")
        sd_done = sem("sd_done")
        rs_done = sem("rs_done")
        x_done = sem("x_done")
        ht_done = sem("ht_done")
        hhi_done = sem("hhi_done")
        h_done = sem("h_done")
        vlo_done = sem("vlo_done")
        job_sq = sem("job_sq")
        job_ss = sem("job_ss")
        job_sd = sem("job_sd")
        job_rs = sem("job_rs")
        job_qn = sem("job_qn")
        job_rot = sem("job_rot")
        job_cos = sem("job_cos")
        job_sin = sem("job_sin")
        job_full = sem("job_full")
        job_hi = sem("job_hi")
        job_lo = sem("job_lo")
        score_done = sem("score_done")
        nmax_done = sem("nmax_done")
        exp_done = sem("exp_done")
        rinv_done = sem("rinv_done")
        p_done = sem("p_done")
        pt_done = sem("pt_done")
        phi_done = sem("phi_done")
        plo_done = sem("plo_done")
        pv_done = sem("pv_done")
        ohi_done = sem("ohi_done")
        olo_done = sem("olo_done")
        relu_done = sem("relu_done")
        g_full = sem("g_full")
        ghi_done = sem("ghi_done")
        g_done = sem("g_done")
        part_done = sem("part_done")
        y_done = sem("y_done")
        y_zero = sem("y_zero")
        u_raw = sem("u_raw")
        tap_done = sem("tap_done")
        v_done = sem("v_done")
        zt_done = sem("zt_done")
        zhi_done = sem("zhi_done")
        zlo_done = sem("zlo_done")
        dft_done = sem("dft_done")
        odd_done = sem("odd_done")
        spec_free = sem("spec_free")
        filt_used = sem("filt_used")
        spec_full = sem("spec_full")
        spec_hi = sem("spec_hi")
        spec_lo = sem("spec_lo")
        inv_done = sem("inv_done")
        skip_done = sem("skip_done")
        conv_done = sem("conv_done")
        z3_hi = sem("z3_hi")
        z3_lo = sem("z3_lo")
        own_act = sem("own_act")
        own_dve = sem("own_dve")
        own_pool = sem("own_pool")

        block = ctx.enter_context(nc.Block())

        FPAIR = ((ghi, glo), (hhi, hlo))
        HF = (fs[:, 8, :], S[:, 4, :])
        FE = (fs[:, 9, :], S[:, 5, :])
        HB = fs[:, 10, :]
        DEC = (fs[:, 11, :], S[:, 9, :])
        JOBS = []
        for g in range(NKV):
            ps = SCD[g]
            JOBS.append((2 + g, ps[:, 0, :], NT, g, True, khi[:, g, 0:NT], klo[:, g, 0:NT]))
            JOBS.append((2 + g, ps[:, 1, 0:NC], NC, None, True, khi[:, g, NT:NK], klo[:, g, NT:NK]))
        for h in range(NH):
            JOBS.append((4 + h, AB[:, h % 2, :], NT, NKV + h, False, ghi[:, h, :], glo[:, h, :]))
        ROPE = [n for n, job in enumerate(JOBS) if job[3] is not None]

        SCORE = [b[:, :, :].rearrange("p a b -> p (a b)")[:, 0:NK] for b in SCD]
        PROB = [S[:, 2 * n:2 * n + 2, :].rearrange("p a b -> p (a b)")[:, 0:NK] for n in range(2)]
        FP, FP_, FQ, FQ_ = (araw[:, n // 2, n % 2 * NT:(n % 2 + 1) * NT] for n in range(4))
        SPEC = (S[:, 10, :], es[:, 2, :], S[:, 11, :], S[:, 8, :])

        def jobs_of(t):
            return [(n, job) for n, job in enumerate(JOBS) if job[0] == t]

        NQ = NH * QT
        STAGES = [(0, 0), (0, 1), (1, 0), (1, 1)]
        UNITS_V, UNITS_X1, UNITS_X2 = U_HY, U_HY + 8, U_HY + 16
        BETWEEN = [UNITS_V + 4, UNITS_X1, UNITS_X1 + 4, UNITS_X2]
        BOUND = [(0, 1, 0, 2, 0, 24), (0, 3, 1, 0, 1, 0), (1, 1, 1, 2, 1, 24), (1, 3, None, None, None, None)]
        NORMS_BEFORE = 2
        FCOL = {n: C_F + n for n in range(4)}

        def f(ap):
            return ap.bitcast(F32)

        def gcol(l, n, j):
            return gain[:, l, n, j:j + 1]

        def shift(l, t, j, v=0):
            return mods[:, l, t + j, v:v + 1]

        class Own:

            def __init__(self, eng, s):
                self.eng, self.s, self.n = eng, s, 0

            def __call__(self, ins):
                self.n += 1
                ins.then_inc(self.s, 1)
                self.eng.wait_ge(self.s, self.n)

        @block.sync
        def _(sp):
            sp.dma_start(cst[:, :, :], consts).then_inc(small_in, 16)
            sp.dma_start(col[:, :], cols).then_inc(small_in, 16)
            sp.dma_start(cs[:, :, :], cT).then_inc(small_in, 16)
            sp.dma_start(S[0:NFEAT, 6, :], featsT).then_inc(small_in, 16)
            sp.dma_start(S[0:NFEAT, 10, 0:FH], fw1).then_inc(small_in, 16)
            sp.dma_start(S[0:FH, 10, FH:2 * FH], fw2).then_inc(small_in, 16)
            sp.dma_start(S[:, 0:6, :], tables).then_inc(table_in, 16)
            sp.dma_start(fs[0:FH, 0:8, :], fw3).then_inc(w3_in, 16)

            def load_decay(n):
                q, tt = divmod(n, 4)
                sp.dma_start(DEC[n % 2], decay[q // 2, tt]).then_inc(decay_in[n % 2], 16)

            load_decay(0)
            sp.dma_start(x[:, :, :], xT).then_inc(x_in, 16)
            sp.dma_start(raw[:, 0, :], wpack[0]).then_inc(raw_in[0], 16)
            sp.dma_start(raw[:, 1, :], wpack[1]).then_inc(raw_in[1], 16)
            sp.wait_ge(sin_done, 2)
            load_decay(1)
            for q in range(5):
                for n in range(4 * q, min(4 * q + 4, 16)):
                    if n >= 2:
                        sp.wait_ge(gen_used, n - 1)
                        load_decay(n)
                if q >= 1:
                    for ft in range(2):
                        m = 2 * (q - 1) + ft
                        sp.wait_ge(fout_done, 4 * m + 4)
                        sp.dma_start(fdram[m], S[:, 0:4, :]).then_inc(filt_out, 16)
            sp.wait_ge(fdft_done, 8)
            sp.wait_ge(eo_lo, 32)
            sp.dma_start(ctxs[:, :, :], ctxT).then_inc(ctx_in, 16)
            with sp.Fori(1, UNITS // 2) as i:
                for s in range(2):
                    sp.wait_ge(hi_done, 2 * i + s - 1)
                    sp.wait_ge(lo_done, 2 * i + s - 1)
                    sp.dma_start(raw[:, s, :], wpack[2 * i + s]).then_inc(raw_in[s], 16)
            for j in range(KC):
                sp.wait_ge(x_done, 3 * KC + j + 1)
                sp.dma_start(out[j], x[:, j, :]).then_inc(x_out, 16)
            sp.wait_ge(filt_out, 8 * 16)
            sp.wait_ge(x_out, KC * 16)

        @block.gpsimd
        def _(pool):
            nc.gpsimd.memset(epst[:, :], EPS).then_inc(eps_set, 1)

            def load_ada(a0, turns):
                with pool.Fori(0, turns) as i:
                    for s in range(2):
                        if a0:
                            pool.wait_ge(ada_done, a0 + 2 * i + s - 1)
                        pool.dma_start(araw[:, s, :], apack[a0 + 2 * i + s]).then_inc(ada_in[s], 16)

            pool.dma_start(araw[:, 0, :], apack[0]).then_inc(ada_in[0], 16)
            pool.dma_start(araw[:, 1, :], apack[1]).then_inc(ada_in[1], 16)
            load_ada(2, 7)
            pool.wait_ge(ada_done, 16)
            pool.dma_start(araw[:, :, 0:NT], ropes).then_inc(rope_in, 16)
            pool.wait_ge(rope_in, 16)
            for r, n in enumerate(ROPE):
                pool.wait_ge(job_qn, n + 1)
                if r >= 2:
                    pool.wait_ge(job_lo, ROPE[r - 2] + 1)
                nc.gpsimd.tensor_tensor(S[:, 10 + r % 2, :], S[:, 8 + n % 2, :], araw[:, 0, 0:NT],
                                        ALU.mult).then_inc(job_cos, 1)
            pool.wait_ge(job_sin, len(ROPE))
            pool.wait_ge(job_cos, len(ROPE))
            for s in range(2):
                pool.dma_start(araw[:, s, :], apack[16 + s]).then_inc(ada_in[s], 16)
            load_ada(18, 15)
            load_ada(48, 8)
            pool.wait_ge(h_done, 3 * KC)
            nc.gpsimd.memset(y, 0.0).then_inc(y_zero, 1)
            load_ada(64, 12)
            pool.wait_ge(ada_done, 88)
            for k, (o, c) in enumerate(STAGES):
                for ft in range(2):
                    n = 2 * k + ft
                    if n:
                        pool.wait_ge(filt_used, n)
                    else:
                        pool.wait_ge(filt_out, 8 * 16)
                    pool.dma_start(araw[:, :, :].rearrange("p a (b n) -> p (a b) n", b=2),
                                   fdram[2 * (2 * c + o) + ft]).then_inc(filt_in, 16)
            pool.wait_ge(filt_used, 8)
            for s in range(2):
                pool.dma_start(araw[:, s, :], apack[88 + s]).then_inc(ada_in[s], 16)
            load_ada(90, 3)
            pool.wait_ge(h_done, 5 * KC)
            nc.gpsimd.memset(y, 0.0).then_inc(y_zero, 1)

        @block.scalar
        def _(act):
            own = Own(act, own_act)
            A = nc.scalar.activation

            def prep(u, s, r):
                act.wait_ge(raw_in[r], (u - r) * 8 + 16)
                if not isinstance(u, int) or u >= 4:
                    act.wait_ge(unit_done, u - 3)
                A(whi[:, s, :], raw[:, r, :], ACT.Copy).then_inc(hi_done, 1)

            def square_sum(b, src, n, after):
                for j in range(KC):
                    m = b * KC + j
                    after(j)
                    if m >= 2:
                        act.wait_ge(ss_done, m - 1)
                    A(S[:, 10 + j % 2, 0:n], src[:, j, :], ACT.Square).then_inc(sq_done, 1)

            def root(b, dst, n):
                act.wait_ge(ss_done, KC * (b + 1))
                A(dst[:, 0:n], B2[:, 0:n], ACT.Sqrt, scale=1.0 / D, bias=epst[:, 0:1]).then_inc(sd_done, 1)

            def operand_hi(k, hi, l, t, v, buf):
                for j in range(KC):
                    act.wait_ge(ht_done, k * KC + j + 1)
                    A(hi[:, j, :], buf[:, j, :], ACT.Identity, bias=shift(l, t, j, v)).then_inc(hhi_done, 1)

            act.wait_ge(small_in, 96)
            A(ce[:, :, :], cs[:, :, :], ACT.Exp, scale=-1.0).then_inc(silu_e, 1)
            act.wait_ge(table_in, 16)
            A(thi[:, :, :], S[:, 0:6, :], ACT.Copy).then_inc(thi_done, 1)
            for k in range(2):
                act.wait_ge(sin_arg, k + 1)
                A(S[0:FH, 7 + k, :], S[0:FH, 9, :], ACT.Sin).then_inc(sin_done, 1)
            prep(0, 0, 0)
            prep(1, 1, 1)

            for q in range(5):
                for n in range(4 * q, min(4 * q + 4, 16)):
                    hi = FPAIR[q % 2][0]
                    tt = n % 4
                    if q >= 2:
                        act.wait_ge(fdft_done, 2 * (q - 1))
                    act.wait_ge(eo_full, 2 * n + 1)
                    A(hi[:, tt, :], FE[n % 2], ACT.Copy).then_inc(eo_hi, 1)
                    act.wait_ge(eo_full, 2 * n + 2)
                    A(hi[:, 4 + tt, :], HF[n % 2], ACT.Copy).then_inc(eo_hi, 1)
                if q >= 1:
                    for ft in range(2):
                        m = 2 * (q - 1) + ft
                        act.wait_ge(fdft_done, m + 1)
                        if m:
                            act.wait_ge(fout_done, 4 * m)
                        A(S[:, 10, :], SC[:, 1, :], ACT.Copy).then_inc(fodd_done, 1)
                        A(S[:, 11, :], SD[:, 1, :], ACT.Copy).then_inc(fodd_done, 1)

            act.wait_ge(fout_done, 32)
            square_sum(0, ctxs, NC, lambda j: act.wait_ge(ctx_in, 16))
            act.wait_ge(eps_set, 1)
            root(0, S[:, 9, :], NC)
            operand_hi(0, chi, 0, 0, 1, ctxs)
            square_sum(1, x, NT, lambda j: act.wait_ge(x_in, 16))
            act.wait_ge(ht_done, KC)
            root(1, S[:, 9, :], NT)
            operand_hi(1, hhi, 0, 0, 0, y)

            prep(2, 2, 0)
            for t in range(QKV_UNITS + 2):
                if t < QKV_UNITS:
                    prep(t + AHEAD, (t + AHEAD) % 4, (t + AHEAD) % 2)
                for n, (_, ps, w, r, key, hi, lo) in jobs_of(t - 2):
                    act.wait_ge(job_full, n + 1)
                    A(hi, S[:, 10 + r % 2, :] if r is not None else S[:, 8 + n % 2, 0:w], ACT.Copy).then_inc(job_hi, 1)
                for n, (_, ps, w, r, key, hi, lo) in jobs_of(t - 1):
                    act.wait_ge(job_ss, n + 1)
                    if n >= 2:
                        act.wait_ge(job_qn, n - 1)
                    A(S[:, 6 + n % 2, 0:w], B2[:, 0:w], ACT.Sqrt, scale=1.0 / HD, bias=epst[:, 0:1]).then_inc(job_sd, 1)
                if t < QKV_UNITS:
                    act.wait_ge(unit_done, t + 1)
                if t < NKV:
                    for half in range(2):
                        ps = SCD[t][:, half, 0:3 * P].rearrange("p (a b) -> p a b", a=3)
                        ins = A(vhi[:, 3 * half:3 * half + 3, t, :], ps, ACT.Copy)
                        if half == 0:
                            own(ins)
                    ins.then_inc(evac_done, 1)
                for i, (n, (_, ps, w, r, key, hi, lo)) in enumerate(jobs_of(t)):
                    if n >= 2:
                        act.wait_ge(job_ss, n - 1)
                    A(S[:, 4 + n % 2, 0:w], ps, ACT.Square).then_inc(job_sq, 1)
                    if n >= 4:
                        act.wait_ge(job_lo, n - 3)
                    ins = A(S[:, n % 4, 0:w], ps, ACT.Copy)
                    if i + 1 < len(jobs_of(t)):
                        own(ins)
                    else:
                        ins.then_inc(evac_done, 1)

            for n in range(NQ + 5):
                m = (n - 6) // 2
                if n >= 6 and n % 2 == 0:
                    act.wait_ge(pv_done, m + 1)
                    A(hhi[:, m // 2, (m % 2) * 2 * P:(m % 2 + 1) * 2 * P],
                      B2[:, (m % 2) * 2 * P:(m % 2 + 1) * 2 * P], ACT.Copy).then_inc(ohi_done, 1)
                if n < NQ:
                    act.wait_ge(nmax_done, n + 1)
                    if n >= 2:
                        act.wait_ge(pt_done, n - 1)
                    A(PROB[n % 2], SCORE[n % 2], ACT.Exp, bias=nmax[:, n % 2:n % 2 + 1],
                      accum_out=rsum[:, n % 2:n % 2 + 1]).then_inc(exp_done, 1)
                m = n - 2
                if 0 <= m < NQ:
                    act.wait_ge(pt_done, m + 1)
                    if m >= 4:
                        act.wait_ge(pv_done, m // 2 - 1)
                    A(phi[:, m // 2 % 2, :, (m % 2) * P:(m % 2 + 1) * P].rearrange("p (a b) c -> p a b c", a=2),
                      AB[:, :, 0:3 * P].rearrange("p a (b c) -> p a b c", b=3), ACT.Copy).then_inc(phi_done, 1)

            act.wait_ge(olo_done, NQ // 2)
            for half in range(2):
                if half:
                    act.wait_ge(tlo_done, 2)
                act.dma_start(es[:, 0:3, :], tables[:, 3 * half:3 * half + 3, :]).then_inc(table2_in, 16)
                act.wait_ge(table2_in, 16 * (half + 1))
                A(t2hi[:, 3 * half:3 * half + 3, :], es[:, 0:3, :], ACT.Copy).then_inc(thi_done, 1)

            def out_units(u0):
                with act.Fori(0, OUT_UNITS // 4) as i:
                    for s in range(4):
                        u = u0 + 4 * i + s
                        prep(u + AHEAD, (s + AHEAD) % 4, (s + AHEAD) % 2)
                        act.wait_ge(unit_done, u + 1)
                        A(S[:, 4 * i + s, :], AB[:, s % 2, :], ACT.Copy).then_inc(evac_done, 1)

            def boundary(b):
                nb = 2 * b + NORMS_BEFORE
                if b % 2 == 0:
                    square_sum(nb, y, NT, lambda j: act.wait_ge(evac_done, (U_MLP0, U_MLP1)[b // 2]))
                else:
                    square_sum(nb, y, NT, lambda j: act.wait_ge(y_done, b // 2 * 32 + 24 + j + 1))
                root(nb, S[:, 8, :], NT)
                if b == 3:
                    return
                square_sum(nb + 1, x, NT, lambda j: act.wait_ge(x_done, b * KC + j + 1))
                root(nb + 1, S[:, 9, :], NT)
                operand_hi(b + 2, hhi, BOUND[b][4], BOUND[b][5], 0, y)

            def quarter(l, q, last=False):
                u0 = (U_MLP0, U_MLP1)[l] + 16 * q
                c0 = l * 32 + 8 * q
                for j in range(8):
                    prep(u0 + j + AHEAD, (j + AHEAD) % 4, (j + AHEAD) % 2)
                    act.wait_ge(unit_done, u0 + j + 1)
                    if j < 2:
                        if not isinstance(c0, int) or c0:
                            act.wait_ge(y_done, c0)
                            act.wait_ge(g_done, c0)
                    else:
                        act.wait_ge(g_done, c0 + j - 1)
                    A(S[:, 8 + j % 2, :], AB[:, j % 2, :], ACT.Relu).then_inc(evac_done, 1)
                    act.wait_ge(evac_done, u0 + j + 1)
                    A(S[:, 10 + j % 2, :], S[:, 8 + j % 2, :], ACT.Square).then_inc(g_full, 1)
                    act.wait_ge(g_full, c0 + j + 1)
                    A(ghi[:, j, :], S[:, 10 + j % 2, :], ACT.Copy).then_inc(ghi_done, 1)
                for j in range(8):
                    u = u0 + 8 + j
                    if not last or u + AHEAD < UNITS:
                        prep(u + AHEAD, (j + AHEAD) % 4, (j + AHEAD) % 2)
                    act.wait_ge(unit_done, u + 1)
                    if j >= 2:
                        act.wait_ge(y_done, c0 + j - 1)
                    A(S[:, 8 + j % 2, :], AB[:, j % 2, :], ACT.Copy).then_inc(evac_done, 1)

            out_units(U_OUT0)
            boundary(0)
            quarter(0, 0)
            with act.Fori(1, QUARTERS) as q:
                quarter(0, q)
            boundary(1)

            def hy_unit(n):
                u = U_HY + n
                act.wait_ge(unit_done, u + 1)
                if n:
                    act.wait_ge(tap_done, n)
                centre = y[:, n, :] if n < KC else es[:, 1, :]
                own(A(centre, AB[:, n % 2, :], ACT.Identity, scale=col[:, C_CW + 24 + n:C_CW + 25 + n],
                      bias=col[:, C_CB + n:C_CB + n + 1]))
                A(es[:, 0, :], AB[:, n % 2, :], ACT.Copy).then_inc(evac_done, 1)

            def hy_prep(n):
                u = U_HY + n + AHEAD
                prep(u, u % 4, u % 2)

            for n in range(4):
                hy_prep(n)
                hy_unit(n)
            for k, (o, c) in enumerate(STAGES):
                for tt in range(4):
                    act.wait_ge(zt_done, 4 * k + tt + 1)
                    A(zhi[:, tt, :], SCD[tt // 2][:, tt % 2, :], ACT.Copy).then_inc(zhi_done, 1)
                for i in range(4):
                    j = 4 * c + i
                    A(y[:, j, :], y[:, j, :], ACT.Copy,
                      scale=col[:, C_SK + 8 * o + j:C_SK + 8 * o + j + 1]).then_inc(skip_done, 1)
                for s in range(4):
                    n = 4 * (k + 1) + s
                    m = 2 * k + s // 2
                    hy_prep(n)
                    if s % 2 == 0:
                        act.wait_ge(dft_done, m + 1)
                        if m:
                            act.wait_ge(spec_lo, 4 * m)
                        A(S[:, 9, :], SC[:, 1, :], ACT.Copy).then_inc(odd_done, 1)
                        A(S[:, 10, :], SD[:, 1, :], ACT.Copy).then_inc(odd_done, 1)
                    else:
                        for e in range(4):
                            act.wait_ge(spec_full, 4 * m + e + 1)
                            A(ghi[:, 2 * e + s // 2, :], SPEC[e], ACT.Copy).then_inc(spec_hi, 1)
                    hy_unit(n)
            for n in range(20, 24):
                hy_prep(n)
                hy_unit(n)
            for j in range(KC):
                act.wait_ge(tap_done, 24 if j >= 4 else 20)
                act.wait_ge(unit_done, U_HY + 24)
                A(ghi[:, j, :], y[:, j, :], ACT.Copy).then_inc(z3_hi, 1)
            act.wait_ge(z3_lo, KC)
            out_units(U_OUT1)
            boundary(2)
            with act.Fori(0, QUARTERS - 1) as q:
                quarter(1, q)
            quarter(1, QUARTERS - 1, last=True)
            boundary(3)

        @block.vector
        def _(dve):
            own = Own(dve, own_dve)
            TT = nc.vector.tensor_tensor
            STT = nc.vector.scalar_tensor_tensor
            TS = nc.vector.tensor_scalar

            def prep(u, s, r):
                dve.wait_ge(hi_done, u + 1)
                TT(wlo[:, s, :], raw[:, r, :], f(whi[:, s, :]), ALU.subtract).then_inc(lo_done, 1)

            def inverse_root(nb, dst, w):
                dve.wait_ge(sd_done, nb + 1)
                nc.vector.reciprocal(dst[:, 0:w], dst[:, 0:w]).then_inc(rs_done, 1)
                dve.wait_ge(rs_done, nb + 1)

            def operand(k, src, buf, rs, gains, hi, lo, l, t, v):
                w = hi.shape[2]

                def lo_part(j):
                    dve.wait_ge(hhi_done, k * KC + j + 1)
                    STT(lo[:, j, :], buf[:, j, :], shift(l, t, j, v), f(hi[:, j, :]), ALU.add,
                        ALU.subtract).then_inc(h_done, 1)

                for j in range(KC):
                    STT(buf[:, j, :], src[:, j, :], gains[:, j:j + 1], rs[:, 0:w], ALU.mult,
                        ALU.mult).then_inc(ht_done, 1)
                    if j:
                        lo_part(j - 1)
                lo_part(KC - 1)

            def modulation(b):
                a, n = ADA_START[b], ADA_BATCHES[b]
                l, t0 = divmod(a, 48)
                dve.wait_ge(ada_done, a + n)
                for v in range(2 if b == 0 else 1):
                    ps = B3[:, l * 96 + 2 * t0:l * 96 + 2 * (t0 + n)].rearrange("p (t v) -> p t v", v=2)
                    own(TT(mods[:, l, t0:t0 + n, v], ps[:, :, v],
                           col[:, C_AB + l * 48 + t0:C_AB + l * 48 + t0 + n], ALU.add))

                def scaled(dst, m, g, v=0):
                    return STT(dst, mods[:, l, 8 * m:8 * m + 8, v], 1.0, col[:, C_G + 8 * g:C_G + 8 * g + 8], ALU.add, ALU.mult)

                def gated(dst, m, g):
                    return TT(dst, mods[:, l, 8 * m:8 * m + 8, 0], col[:, C_G + 8 * g:C_G + 8 * g + 8], ALU.mult)

                if b == 0:
                    own(scaled(gainc[:, :], 1, 0, 1))
                    last = scaled(gain[:, 0, 0, :], 1, 0)
                elif b == 1:
                    own(gated(gain[:, 0, 1, :], 2, 1))
                    own(scaled(gain[:, 0, 2, :], 4, 2))
                    last = gated(gain[:, 0, 3, :], 5, 3)
                elif b == 2:
                    last = scaled(gain[:, 1, 0, :], 1, 4)
                elif b == 3:
                    own(gated(gain[:, 1, 1, :], 2, 5))
                    last = scaled(gain[:, 1, 2, :], 4, 6)
                else:
                    last = gated(gain[:, 1, 3, :], 5, 7)
                last.then_inc(mod_done, 1)
                dve.wait_ge(mod_done, b + 1)

            dve.wait_ge(silu_e, 1)
            own(nc.vector.tensor_scalar_add(ce[:, :, :], ce[:, :, :], 1.0))
            own(nc.vector.reciprocal(ce[:, :, :], ce[:, :, :]))
            TT(ce[:, :, :], ce[:, :, :], cs[:, :, :], ALU.mult).then_inc(silu_done, 1)
            nc.vector.tensor_scalar_mul(qg[:, :], col[:, C_QG:C_QG + 1], HD ** -0.5)

            dve.wait_ge(thi_done, 1)
            TT(tlo[:, :, :], S[:, 0:6, :], f(thi[:, :, :]), ALU.subtract).then_inc(tlo_done, 1)

            arg, turns = S[0:FH, 9, :], S[0:FH, 11, :]
            for k in range(2):
                dve.wait_ge(fmlp_done, k + 1)
                if k:
                    dve.wait_ge(sin_done, 1)
                own(TS(arg, B2[0:FH, :], col[0:FH, FCOL[k]:FCOL[k] + 1], col[0:FH, FCOL[2 + k]:FCOL[2 + k] + 1],
                       ALU.add, ALU.mult))
                own(TS(turns, arg, 1.0 / (2 * math.pi), MAGIC, ALU.mult, ALU.add))
                own(nc.vector.tensor_scalar_add(turns, turns, -MAGIC))
                for part in (TWO_PI_A, TWO_PI_B, TWO_PI_C):
                    own(STT(arg, turns, -part, arg, ALU.mult, ALU.add))
                TS(arg, arg, 3.1415925, -3.1415925, ALU.min, ALU.max).then_inc(sin_arg, 1)
            prep(0, 0, 0)
            prep(1, 1, 1)

            def eo_los(n):
                q, tt = divmod(n, 4)
                hi, lo = FPAIR[q % 2]
                dve.wait_ge(eo_hi, 2 * n + 2)
                TT(lo[:, tt, :], FE[n % 2], f(hi[:, tt, :]), ALU.subtract).then_inc(eo_lo, 1)
                TT(lo[:, 4 + tt, :], HF[n % 2], f(hi[:, 4 + tt, :]), ALU.subtract).then_inc(eo_lo, 1)

            for q in range(5):
                for n in range(4 * q, min(4 * q + 4, 16)):
                    tt = n % 4
                    dve.wait_ge(gen_done, n + 1)
                    dve.wait_ge(decay_in[n % 2], 16 * (n // 2 + 1))
                    if n >= 2:
                        dve.wait_ge(eo_lo, 2 * n - 2)
                    own(TT(HF[n % 2], AB[:, 0, :], DEC[n % 2], ALU.mult))
                    ins = TT(HB, AB[:, 1, :], DEC[n % 2], ALU.mult)
                    ins.then_inc(gen_used, 1)
                    dve.wait_ge(gen_used, n + 1)
                    if tt == 0:
                        own(nc.vector.memset(HB[0:1, :], 0.0))
                    TT(FE[n % 2], HF[n % 2], HB, ALU.add).then_inc(eo_full, 1)
                    dve.wait_ge(eo_full, 2 * n + 1)
                    TT(HF[n % 2], HF[n % 2], HB, ALU.subtract).then_inc(eo_full, 1)
                    dve.wait_ge(eo_full, 2 * n + 2)
                    if tt:
                        eo_los(n - 1)
                    if tt == 3:
                        eo_los(n)
                if q >= 1:
                    for ft in range(2):
                        m = 2 * (q - 1) + ft
                        dve.wait_ge(fodd_done, 2 * m + 2)
                        if m:
                            dve.wait_ge(filt_out, 16 * m)
                        TT(S[:, 0, :], SC[:, 0, :], S[:, 10, :], ALU.add).then_inc(fout_done, 1)
                        TT(S[:, 1, :], SC[:, 0, :], S[:, 10, :], ALU.subtract).then_inc(fout_done, 1)
                        TT(S[:, 2, :], SD[:, 0, :], S[:, 11, :], ALU.add).then_inc(fout_done, 1)
                        TT(S[:, 3, :], S[:, 11, :], SD[:, 0, :], ALU.subtract).then_inc(fout_done, 1)

            modulation(0)
            inverse_root(0, S[:, 9, :], NC)
            operand(0, ctxs, ctxs, S[:, 9, :], gainc, chi, clo, 0, 0, 1)
            inverse_root(1, S[:, 9, :], NT)
            dve.wait_ge(filt_out, 8 * 16)
            operand(1, x, y, S[:, 9, :], gain[:, 0, 0, :], hhi, hlo, 0, 0, 0)

            prep(2, 2, 0)
            for t in range(QKV_UNITS + 2):
                if t < QKV_UNITS:
                    prep(t + AHEAD, (t + AHEAD) % 4, (t + AHEAD) % 2)
                if t < NKV:
                    dve.wait_ge(evac_done, t + 1)
                    for half in range(2):
                        ps = SCD[t][:, half, 0:3 * P].rearrange("p (a b) -> p a b", a=3)
                        TT(vlo[:, 3 * half:3 * half + 3, t, :], ps, f(vhi[:, 3 * half:3 * half + 3, t, :]),
                           ALU.subtract).then_inc(vlo_done, 1)
                for n, (_, ps, w, r, key, hi, lo) in jobs_of(t - 2):
                    if r is not None:
                        dve.wait_ge(rope_in, 16)
                        dve.wait_ge(job_rot, r + 1)
                        dve.wait_ge(job_qn, n + 1)
                        TT(S[:, n % 4, :], B3[:, :], araw[:, 1, 0:NT], ALU.mult).then_inc(job_sin, 1)
                        dve.wait_ge(job_sin, r + 1)
                        dve.wait_ge(job_cos, r + 1)
                        full = S[:, 10 + r % 2, :]
                        TT(full, full, S[:, n % 4, :], ALU.add).then_inc(job_full, 1)
                    else:
                        full = S[:, 8 + n % 2, 0:w]
                        dve.wait_ge(job_qn, n + 1)
                        dve.sem_inc(job_full, 1)
                    dve.wait_ge(job_hi, n + 1)
                    TT(lo, full, f(hi), ALU.subtract).then_inc(job_lo, 1)
                for n, (_, ps, w, r, key, hi, lo) in jobs_of(t - 1):
                    dve.wait_ge(job_sd, n + 1)
                    own(nc.vector.reciprocal(S[:, 6 + n % 2, 0:w], S[:, 6 + n % 2, 0:w]))
                    dve.wait_ge(evac_done, t)
                    if n >= 2:
                        dve.wait_ge(job_lo, n - 1)
                    g = col[:, C_KG:C_KG + 1] if key else qg[:, 0:1]
                    STT(S[:, 8 + n % 2, 0:w], S[:, n % 4, 0:w], g, S[:, 6 + n % 2, 0:w], ALU.mult,
                        ALU.mult).then_inc(job_qn, 1)

            def o_lo(m):
                dve.wait_ge(ohi_done, m + 1)
                cols_ = slice((m % 2) * 2 * P, (m % 2 + 1) * 2 * P)
                TT(hlo[:, m // 2, cols_], B2[:, cols_], f(hhi[:, m // 2, cols_]), ALU.subtract).then_inc(olo_done, 1)

            for n in range(NQ + 5):
                m = n - 3
                if 0 <= m < NQ:
                    dve.wait_ge(phi_done, m + 1)
                    for half in range(2):
                        at = slice(3 * half, 3 * half + 3)
                        TT(plo[:, m // 2 % 2, at, (m % 2) * P:(m % 2 + 1) * P],
                           AB[:, half, 0:3 * P].rearrange("p (b c) -> p b c", b=3),
                           f(phi[:, m // 2 % 2, at, (m % 2) * P:(m % 2 + 1) * P]), ALU.subtract).then_inc(plo_done, 1)
                if n < NQ:
                    dve.wait_ge(score_done, n + 1)
                    if n >= 2:
                        dve.wait_ge(exp_done, n - 1)
                    nc.vector.tensor_reduce(out=nmax[:, n % 2:n % 2 + 1], in_=SCORE[n % 2], op=ALU.max,
                                            axis=AX.X, negate=True).then_inc(nmax_done, 1)
                m = n - 1
                if 0 <= m < NQ:
                    dve.wait_ge(exp_done, m + 1)
                    if m >= 2:
                        dve.wait_ge(p_done, m - 1)
                    own(nc.vector.reciprocal(rinv[:, m % 2:m % 2 + 1], rsum[:, m % 2:m % 2 + 1]))
                    TS(PROB[m % 2], PROB[m % 2], rinv[:, m % 2:m % 2 + 1], None, ALU.mult).then_inc(p_done, 1)
                if n >= 6 and n % 2 == 0:
                    o_lo((n - 6) // 2)
            modulation(1)
            for half in range(2):
                dve.wait_ge(thi_done, 2 + half)
                TT(t2lo[:, 3 * half:3 * half + 3, :], es[:, 0:3, :], f(t2hi[:, 3 * half:3 * half + 3, :]),
                   ALU.subtract).then_inc(tlo_done, 1)

            def preps(u0, groups):
                with dve.Fori(0, groups) as i:
                    for s in range(4):
                        prep(u0 + 4 * i + s + AHEAD, (s + AHEAD) % 4, (s + AHEAD) % 2)

            def boundary(b):
                nb = 2 * b + NORMS_BEFORE
                lg, ng, lo_, no_, ls, ts = BOUND[b]
                inverse_root(nb, S[:, 8, :], NT)
                for j in range(KC):
                    own(STT(y[:, j, :], y[:, j, :], gcol(lg, ng, j), S[:, 8, :], ALU.mult, ALU.mult))
                    TT(x[:, j, :], x[:, j, :], y[:, j, :], ALU.add).then_inc(x_done, 1)
                if b == 3:
                    return
                inverse_root(nb + 1, S[:, 9, :], NT)
                dve.wait_ge(x_done, KC * (b + 1))
                operand(b + 2, x, y, S[:, 9, :], gain[:, lo_, no_, :], hhi, hlo, ls, ts, 0)
                modulation(b + 2)

            def quarter(l, q, last=False):
                u0 = (U_MLP0, U_MLP1)[l] + 16 * q
                c0 = l * 32 + 8 * q
                for j in range(8):
                    prep(u0 + j + AHEAD, (j + AHEAD) % 4, (j + AHEAD) % 2)
                    dve.wait_ge(ghi_done, c0 + j + 1)
                    TT(glo[:, j, :], S[:, 10 + j % 2, :], f(ghi[:, j, :]), ALU.subtract).then_inc(g_done, 1)
                for j in range(8):
                    u = u0 + 8 + j
                    if not last or u + AHEAD < UNITS:
                        prep(u + AHEAD, (j + AHEAD) % 4, (j + AHEAD) % 2)
                    dve.wait_ge(evac_done, u + 1)
                    if j == 0:
                        dve.wait_ge(y_zero, l + 1)
                        if not isinstance(c0, int) or c0:
                            dve.wait_ge(y_done, c0)
                    TT(y[:, j, :], y[:, j, :], S[:, 8 + j % 2, :], ALU.add).then_inc(y_done, 1)

            preps(U_OUT0, OUT_UNITS // 4)
            boundary(0)
            quarter(0, 0)
            with dve.Fori(1, QUARTERS) as q:
                quarter(0, q)
            boundary(1)

            def hy_prep(n):
                u = U_HY + n + AHEAD
                prep(u, u % 4, u % 2)

            def hy_unit(n):
                dve.wait_ge(evac_done, U_HY + n + 1)
                dst = y[:, n, :] if n < KC else es[:, 1, :]
                own(STT(dst[:, 1:NT], es[:, 0, 0:NT - 1], col[:, C_CW + n:C_CW + n + 1], dst[:, 1:NT],
                        ALU.mult, ALU.add))
                ins = STT(dst[:, 0:NT - 1], es[:, 0, 1:NT], col[:, C_CW + 48 + n:C_CW + 49 + n], dst[:, 0:NT - 1],
                          ALU.mult, ALU.add)
                if n >= KC:
                    own(ins)
                    ins = TT(y[:, n % KC, :], y[:, n % KC, :], dst, ALU.mult)
                ins.then_inc(tap_done, 1)

            def spectrum_a(m):
                dve.wait_ge(odd_done, 2 * m + 2)
                if m:
                    dve.wait_ge(spec_lo, 4 * m)
                c, c_, s, s_, e2, e3 = S[:, 8, :], S[:, 9, :], S[:, 10, :], S[:, 11, :], es[:, 2, :], es[:, 3, :]
                own(TT(c, SC[:, 0, :], c_, ALU.add))
                own(TT(c_, SC[:, 0, :], c_, ALU.subtract))
                own(TT(s_, s, SD[:, 0, :], ALU.subtract))
                TT(s, SD[:, 0, :], s, ALU.add).then_inc(spec_free, 1)
                dve.wait_ge(filt_in, 16 * (m + 1))
                dve.wait_ge(spec_free, m + 1)
                own(TT(e2, c, FP, ALU.mult))
                own(TT(e3, s, FQ, ALU.mult))
                own(TT(e2, e2, e3, ALU.subtract))
                own(TT(c, c, FQ, ALU.mult))
                own(TT(s, s, FP, ALU.mult))
                own(TT(c, c, s, ALU.add))

            def spectrum_b(m):
                c, c_, s, s_, e2, e3 = S[:, 8, :], S[:, 9, :], S[:, 10, :], S[:, 11, :], es[:, 2, :], es[:, 3, :]
                own(TT(e3, c_, FP_, ALU.mult))
                own(TT(s, s_, FQ_, ALU.mult))
                own(TT(e3, e3, s, ALU.subtract))
                own(TT(c_, c_, FQ_, ALU.mult))
                TT(s_, s_, FP_, ALU.mult).then_inc(filt_used, 1)
                dve.wait_ge(filt_used, m + 1)
                own(TT(c_, c_, s_, ALU.add))
                TT(SPEC[0], e2, e3, ALU.add).then_inc(spec_full, 1)
                dve.wait_ge(spec_full, 4 * m + 1)
                TT(SPEC[1], e2, e3, ALU.subtract).then_inc(spec_full, 1)
                TT(SPEC[2], c, c_, ALU.add).then_inc(spec_full, 1)
                dve.wait_ge(spec_full, 4 * m + 3)
                TT(SPEC[3], c, c_, ALU.subtract).then_inc(spec_full, 1)
                for e in range(4):
                    dve.wait_ge(spec_hi, 4 * m + e + 1)
                    TT(glo[:, 2 * e + m % 2, :], SPEC[e], f(ghi[:, 2 * e + m % 2, :]),
                       ALU.subtract).then_inc(spec_lo, 1)

            for n in range(4):
                hy_prep(n)
                hy_unit(n)
            for k, (o, c) in enumerate(STAGES):
                for tt in range(4):
                    dve.wait_ge(zhi_done, 4 * k + tt + 1)
                    TT(zlo[:, tt, :], SCD[tt // 2][:, tt % 2, :], f(zhi[:, tt, :]), ALU.subtract).then_inc(zlo_done, 1)
                for s in range(4):
                    hy_prep(4 * (k + 1) + s)
                    (spectrum_a, spectrum_b)[s % 2](2 * k + s // 2)
                    hy_unit(4 * (k + 1) + s)
                for i in range(4):
                    j = 4 * c + i
                    dve.wait_ge(inv_done, 4 * k + i + 1)
                    dve.wait_ge(skip_done, 4 * k + i + 1)
                    v = y[:, j, :].rearrange("p (m two) -> p two m", two=2)
                    STT(v, (B2, B3)[i % 2][:, :].rearrange("p (two m) -> p two m", two=2), 1.0 / 512, v,
                        ALU.mult, ALU.add).then_inc(conv_done, 1)
                dve.wait_ge(conv_done, 4 * k + 4)
            for n in range(20, 24):
                hy_prep(n)
                hy_unit(n)
            for j in range(KC):
                dve.wait_ge(z3_hi, j + 1)
                TT(glo[:, j, :], y[:, j, :], f(ghi[:, j, :]), ALU.subtract).then_inc(z3_lo, 1)
            preps(U_OUT1, OUT_UNITS // 4)
            boundary(2)
            with dve.Fori(0, QUARTERS - 1) as q:
                quarter(1, q)
            quarter(1, QUARTERS - 1, last=True)
            boundary(3)

        @block.tensor
        def _(pe):
            mm = nc.tensor.matmul

            def mm3(o, lh, ll, rh, rl, first, last):
                mm(o, lh, rh, start=first, stop=False)
                mm(o, lh, rl, start=False, stop=False)
                return mm(o, ll, rh, start=False, stop=last)

            def unit_ready(u):
                pe.wait_ge(hi_done, u + 1)
                pe.wait_ge(lo_done, u + 1)
                if not isinstance(u, int) or u >= 2:
                    pe.wait_ge(evac_done, u - 1)

            def unit(u, s, o, hi, lo, chunk_ready=None):
                unit_ready(u)
                for k in range(KC):
                    if chunk_ready:
                        chunk_ready(k)
                    w = slice(k * P, (k + 1) * P)
                    ins = mm3(o, whi[:, s, w], wlo[:, s, w], hi[:, k, :], lo[:, k, :], k == 0, k == KC - 1)
                return ins

            def ada(a):
                pe.wait_ge(ada_in[a % 2], 16 * (a // 2 + 1))
                at = 96 * (a // 48) + 2 * (a % 48)
                for k in range(KC):
                    ins = mm(B3[:, at:at + 2], araw[:, a % 2, k * P:(k + 1) * P], ce[:, k, :],
                             start=k == 0, stop=k == KC - 1)
                ins.then_inc(ada_done, 1)

            def add_squares(nb, j, w):
                pe.wait_ge(sq_done, nb * KC + j + 1)
                if j == 0 and nb:
                    pe.wait_ge(sd_done, nb)
                mm(B2[:, 0:w], ones, S[:, 10 + j % 2, 0:w], start=j == 0, stop=j == KC - 1).then_inc(ss_done, 1)

            pe.wait_ge(small_in, 96)
            mm(B2[0:FH, :], S[0:NFEAT, 10, 0:FH], S[0:NFEAT, 6, :], start=True, stop=True).then_inc(fmlp_done, 1)
            pe.wait_ge(sin_done, 1)
            mm(B2[0:FH, :], S[0:FH, 10, FH:2 * FH], S[0:FH, 7, :], start=True, stop=True).then_inc(fmlp_done, 1)
            pe.wait_ge(sin_done, 2)
            pe.wait_ge(w3_in, 16)
            pe.wait_ge(silu_done, 1)
            for q in range(5):
                for n in range(4 * q, min(4 * q + 4, 16)):
                    tt = n % 4
                    if n:
                        pe.wait_ge(gen_used, n)
                    for d in range(2):
                        ins = mm(AB[:, d, :], S[0:FH, 8, tt * P:(tt + 1) * P],
                                 fs[0:FH, (2 * (q % 2) + d) * 2 + q // 2, :], start=True, stop=True)
                    ins.then_inc(gen_done, 1)
                    ada(n)
                if q >= 1:
                    hi, lo = FPAIR[(q - 1) % 2]
                    pe.wait_ge(eo_lo, 8 * q)
                    pe.wait_ge(tlo_done, 1)
                    for ft in range(2):
                        m = 2 * (q - 1) + ft
                        if m:
                            pe.wait_ge(fout_done, 4 * m)
                        for kind, bank in ((CE, SC[:, 0, :]), (CO, SC[:, 1, :]), (SE, SD[:, 0, :]), (SO, SD[:, 1, :])):
                            at = (4 if kind in (SE, SO) else 0) + (2 if kind in (CO, SO) else 0)
                            for kt in range(2):
                                w = slice(kt * 256 + ft * P, kt * 256 + (ft + 1) * P)
                                ins = mm3(bank, thi[:, kind, w], tlo[:, kind, w], hi[:, at + kt, :],
                                          lo[:, at + kt, :], kt == 0, kt == 1)
                        ins.then_inc(fdft_done, 1)

            for j in range(KC):
                add_squares(0, j, NC)
            for j in range(KC):
                add_squares(1, j, NT)

            for t in range(QKV_UNITS + 2):
                if t < NKV:
                    unit_ready(t)
                    for kt in range(KT):
                        th, tl = (hhi, hlo) if kt < NT // P else (chi, clo)
                        at = (kt if kt < NT // P else kt - NT // P) * P
                        for k in range(KC):
                            if kt == 0:
                                pe.wait_ge(h_done, KC + k + 1)
                            w = slice(k * P, (k + 1) * P)
                            ins = mm3(SCD[t][:, kt // 3, kt % 3 * P:(kt % 3 + 1) * P], th[:, k, at:at + P],
                                      tl[:, k, at:at + P], whi[:, t % 4, w], wlo[:, t % 4, w], k == 0, k == KC - 1)
                    ins.then_inc(unit_done, 1)
                elif t < 2 * NKV:
                    g = t - NKV
                    pe.wait_ge(vlo_done, 2 * g + 2)
                    unit(t, t % 4, SCD[g][:, 0, :], hhi, hlo)
                    unit(t, t % 4, SCD[g][:, 1, 0:NC], chi, clo).then_inc(unit_done, 1)
                elif t < QKV_UNITS:
                    unit(t, t % 4, AB[:, t % 2, :], hhi, hlo).then_inc(unit_done, 1)
                for n, (_, ps, w, r, key, hi, lo) in jobs_of(t - 2):
                    if r is not None:
                        pe.wait_ge(job_qn, n + 1)
                        if r:
                            pe.wait_ge(job_sin, r)
                        mm(B3[:, :], rotm, S[:, 8 + n % 2, :], start=True, stop=True).then_inc(job_rot, 1)
                for n, (_, ps, w, r, key, hi, lo) in jobs_of(t - 1):
                    pe.wait_ge(job_sq, n + 1)
                    if n:
                        pe.wait_ge(job_sd, n)
                    mm(B2[:, 0:w], ones, S[:, 4 + n % 2, 0:w], start=True, stop=True).then_inc(job_ss, 1)

            def prob_values(m):
                pe.wait_ge(plo_done, 4 * m + 4)
                if m:
                    pe.wait_ge(olo_done, m)
                g = m // 2 // GROUP
                for kt in range(KT):
                    ins = mm3(B2[:, (m % 2) * 2 * P:(m % 2 + 1) * 2 * P], vhi[:, kt, g, :], vlo[:, kt, g, :],
                              phi[:, m % 2, kt, :], plo[:, m % 2, kt, :], kt == 0, kt == KT - 1)
                ins.then_inc(pv_done, 1)

            for n in range(NQ + 4):
                if n < NQ:
                    h, qt = divmod(n, QT)
                    g = h // GROUP
                    pe.wait_ge(job_lo, len(JOBS) - NH + h + 1)
                    if n >= 2:
                        pe.wait_ge(exp_done, n - 1)
                    w = slice(qt * P, (qt + 1) * P)
                    mm3(SCD[n % 2][:, 0, :], ghi[:, h, w], glo[:, h, w], khi[:, g, 0:NT], klo[:, g, 0:NT], True, True)
                    mm3(SCD[n % 2][:, 1, 0:NC], ghi[:, h, w], glo[:, h, w], khi[:, g, NT:NK], klo[:, g, NT:NK],
                        True, True).then_inc(score_done, 1)
                m = n - 2
                if 0 <= m < NQ:
                    pe.wait_ge(p_done, m + 1)
                    if m:
                        pe.wait_ge(plo_done, 2 * m)
                    for kt in range(KT):
                        ins = nc.tensor.transpose(AB[:, kt // 3, kt % 3 * P:(kt % 3 + 1) * P],
                                                  PROB[m % 2][:, kt * P:(kt + 1) * P], ident)
                    ins.then_inc(pt_done, 1)
                if n < ADA_BATCHES[1]:
                    ada(ADA_START[1] + n)
                if n >= 5 and n % 2 == 1:
                    prob_values((n - 5) // 2)

            def boundary(b):
                nb = 2 * b + NORMS_BEFORE
                for j in range(KC):
                    add_squares(nb, j, NT)
                if b == 3:
                    return
                a, n = ADA_START[b + 2], ADA_BATCHES[b + 2]
                pe.wait_ge(mod_done, b + 2)
                for j in range(KC):
                    add_squares(nb + 1, j, NT)
                    ada(a + j)
                for j in range(KC, n):
                    ada(a + j)

            def out_units(u0, hi, lo, ready):
                with pe.Fori(0, OUT_UNITS // 4) as i:
                    for s in range(4):
                        unit(u0 + 4 * i + s, s, AB[:, s % 2, :], hi, lo,
                             ready if s == 0 else None).then_inc(unit_done, 1)

            def quarter(l, q):
                u0 = (U_MLP0, U_MLP1)[l] + 16 * q
                c0 = l * 32 + 8 * q
                for j in range(8):
                    unit(u0 + j, j % 4, AB[:, j % 2, :], hhi, hlo,
                         (lambda k: pe.wait_ge(h_done, (2 + 2 * l) * KC + k + 1)) if j == 0 else None
                         ).then_inc(unit_done, 1)
                for j in range(8):
                    unit(u0 + 8 + j, j % 4, AB[:, j % 2, :], ghi, glo,
                         (lambda k: pe.wait_ge(g_done, c0 + k + 1)) if j == 0 else None).then_inc(unit_done, 1)

            pe.wait_ge(plo_done, 2 * NQ)
            out_units(U_OUT0, hhi, hlo, lambda k: pe.wait_ge(olo_done, NQ // 2))
            boundary(0)
            with pe.Fori(0, QUARTERS) as q:
                quarter(0, q)
            boundary(1)

            def hy_unit(n):
                u = U_HY + n
                unit(u, u % 4, AB[:, n % 2, :], hhi, hlo,
                     (lambda k: pe.wait_ge(h_done, 3 * KC + k + 1)) if n == 0 else None).then_inc(unit_done, 1)

            for n in range(4):
                hy_unit(n)
            for k, (o, c) in enumerate(STAGES):
                pe.wait_ge(tap_done, 4 * (k + 1))
                if k:
                    pe.wait_ge(spec_free, 2 * k)
                    pe.wait_ge(conv_done, 4 * k)
                for tt in range(4):
                    for i in range(4):
                        at = tt // 2 + 256 * (tt % 2)
                        ins = nc.tensor.transpose(SCD[tt // 2][:, tt % 2, i * P:(i + 1) * P],
                                                  y[:, 4 * c + i, at:at + 255:2], ident)
                    ins.then_inc(zt_done, 1)
                for s in range(4):
                    ft = s // 2
                    if s % 2 == 0:
                        if ft == 0:
                            pe.wait_ge(zlo_done, 4 * k + 4)
                            pe.wait_ge(tlo_done, 3)
                        else:
                            pe.wait_ge(spec_free, 2 * k + 1)
                        for kind, bank in ((CE, SC[:, 0, :]), (CO, SC[:, 1, :]), (SE, SD[:, 0, :]), (SO, SD[:, 1, :])):
                            at = 2 if kind in (CO, SO) else 0
                            for kt in range(2):
                                w = slice(kt * 256 + ft * P, kt * 256 + (ft + 1) * P)
                                ins = mm3(bank, t2hi[:, kind, w], t2lo[:, kind, w], zhi[:, at + kt, :],
                                          zlo[:, at + kt, :], kt == 0, kt == 1)
                        ins.then_inc(dft_done, 1)
                    hy_unit(4 * (k + 1) + s)
                pe.wait_ge(spec_lo, 8 * k + 8)
                pe.wait_ge(mod_done, 4)
                for i in range(4):
                    if 4 * k + i >= 2:
                        pe.wait_ge(conv_done, 4 * k + i - 1)
                    bank = (B2, B3)[i % 2]
                    w = slice(i * P, (i + 1) * P)
                    for half, terms in enumerate((((0, CEI), (3, SEI)), ((1, CO), (2, SO)))):
                        for a, (e, kind) in enumerate(terms):
                            for ft in range(2):
                                r = slice(ft * 256, (ft + 1) * 256)
                                ins = mm3(bank[:, half * 256:(half + 1) * 256], ghi[:, 2 * e + ft, w],
                                          glo[:, 2 * e + ft, w], t2hi[:, kind, r], t2lo[:, kind, r],
                                          a == 0 and ft == 0, a == 1 and ft == 1)
                    ins.then_inc(inv_done, 1)
            for n in range(20, 24):
                hy_unit(n)
            out_units(U_OUT1, ghi, glo, lambda k: pe.wait_ge(z3_lo, k + 1))
            boundary(2)
            with pe.Fori(0, QUARTERS) as q:
                quarter(1, q)
            boundary(3)


def even_first(n):
    return np.concatenate([np.arange(0, n, 2), np.arange(1, n, 2)])


def shape_tables():
    f32 = np.float32
    q = P // 4
    rot = np.zeros((P, P), f32)
    for o in range(P):
        quarter, r = divmod(o, q)
        rot[(quarter ^ 1) * q + r, o] = -1.0 if quarter % 2 == 0 else 1.0
    consts = np.stack([np.eye(P, dtype=f32), np.ones((P, P), f32), rot], axis=1)
    t = np.arange(NT)
    nf = HD // 4
    inv = (f32(10000.0) ** (-np.arange(nf, dtype=f32) / f32(nf))).astype(f32)
    ar = (t // GRID_W).astype(f32)[None] * inv[:, None]
    ac = (t % GRID_W).astype(f32)[None] * inv[:, None]
    ang = np.concatenate([ar, ar, ac, ac], axis=0)
    ropes = np.stack([np.cos(ang), np.sin(ang)], axis=1).astype(f32)
    tl = np.linspace(0.0, 1.0, NT, dtype=f32)
    w = (f32(2.0 * math.pi) * np.arange(NT, dtype=f32) / f32(NT)).astype(f32)
    bands = np.linspace(1e-4, 15, 16, dtype=f32)
    bw = (bands[:, None] * w[None]).astype(f32)
    feats = np.concatenate([tl[None], np.cos(bw), -np.sin(bw)], axis=0).astype(f32)
    deltas = np.abs(np.linspace(math.log(1e-2) / 0.3, math.log(1e-2) / 1.5, D, dtype=f32))
    window = np.exp(-tl[:, None] * deltas[None]).astype(f32)
    order = even_first(NT)
    window = window[order].reshape(4, P, 2, NT).transpose(2, 0, 1, 3)
    k = np.arange(256)[None]
    m = np.arange(256)[:, None]
    even = np.pi * (2 * k + 1) * (2 * m) / 1024.0
    odd = np.pi * (2 * k + 1) * (2 * m + 1) / 1024.0
    kinds = [np.cos(even), np.cos(odd), np.sin(even), np.sin(odd), np.cos(even).T, np.sin(even).T]
    tables = np.stack([a.astype(f32).reshape(2, P, 256).transpose(1, 0, 2).reshape(P, 512) for a in kinds], axis=1)
    return consts, ropes, np.ascontiguousarray(feats[:, order]), np.ascontiguousarray(window), tables


def units_of(w):
    n = w.shape[1] // P
    return w.reshape(KC, P, n, P).transpose(2, 1, 0, 3).reshape(n, P, D)


def kernel(**inputs):
    import concourse.bacc as bacc
    from concourse.bass_utils import run_bass_kernel_spmd

    a = {k: np.asarray(v) for k, v in inputs.items()}
    f32 = np.float32

    def mlp_units(l):
        w1, w2 = a["mlp_w1"][l], a["mlp_w2"][l]
        parts = []
        for q in range(QUARTERS):
            parts += [units_of(w1[:, q * D:(q + 1) * D]), units_of(w2[q * D:(q + 1) * D])]
        return parts

    win = units_of(a["ga_w_in"][0])
    wpack = np.concatenate([win[10:12], win[8:10], win[0:8], units_of(a["ga_w_out"][0])] + mlp_units(0)
                           + [units_of(a["hy_w_in"][0]), units_of(a["hy_w_out"][0])] + mlp_units(1))
    apack = np.concatenate([units_of(a["ada_w"][0]), units_of(a["ada_w"][1])])

    def chunks(v):
        return v.reshape(-1, P).T

    cols = np.zeros((P, NCOLS), f32)
    cols[:, C_G:C_G + 64] = chunks(a["norm_g"])
    cols[:, C_AB:C_AB + 96] = chunks(a["ada_b"])
    cols[:, C_QG:C_QG + 1] = chunks(a["ga_q_gain"])
    cols[:, C_KG:C_KG + 1] = chunks(a["ga_k_gain"])
    cols[:, C_CW:C_CW + 72] = chunks(a["hy_conv_w"])
    cols[:, C_CB:C_CB + 24] = chunks(a["hy_conv_b"])
    cols[:, C_SK:C_SK + 16] = chunks(a["hy_skip"])
    cols[0:FH, C_F] = a["hy_f_b1"][0]
    cols[0:FH, C_F + 1] = a["hy_f_b2"][0]
    cols[0:FH, C_F + 2:C_F + 4] = a["hy_f_freq"][0].T
    consts, ropes, feats, window, tables = shape_tables()
    cT = np.stack([a["c"][0], a["c_ctx"]], axis=-1).reshape(KC, P, 2).transpose(1, 0, 2)
    arrays = {
        "xT": a["x"][0].T.reshape(KC, P, NT).transpose(1, 0, 2),
        "ctxT": a["ctx"][0].T.reshape(KC, P, NC).transpose(1, 0, 2),
        "cT": cT, "cols": cols, "wpack": wpack, "apack": apack,
        "fw1": a["hy_f_w1"][0], "fw2": a["hy_f_w2"][0], "fw3": a["hy_f_w3"][0].reshape(FH, 8, NT),
        "featsT": feats, "decay": window, "tables": tables, "consts": consts, "ropes": ropes,
    }
    arrays = {k: np.ascontiguousarray(v) for k, v in arrays.items()}
    nc = bacc.Bacc("TRN2", target_bir_lowering=False, num_devices=1)
    args = [nc.dram_tensor(f"in_{k}", v.shape, F32, kind="ExternalInput").ap() for k, v in arrays.items()]
    args.append(nc.dram_tensor("spectra", [8, P, 4, NT], F32, kind="Internal").ap())
    args.append(nc.dram_tensor("outT", [KC, P, NT], F32, kind="ExternalOutput").ap())
    build(nc, *args)
    r = run_bass_kernel_spmd(nc, [{f"in_{k}": v for k, v in arrays.items()}], core_ids=[0])
    o = r.results[0]["outT"]
    return np.ascontiguousarray(o.reshape(D, NT).T)[None]
```

```python
import math
from contextlib import ExitStack

import concourse.bass as bass
import concourse.mybir as mybir
import numpy as np

F32 = mybir.dt.float32
F32R = mybir.dt.float32r
ALU = mybir.AluOpType
ACT = mybir.ActivationFunctionType
AX = mybir.AxisListType

P = 128
D = 1024
KC = D // P
NT = 512
NC = 256
NK = NT + NC
KT = NK // P
HD = 128
NH = 8
NKV = 2
GROUP = NH // NKV
QT = NT // P
EPS = 1e-6
FH = 64
NFEAT = 33
GRID_W = 64
QUARTERS = 4
QKV_UNITS = 12
OUT_UNITS = 8
MLP_UNITS = QUARTERS * 16
HY_UNITS = 24
U_QKV = 0
U_OUT0 = U_QKV + QKV_UNITS
U_MLP0 = U_OUT0 + OUT_UNITS
U_HY = U_MLP0 + MLP_UNITS
U_OUT1 = U_HY + HY_UNITS
U_MLP1 = U_OUT1 + OUT_UNITS
UNITS = U_MLP1 + MLP_UNITS
AHEAD = 3
ADA_START = [0, 16, 48, 96]
ADA_RING = 4
ADA_QUARTER = 48 // QUARTERS
C_G, C_AB, C_QG, C_KG = 0, 64, 160, 161
C_CW, C_CB, C_SK, C_F = 162, 234, 258, 274
NCOLS = 280
CE, CO, SE, SO, CEI, SEI = range(6)
TWO_PI_A = 6.28125
TWO_PI_B = float(np.float32(2 * math.pi - 6.28125))
TWO_PI_C = float(np.float32(2 * math.pi - 6.28125 - TWO_PI_B))
MAGIC = 12582912.0


def build(nc, xT, ctxT, cT, cols, wpack, apack, fw1, fw2, fw3, featsT, decay, tables, consts, ropes, fdram, out):
    with ExitStack() as ctx:
        def sb(name, shape, dt=F32, stack=ctx):
            return stack.enter_context(nc.sbuf_tensor(name, shape, dt))

        def sem(name):
            return ctx.enter_context(nc.semaphore(name))

        raw = sb("raw", [P, 2, D])
        whi = sb("whi", [P, 4, D], F32R)
        wlo = sb("wlo", [P, 4, D], F32R)
        araw = sb("araw", [P, 2, D])
        x = sb("x", [P, KC, NT])
        hhi = sb("hhi", [P, KC, NT], F32R)
        hlo = sb("hlo", [P, KC, NT], F32R)
        ghi = sb("ghi", [P, KC, NT], F32R)
        glo = sb("glo", [P, KC, NT], F32R)
        S = sb("scratch", [P, 12, NT])
        cst = sb("consts", [P, 3, P])
        col = sb("cols", [P, NCOLS])
        cs = sb("cs", [P, KC, 2])
        ce = sb("ce", [P, KC, 2])
        mods = sb("mods", [P, 2, 96])
        gain = sb("gain", [P, 2, 4, KC])
        gainc = sb("gainc", [P, KC])
        nmax = sb("nmax", [P, 2])
        rsum = sb("rsum", [P, 2])
        rinv = sb("rinv", [P, 2])
        asum = sb("asum", [P, ADA_QUARTER])
        qg = sb("qg", [P, 1])
        epst = sb("eps", [P, 1])
        ident, ones, rotm = (cst[:, n, :] for n in range(3))
        y = S[:, 0:KC, :]
        with ExitStack() as area:
            thi = sb("thi", [P, 6, NT], F32R, area)
            tlo = sb("tlo", [P, 6, NT], F32R, area)
            fs = sb("fs", [P, 12, NT], F32, area)
        with ExitStack() as area:
            khi = sb("khi", [P, NKV, NK], F32R, area)
            klo = sb("klo", [P, NKV, NK], F32R, area)
            vhi = sb("vhi", [P, KT, NKV, HD], F32R, area)
            vlo = sb("vlo", [P, KT, NKV, HD], F32R, area)
            phi = sb("phi", [P, 2, KT, 2 * P], F32R, area)
            plo = sb("plo", [P, 2, KT, 2 * P], F32R, area)
        with ExitStack() as area:
            sb("below", [P, 4 * NKV * NK], F32, area)
            chi = sb("chi", [P, KC, NC], F32R, area)
            clo = sb("clo", [P, KC, NC], F32R, area)
            ctxs = sb("ctxs", [P, KC, NC], F32, area)
        with ExitStack() as area:
            t2hi = sb("t2hi", [P, 6, NT], F32R, area)
            t2lo = sb("t2lo", [P, 6, NT], F32R, area)
            zhi = sb("zhi", [P, 4, NT], F32R, area)
            zlo = sb("zlo", [P, 4, NT], F32R, area)
            es = sb("es", [P, 4, NT], F32, area)
        with ExitStack() as area:
            sb("below2", [P, 12 * NT], F32, area)
            amore = sb("amore", [P, ADA_RING - 2, D], F32, area)
            crow1 = sb("crow1", [P, D], F32, area)

        AB = ctx.enter_context(nc.psum_tensor("bank01", [P, 2, NT], F32))
        B2 = ctx.enter_context(nc.psum_tensor("bank2", [P, NT], F32))
        B3 = ctx.enter_context(nc.psum_tensor("bank3", [P, NT], F32))
        SC = ctx.enter_context(nc.psum_tensor("bank45", [P, 2, NT], F32))
        SD = ctx.enter_context(nc.psum_tensor("bank67", [P, 2, NT], F32))
        SCD = (SC, SD)

        small_in = sem("small_in")
        x_in = sem("x_in")
        table_in = sem("table_in")
        w3_in = sem("w3_in")
        decay_in = [sem(f"decay_in{n}") for n in range(2)]
        ctx_in = sem("ctx_in")
        rope_in = sem("rope_in")
        table2_in = sem("table2_in")
        filt_in = sem("filt_in")
        filt_out = sem("filt_out")
        raw_in = [sem(f"raw_in{n}") for n in range(2)]
        ada_in = [sem(f"ada_in{n}") for n in range(2)]
        arow_in = [sem(f"arow_in{n}") for n in range(ADA_RING)]
        ysq_done = sem("ysq_done")
        yss_done = sem("yss_done")
        own_pool2 = sem("own_pool2")
        x_out = sem("x_out")
        hi_done = sem("hi_done")
        lo_done = sem("lo_done")
        unit_done = sem("unit_done")
        evac_done = sem("evac_done")
        eps_set = sem("eps_set")
        silu_e = sem("silu_e")
        silu_done = sem("silu_done")
        ada_done = sem("ada_done")
        mod_done = sem("mod_done")
        cdiag_done = sem("cdiag_done")
        csum_done = sem("csum_done")
        crow_done = sem("crow_done")
        amul_done = sem("amul_done")
        asum_done = sem("asum_done")
        asum1_done = sem("asum1_done")
        bias_done = sem("bias_done")
        sin_arg = sem("sin_arg")
        sin_done = sem("sin_done")
        fmlp_done = sem("fmlp_done")
        thi_done = sem("thi_done")
        tlo_done = sem("tlo_done")
        gen_done = sem("gen_done")
        gen_used = sem("gen_used")
        eo_full = sem("eo_full")
        eo_hi = sem("eo_hi")
        eo_lo = sem("eo_lo")
        fdft_done = sem("fdft_done")
        fodd_done = sem("fodd_done")
        fout_done = sem("fout_done")
        sq_done = sem("sq_done")
        ss_done = sem("ss_done")
        sd_done = sem("sd_done")
        rs_done = sem("rs_done")
        x_done = sem("x_done")
        ht_done = sem("ht_done")
        hhi_done = sem("hhi_done")
        h_done = sem("h_done")
        vlo_done = sem("vlo_done")
        job_sq = sem("job_sq")
        job_ss = sem("job_ss")
        job_sd = sem("job_sd")
        job_qn = sem("job_qn")
        job_rot = sem("job_rot")
        job_cos = sem("job_cos")
        job_sin = sem("job_sin")
        job_full = sem("job_full")
        job_hi = sem("job_hi")
        job_lo = sem("job_lo")
        score_done = sem("score_done")
        nmax_done = sem("nmax_done")
        exp_done = sem("exp_done")
        rinv_done = sem("rinv_done")
        p_done = sem("p_done")
        pt_done = sem("pt_done")
        phi_done = sem("phi_done")
        plo_done = sem("plo_done")
        pv_done = sem("pv_done")
        ohi_done = sem("ohi_done")
        olo_done = sem("olo_done")
        g_full = sem("g_full")
        ghi_done = sem("ghi_done")
        g_done = sem("g_done")
        y_done = sem("y_done")
        y_zero = sem("y_zero")
        tap_done = sem("tap_done")
        zt_done = sem("zt_done")
        zhi_done = sem("zhi_done")
        zlo_done = sem("zlo_done")
        dft_done = sem("dft_done")
        odd_done = sem("odd_done")
        spec_free = sem("spec_free")
        filt_used = sem("filt_used")
        spec_full = sem("spec_full")
        spec_hi = sem("spec_hi")
        spec_lo = sem("spec_lo")
        inv_done = sem("inv_done")
        skip_done = sem("skip_done")
        conv_done = sem("conv_done")
        z3_hi = sem("z3_hi")
        z3_lo = sem("z3_lo")
        own_act = sem("own_act")
        own_dve = sem("own_dve")
        own_pool = sem("own_pool")

        block = ctx.enter_context(nc.Block())

        FPAIR = ((ghi, glo), (hhi, hlo))
        HF = (fs[:, 8, :], S[:, 4, :])
        FE = (fs[:, 9, :], S[:, 5, :])
        HB = fs[:, 10, :]
        DEC = (fs[:, 11, :], S[:, 9, :])
        JOBS = []
        for g in range(NKV):
            ps = SCD[g]
            JOBS.append((2 + g, ps[:, 0, :], NT, g, True, khi[:, g, 0:NT], klo[:, g, 0:NT]))
            JOBS.append((2 + g, ps[:, 1, 0:NC], NC, None, True, khi[:, g, NT:NK], klo[:, g, NT:NK]))
        for h in range(NH):
            JOBS.append((4 + h, AB[:, h % 2, :], NT, NKV + h, False, ghi[:, h, :], glo[:, h, :]))
        ROPE = [n for n, job in enumerate(JOBS) if job[3] is not None]

        SCORE = [b[:, :, :].rearrange("p a b -> p (a b)")[:, 0:NK] for b in SCD]
        PROB = [S[:, 2 * n:2 * n + 2, :].rearrange("p a b -> p (a b)")[:, 0:NK] for n in range(2)]
        FP, FP_, FQ, FQ_ = (araw[:, n // 2, n % 2 * NT:(n % 2 + 1) * NT] for n in range(4))
        SPEC = (S[:, 10, :], es[:, 2, :], S[:, 11, :], S[:, 8, :])

        def jobs_of(t):
            return [(n, job) for n, job in enumerate(JOBS) if job[0] == t]

        NQ = NH * QT
        STAGES = [(0, 0), (0, 1), (1, 0), (1, 1)]
        UNITS_V, UNITS_X1, UNITS_X2 = U_HY, U_HY + 8, U_HY + 16
        BETWEEN = [UNITS_V + 4, UNITS_X1, UNITS_X1 + 4, UNITS_X2]
        BOUND = [(0, 1, 0, 2, 0, 24), (0, 3, 1, 0, 1, 0), (1, 1, 1, 2, 1, 24), (1, 3, None, None, None, None)]
        NORMS_BEFORE = 2
        FCOL = {n: C_F + n for n in range(4)}

        def f(ap):
            return ap.bitcast(F32)

        crow = S[:, 6:8, :].rearrange("p a b -> p (a b)")

        def arow_slot(a, k):
            if k < 2:
                return araw[:, k, :]
            if a < 48:
                return S[:, 4 + 2 * k:6 + 2 * k, :].rearrange("p a b -> p (a b)")
            return amore[:, k - 2, :]

        def gcol(l, n, j):
            return gain[:, l, n, j:j + 1]

        def shift(l, t, j, v=0):
            return mods[:, v, 48 * l + t + j:48 * l + t + j + 1]

        class Own:

            def __init__(self, eng, s):
                self.eng, self.s, self.n = eng, s, 0

            def __call__(self, ins):
                self.n += 1
                ins.then_inc(self.s, 1)
                self.eng.wait_ge(self.s, self.n)

        @block.sync
        def _(sp):
            sp.dma_start(cst[:, :, :], consts).then_inc(small_in, 16)
            sp.dma_start(col[:, :], cols).then_inc(small_in, 16)
            sp.dma_start(cs[:, :, :], cT).then_inc(small_in, 16)
            sp.dma_start(S[0:NFEAT, 6, :], featsT).then_inc(small_in, 16)
            sp.dma_start(S[0:NFEAT, 10, 0:FH], fw1).then_inc(small_in, 16)
            sp.dma_start(S[0:FH, 10, FH:2 * FH], fw2).then_inc(small_in, 16)
            sp.dma_start(S[:, 0:6, :], tables).then_inc(table_in, 16)
            sp.dma_start(fs[0:FH, 0:8, :], fw3).then_inc(w3_in, 16)

            def load_decay(n):
                q, tt = divmod(n, 4)
                sp.dma_start(DEC[n % 2], decay[q // 2, tt]).then_inc(decay_in[n % 2], 16)

            load_decay(0)
            sp.dma_start(x[:, :, :], xT).then_inc(x_in, 16)
            sp.dma_start(raw[:, 0, :], wpack[0]).then_inc(raw_in[0], 16)
            sp.dma_start(raw[:, 1, :], wpack[1]).then_inc(raw_in[1], 16)
            sp.wait_ge(sin_done, 2)
            load_decay(1)
            for q in range(5):
                for n in range(4 * q, min(4 * q + 4, 16)):
                    if n >= 2:
                        sp.wait_ge(gen_used, n - 1)
                        load_decay(n)
                if q >= 1:
                    for ft in range(2):
                        m = 2 * (q - 1) + ft
                        sp.wait_ge(fout_done, 4 * m + 4)
                        sp.dma_start(fdram[m], S[:, 0:4, :]).then_inc(filt_out, 16)
            sp.wait_ge(fdft_done, 8)
            sp.wait_ge(eo_lo, 32)
            sp.dma_start(ctxs[:, :, :], ctxT).then_inc(ctx_in, 16)

            def load_unit(u, s):
                sp.wait_ge(hi_done, u - 1)
                sp.wait_ge(lo_done, u - 1)
                sp.dma_start(raw[:, s, :], wpack[u]).then_inc(raw_in[s], 16)

            def load_units(u0, u1):
                if u0 % 2:
                    load_unit(u0, 1)
                    u0 += 1
                with sp.Fori(0, (u1 - u0) // 2) as i:
                    for s in range(2):
                        load_unit(u0 + 2 * i + s, s)
                if u1 % 2:
                    load_unit(u1 - 1, 0)

            load_units(2, U_OUT0 + 5)
            sp.wait_ge(job_sin, len(ROPE))
            sp.wait_ge(job_cos, len(ROPE))
            sp.wait_ge(job_lo, len(JOBS))
            for a in range(16, 48):
                if a >= 16 + ADA_RING:
                    sp.wait_ge(asum_done, a - 16 - ADA_RING + 1)
                sp.dma_start(arow_slot(a, a % ADA_RING), apack[a]).then_inc(arow_in[a % ADA_RING], 16)
            load_units(U_OUT0 + 5, U_MLP0 + 5)
            sp.wait_ge(asum_done, 32)
            sp.wait_ge(olo_done, NQ // 2)
            for k in range(ADA_RING):
                sp.dma_start(arow_slot(48, k), apack[48 + k]).then_inc(arow_in[k], 16)

            def load_quarter(q, last=False):
                for s in range(16):
                    load_unit(U_MLP0 + 5 + 16 * q + s, (s + 1) % 2)
                    if s < ADA_QUARTER - (ADA_RING if last else 0):
                        sp.wait_ge(asum1_done, ADA_QUARTER * q + s + 1)
                        sp.dma_start(arow_slot(48, s % ADA_RING),
                                     apack[48 + ADA_RING + ADA_QUARTER * q + s]).then_inc(arow_in[s % ADA_RING], 16)

            with sp.Fori(0, QUARTERS - 1) as q:
                load_quarter(q)
            load_quarter(QUARTERS - 1, last=True)
            load_units(U_HY + 5, UNITS)
            for j in range(KC):
                sp.wait_ge(x_done, 3 * KC + j + 1)
                sp.dma_start(out[j], x[:, j, :]).then_inc(x_out, 16)
            sp.wait_ge(filt_out, 8 * 16)
            sp.wait_ge(x_out, KC * 16)

        @block.gpsimd
        def _(pool):
            nc.gpsimd.memset(epst[:, :], EPS).then_inc(eps_set, 1)

            pool.dma_start(araw[:, 0, :], apack[0]).then_inc(ada_in[0], 16)
            pool.dma_start(araw[:, 1, :], apack[1]).then_inc(ada_in[1], 16)
            with pool.Fori(1, 8) as i:
                for s in range(2):
                    pool.wait_ge(ada_done, 2 * i + s - 1)
                    pool.dma_start(araw[:, s, :], apack[2 * i + s]).then_inc(ada_in[s], 16)
            pool.wait_ge(ada_done, 16)
            pool.dma_start(araw[:, :, 0:NT], ropes).then_inc(rope_in, 16)
            pool.wait_ge(rope_in, 16)
            for r, n in enumerate(ROPE):
                pool.wait_ge(job_qn, n + 1)
                if r >= 2:
                    pool.wait_ge(job_lo, ROPE[r - 2] + 1)
                nc.gpsimd.tensor_tensor(S[:, 10 + r % 2, :], S[:, 8 + n % 2, :], araw[:, 0, 0:NT],
                                        ALU.mult).then_inc(job_cos, 1)
            pool.wait_ge(crow_done, 1)
            for a in range(16, 48):
                pool.wait_ge(arow_in[a % ADA_RING], 16 * ((a - 16) // ADA_RING + 1))
                slot = arow_slot(a, a % ADA_RING)
                nc.gpsimd.tensor_tensor(slot, slot, crow, ALU.mult).then_inc(amul_done, 1)
            own = Own(pool, own_pool2)

            def y_squares(b):
                for j in range(KC):
                    if b % 2 == 0:
                        pool.wait_ge(evac_done, (U_OUT0, U_OUT1)[b // 2] + j + 1)
                    else:
                        pool.wait_ge(y_done, b // 2 * 32 + 24 + j + 1)
                    dst = S[:, 10 + (j == 0), :]
                    ins = nc.gpsimd.tensor_tensor(dst, y[:, j, :], y[:, j, :], ALU.mult)
                    if j:
                        own(ins)
                        ins = nc.gpsimd.tensor_tensor(S[:, 11, :], S[:, 11, :], S[:, 10, :], ALU.add)
                    ins.then_inc(ysq_done, 1)
                    pool.wait_ge(ysq_done, b * KC + j + 1)

            y_squares(0)
            pool.wait_ge(h_done, 3 * KC)
            nc.gpsimd.memset(y, 0.0).then_inc(y_zero, 1)
            pool.wait_ge(g_done, 32)
            y_squares(1)
            pool.wait_ge(asum1_done, 48)
            for k, (o, c) in enumerate(STAGES):
                for ft in range(2):
                    n = 2 * k + ft
                    if n:
                        pool.wait_ge(filt_used, n)
                    else:
                        pool.wait_ge(filt_out, 8 * 16)
                    pool.dma_start(araw[:, :, :].rearrange("p a (b n) -> p (a b) n", b=2),
                                   fdram[2 * (2 * c + o) + ft]).then_inc(filt_in, 16)
            y_squares(2)
            pool.wait_ge(h_done, 5 * KC)
            nc.gpsimd.memset(y, 0.0).then_inc(y_zero, 1)
            pool.wait_ge(g_done, 64)
            y_squares(3)

        @block.scalar
        def _(act):
            own = Own(act, own_act)
            A = nc.scalar.activation

            def prep(u, s, r):
                act.wait_ge(raw_in[r], (u - r) * 8 + 16)
                if not isinstance(u, int) or u >= 4:
                    act.wait_ge(unit_done, u - 3)
                A(whi[:, s, :], raw[:, r, :], ACT.Copy).then_inc(hi_done, 1)

            def square_sum(b, src, n, after):
                for j in range(KC):
                    m = b * KC + j
                    after(j)
                    if m >= 2:
                        act.wait_ge(ss_done, m - 1)
                    A(S[:, 10 + j % 2, 0:n], src[:, j, :], ACT.Square).then_inc(sq_done, 1)

            def root(b, dst, n):
                act.wait_ge(ss_done, KC * (b + 1))
                A(dst[:, 0:n], B2[:, 0:n], ACT.Sqrt, scale=1.0 / D, bias=epst[:, 0:1]).then_inc(sd_done, 1)

            def operand_hi(k, hi, l, t, v, buf):
                for j in range(KC):
                    act.wait_ge(ht_done, k * KC + j + 1)
                    A(hi[:, j, :], buf[:, j, :], ACT.Identity, bias=shift(l, t, j, v)).then_inc(hhi_done, 1)

            act.wait_ge(small_in, 96)
            A(ce[:, :, :], cs[:, :, :], ACT.Exp, scale=-1.0).then_inc(silu_e, 1)
            act.wait_ge(table_in, 16)
            A(thi[:, :, :], S[:, 0:6, :], ACT.Copy).then_inc(thi_done, 1)
            for k in range(2):
                act.wait_ge(sin_arg, k + 1)
                A(S[0:FH, 7 + k, :], S[0:FH, 9, :], ACT.Sin).then_inc(sin_done, 1)
            prep(0, 0, 0)
            prep(1, 1, 1)

            for q in range(5):
                for n in range(4 * q, min(4 * q + 4, 16)):
                    hi = FPAIR[q % 2][0]
                    tt = n % 4
                    if q >= 2:
                        act.wait_ge(fdft_done, 2 * (q - 1))
                    act.wait_ge(eo_full, 2 * n + 1)
                    A(hi[:, tt, :], FE[n % 2], ACT.Copy).then_inc(eo_hi, 1)
                    act.wait_ge(eo_full, 2 * n + 2)
                    A(hi[:, 4 + tt, :], HF[n % 2], ACT.Copy).then_inc(eo_hi, 1)
                if q >= 1:
                    for ft in range(2):
                        m = 2 * (q - 1) + ft
                        act.wait_ge(fdft_done, m + 1)
                        if m:
                            act.wait_ge(fout_done, 4 * m)
                        A(S[:, 10, :], SC[:, 1, :], ACT.Copy).then_inc(fodd_done, 1)
                        A(S[:, 11, :], SD[:, 1, :], ACT.Copy).then_inc(fodd_done, 1)

            act.wait_ge(fout_done, 32)
            square_sum(0, ctxs, NC, lambda j: act.wait_ge(ctx_in, 16))
            act.wait_ge(eps_set, 1)
            root(0, S[:, 9, :], NC)
            operand_hi(0, chi, 0, 0, 1, ctxs)
            square_sum(1, x, NT, lambda j: act.wait_ge(x_in, 16))
            act.wait_ge(ht_done, KC)
            root(1, S[:, 9, :], NT)
            operand_hi(1, hhi, 0, 0, 0, y)

            prep(2, 2, 0)
            for t in range(QKV_UNITS + 2):
                if t < QKV_UNITS:
                    prep(t + AHEAD, (t + AHEAD) % 4, (t + AHEAD) % 2)
                for n, (_, ps, w, r, key, hi, lo) in jobs_of(t - 2):
                    act.wait_ge(job_full, n + 1)
                    A(hi, S[:, 10 + r % 2, :] if r is not None else S[:, 8 + n % 2, 0:w], ACT.Copy).then_inc(job_hi, 1)
                for n, (_, ps, w, r, key, hi, lo) in jobs_of(t - 1):
                    act.wait_ge(job_ss, n + 1)
                    if n >= 2:
                        act.wait_ge(job_qn, n - 1)
                    A(S[:, 6 + n % 2, 0:w], B2[:, 0:w], ACT.Sqrt, scale=1.0 / HD, bias=epst[:, 0:1]).then_inc(job_sd, 1)
                if t < QKV_UNITS:
                    act.wait_ge(unit_done, t + 1)
                if t < NKV:
                    for half in range(2):
                        ps = SCD[t][:, half, 0:3 * P].rearrange("p (a b) -> p a b", a=3)
                        ins = A(vhi[:, 3 * half:3 * half + 3, t, :], ps, ACT.Copy)
                        if half == 0:
                            own(ins)
                    ins.then_inc(evac_done, 1)
                for i, (n, (_, ps, w, r, key, hi, lo)) in enumerate(jobs_of(t)):
                    if n >= 2:
                        act.wait_ge(job_ss, n - 1)
                    A(S[:, 4 + n % 2, 0:w], ps, ACT.Square).then_inc(job_sq, 1)
                    if n >= 4:
                        act.wait_ge(job_lo, n - 3)
                    ins = A(S[:, n % 4, 0:w], ps, ACT.Copy)
                    if i + 1 < len(jobs_of(t)):
                        own(ins)
                    else:
                        ins.then_inc(evac_done, 1)

            for n in range(NQ + 5):
                if n >= 6 and n % 2 == 0:
                    m = (n - 6) // 2
                    act.wait_ge(pv_done, m + 1)
                    A(hhi[:, m // 2, (m % 2) * 2 * P:(m % 2 + 1) * 2 * P], (B2, B3)[m % 2][:, 0:2 * P],
                      ACT.Copy).then_inc(ohi_done, 1)
                m = n - 3
                if 0 <= m < NQ:
                    act.wait_ge(pt_done, m + 1)
                    if m >= 4:
                        act.wait_ge(pv_done, m // 2 - 1)
                    A(phi[:, m // 2 % 2, :, (m % 2) * P:(m % 2 + 1) * P].rearrange("p (a b) c -> p a b c", a=2),
                      AB[:, :, 0:3 * P].rearrange("p a (b c) -> p a b c", b=3), ACT.Copy).then_inc(phi_done, 1)
                m = n - 1
                if 0 <= m < NQ:
                    act.wait_ge(nmax_done, m + 1)
                    if m >= 2:
                        act.wait_ge(pt_done, m - 1)
                    A(PROB[m % 2], SCORE[m % 2], ACT.Exp, bias=nmax[:, m % 2:m % 2 + 1],
                      accum_out=rsum[:, m % 2:m % 2 + 1]).then_inc(exp_done, 1)
                if n == 1:
                    act.wait_ge(csum_done, 1)
                    A(crow, AB[:, :, :].rearrange("p a b -> p (a b)"), ACT.Copy).then_inc(crow_done, 1)
                a = n - 4
                if 0 <= a < 32:
                    act.wait_ge(amul_done, a + 1)
                    slot = arow_slot(16, a % ADA_RING)
                    A(slot, slot, ACT.Copy, accum_out=mods[:, 0, 16 + a:17 + a]).then_inc(asum_done, 1)

            act.wait_ge(olo_done, NQ // 2)
            A(crow1[:, :], crow, ACT.Copy).then_inc(crow_done, 1)
            act.wait_ge(crow_done, 2)
            act.wait_ge(asum_done, 32)
            for third in range(3):
                if third:
                    act.wait_ge(tlo_done, third + 1)
                act.dma_start(S[:, 8:10, :], tables[:, 2 * third:2 * third + 2, :]).then_inc(table2_in, 16)
                act.wait_ge(table2_in, 16 * (third + 1))
                A(t2hi[:, 2 * third:2 * third + 2, :], S[:, 8:10, :], ACT.Copy).then_inc(thi_done, 1)

            def out_units(u0):
                with act.Fori(0, OUT_UNITS // 4) as i:
                    for s in range(4):
                        u = u0 + 4 * i + s
                        prep(u + AHEAD, (s + AHEAD) % 4, (s + AHEAD) % 2)
                        act.wait_ge(unit_done, u + 1)
                        A(S[:, 4 * i + s, :], AB[:, s % 2, :], ACT.Copy).then_inc(evac_done, 1)

            def boundary(b):
                nb = 2 * b + NORMS_BEFORE
                act.wait_ge(yss_done, b + 1)
                A(S[:, 8, :], B2[:, :], ACT.Sqrt, scale=1.0 / D, bias=epst[:, 0:1]).then_inc(sd_done, 1)
                if b == 3:
                    return
                square_sum(b + 2, x, NT, lambda j: act.wait_ge(x_done, b * KC + j + 1))
                root(b + 2, S[:, 9, :], NT)
                operand_hi(b + 2, hhi, BOUND[b][4], BOUND[b][5], 0, y)

            def quarter(l, q, last=False):
                u0 = (U_MLP0, U_MLP1)[l] + 16 * q
                c0 = l * 32 + 8 * q
                for j in range(8):
                    prep(u0 + j + AHEAD, (j + AHEAD) % 4, (j + AHEAD) % 2)
                    act.wait_ge(unit_done, u0 + j + 1)
                    if j < 2:
                        if not isinstance(c0, int) or c0:
                            act.wait_ge(y_done, c0)
                            act.wait_ge(g_done, c0)
                    else:
                        act.wait_ge(g_done, c0 + j - 1)
                    A(S[:, 8 + j % 2, :], AB[:, j % 2, :], ACT.Relu).then_inc(evac_done, 1)
                    act.wait_ge(evac_done, u0 + j + 1)
                    A(S[:, 10 + j % 2, :], S[:, 8 + j % 2, :], ACT.Square).then_inc(g_full, 1)
                    act.wait_ge(g_full, c0 + j + 1)
                    A(ghi[:, j, :], S[:, 10 + j % 2, :], ACT.Copy).then_inc(ghi_done, 1)
                for j in range(8):
                    u = u0 + 8 + j
                    if not last or u + AHEAD < UNITS:
                        prep(u + AHEAD, (j + AHEAD) % 4, (j + AHEAD) % 2)
                    act.wait_ge(unit_done, u + 1)
                    if j >= 2:
                        act.wait_ge(y_done, c0 + j - 1)
                    A(S[:, 8 + j % 2, :], AB[:, j % 2, :], ACT.Copy).then_inc(evac_done, 1)

            out_units(U_OUT0)
            boundary(0)
            quarter(0, 0)
            with act.Fori(1, QUARTERS) as q:
                quarter(0, q)
            boundary(1)

            def hy_unit(n):
                u = U_HY + n
                act.wait_ge(unit_done, u + 1)
                if n:
                    act.wait_ge(tap_done, n)
                centre = y[:, n, :] if n < KC else es[:, 1, :]
                own(A(centre, AB[:, n % 2, :], ACT.Identity, scale=col[:, C_CW + 24 + n:C_CW + 25 + n],
                      bias=col[:, C_CB + n:C_CB + n + 1]))
                A(es[:, 0, :], AB[:, n % 2, :], ACT.Copy).then_inc(evac_done, 1)

            def hy_prep(n):
                u = U_HY + n + AHEAD
                prep(u, u % 4, u % 2)

            for n in range(4):
                hy_prep(n)
                hy_unit(n)
            def z_hi(k):
                for tt in range(4):
                    act.wait_ge(zt_done, 4 * k + tt + 1)
                    A(zhi[:, tt, :], SCD[tt // 2][:, tt % 2, :], ACT.Copy).then_inc(zhi_done, 1)

            def skip(k):
                o, c = STAGES[k]
                for j in range(4 * c, 4 * c + 4):
                    A(y[:, j, :], y[:, j, :], ACT.Copy,
                      scale=col[:, C_SK + 8 * o + j:C_SK + 8 * o + j + 1]).then_inc(skip_done, 1)

            def odd_halves(m):
                act.wait_ge(dft_done, m + 1)
                if m:
                    act.wait_ge(spec_lo, 4 * m)
                A(S[:, 9, :], SC[:, 1, :], ACT.Copy).then_inc(odd_done, 1)
                A(S[:, 10, :], SD[:, 1, :], ACT.Copy).then_inc(odd_done, 1)

            def spectrum_hi(m):
                if m % 2 == 0 and m:
                    act.wait_ge(inv_done, 2 * m)
                for e in range(4):
                    act.wait_ge(spec_full, 4 * m + e + 1)
                    A(ghi[:, 2 * e + m % 2, :], SPEC[e], ACT.Copy).then_inc(spec_hi, 1)

            for k in range(4):
                z_hi(k)
                skip(k)
                odd_halves(2 * k)
                n = 4 * (k + 1)
                hy_prep(n)
                spectrum_hi(2 * k)
                hy_unit(n)
                hy_prep(n + 1)
                odd_halves(2 * k + 1)
                hy_unit(n + 1)
                hy_prep(n + 2)
                spectrum_hi(2 * k + 1)
                hy_unit(n + 2)
                hy_prep(n + 3)
                hy_unit(n + 3)
            for n in range(20, 24):
                hy_prep(n)
                hy_unit(n)
            for j in range(KC):
                act.wait_ge(tap_done, 24 if j >= 4 else 20)
                act.wait_ge(unit_done, U_HY + 24)
                A(ghi[:, j, :], y[:, j, :], ACT.Copy).then_inc(z3_hi, 1)
            act.wait_ge(z3_lo, KC)
            out_units(U_OUT1)
            boundary(2)
            with act.Fori(0, QUARTERS - 1) as q:
                quarter(1, q)
            quarter(1, QUARTERS - 1, last=True)
            boundary(3)

        @block.vector
        def _(dve):
            own = Own(dve, own_dve)
            TT = nc.vector.tensor_tensor
            STT = nc.vector.scalar_tensor_tensor
            TS = nc.vector.tensor_scalar

            def prep(u, s, r):
                dve.wait_ge(hi_done, u + 1)
                TT(wlo[:, s, :], raw[:, r, :], f(whi[:, s, :]), ALU.subtract).then_inc(lo_done, 1)

            def inverse_root(nb, dst, w):
                dve.wait_ge(sd_done, nb + 1)
                nc.vector.reciprocal(dst[:, 0:w], dst[:, 0:w]).then_inc(rs_done, 1)
                dve.wait_ge(rs_done, nb + 1)

            def operand(k, src, buf, rs, gains, hi, lo, l, t, v):
                w = hi.shape[2]

                def lo_part(j):
                    dve.wait_ge(hhi_done, k * KC + j + 1)
                    STT(lo[:, j, :], buf[:, j, :], shift(l, t, j, v), f(hi[:, j, :]), ALU.add,
                        ALU.subtract).then_inc(h_done, 1)

                for j in range(KC):
                    STT(buf[:, j, :], src[:, j, :], gains[:, j:j + 1], rs[:, 0:w], ALU.mult,
                        ALU.mult).then_inc(ht_done, 1)
                    if j:
                        lo_part(j - 1)
                lo_part(KC - 1)

            def modulation(b):
                a, a1 = ADA_START[b], ADA_START[b + 1]
                l = a // 48
                bias = col[:, C_AB + a:C_AB + a1]
                if b == 0:
                    dve.wait_ge(ada_done, 16)
                    for v in range(2):
                        ps = B3[:, 0:32].rearrange("p (t v) -> p t v", v=2)
                        own(TT(mods[:, v, 0:16], ps[:, :, v], bias, ALU.add))
                elif b == 1:
                    dve.wait_ge(asum_done, 32)
                    own(TT(mods[:, 0, a:a1], mods[:, 0, a:a1], bias, ALU.add))

                def scaled(dst, m, g, v=0):
                    return STT(dst, mods[:, v, 48 * l + 8 * m:48 * l + 8 * m + 8], 1.0, col[:, C_G + 8 * g:C_G + 8 * g + 8], ALU.add, ALU.mult)

                def gated(dst, m, g):
                    return TT(dst, mods[:, 0, 48 * l + 8 * m:48 * l + 8 * m + 8], col[:, C_G + 8 * g:C_G + 8 * g + 8], ALU.mult)

                if b == 0:
                    own(scaled(gainc[:, :], 1, 0, 1))
                if b != 1:
                    last = scaled(gain[:, l, 0, :], 1, 4 * l)
                if b:
                    if b == 2:
                        own(last)
                    own(gated(gain[:, l, 1, :], 2, 4 * l + 1))
                    own(scaled(gain[:, l, 2, :], 4, 4 * l + 2))
                    last = gated(gain[:, l, 3, :], 5, 4 * l + 3)
                last.then_inc(mod_done, 1)
                dve.wait_ge(mod_done, b + 1)

            dve.wait_ge(silu_e, 1)
            own(nc.vector.tensor_scalar_add(ce[:, :, :], ce[:, :, :], 1.0))
            own(nc.vector.reciprocal(ce[:, :, :], ce[:, :, :]))
            TT(ce[:, :, :], ce[:, :, :], cs[:, :, :], ALU.mult).then_inc(silu_done, 1)
            nc.vector.tensor_scalar_mul(qg[:, :], col[:, C_QG:C_QG + 1], HD ** -0.5)

            dve.wait_ge(thi_done, 1)
            TT(tlo[:, :, :], S[:, 0:6, :], f(thi[:, :, :]), ALU.subtract).then_inc(tlo_done, 1)

            arg, turns = S[0:FH, 9, :], S[0:FH, 11, :]
            for k in range(2):
                dve.wait_ge(fmlp_done, k + 1)
                if k:
                    dve.wait_ge(sin_done, 1)
                own(TS(arg, B2[0:FH, :], col[0:FH, FCOL[k]:FCOL[k] + 1], col[0:FH, FCOL[2 + k]:FCOL[2 + k] + 1],
                       ALU.add, ALU.mult))
                own(TS(turns, arg, 1.0 / (2 * math.pi), MAGIC, ALU.mult, ALU.add))
                own(nc.vector.tensor_scalar_add(turns, turns, -MAGIC))
                for part in (TWO_PI_A, TWO_PI_B, TWO_PI_C):
                    own(STT(arg, turns, -part, arg, ALU.mult, ALU.add))
                TS(arg, arg, 3.1415925, -3.1415925, ALU.min, ALU.max).then_inc(sin_arg, 1)
            prep(0, 0, 0)
            prep(1, 1, 1)

            def eo_los(n):
                q, tt = divmod(n, 4)
                hi, lo = FPAIR[q % 2]
                dve.wait_ge(eo_hi, 2 * n + 2)
                TT(lo[:, tt, :], FE[n % 2], f(hi[:, tt, :]), ALU.subtract).then_inc(eo_lo, 1)
                TT(lo[:, 4 + tt, :], HF[n % 2], f(hi[:, 4 + tt, :]), ALU.subtract).then_inc(eo_lo, 1)

            for q in range(5):
                for n in range(4 * q, min(4 * q + 4, 16)):
                    tt = n % 4
                    dve.wait_ge(gen_done, n + 1)
                    dve.wait_ge(decay_in[n % 2], 16 * (n // 2 + 1))
                    if n >= 2:
                        dve.wait_ge(eo_lo, 2 * n - 2)
                    own(TT(HF[n % 2], AB[:, 0, :], DEC[n % 2], ALU.mult))
                    ins = TT(HB, AB[:, 1, :], DEC[n % 2], ALU.mult)
                    ins.then_inc(gen_used, 1)
                    dve.wait_ge(gen_used, n + 1)
                    if tt == 0:
                        own(nc.vector.memset(HB[0:1, :], 0.0))
                    TT(FE[n % 2], HF[n % 2], HB, ALU.add).then_inc(eo_full, 1)
                    dve.wait_ge(eo_full, 2 * n + 1)
                    TT(HF[n % 2], HF[n % 2], HB, ALU.subtract).then_inc(eo_full, 1)
                    dve.wait_ge(eo_full, 2 * n + 2)
                    if tt:
                        eo_los(n - 1)
                    if tt == 3:
                        eo_los(n)
                if q >= 1:
                    for ft in range(2):
                        m = 2 * (q - 1) + ft
                        dve.wait_ge(fodd_done, 2 * m + 2)
                        if m:
                            dve.wait_ge(filt_out, 16 * m)
                        TT(S[:, 0, :], SC[:, 0, :], S[:, 10, :], ALU.add).then_inc(fout_done, 1)
                        TT(S[:, 1, :], SC[:, 0, :], S[:, 10, :], ALU.subtract).then_inc(fout_done, 1)
                        TT(S[:, 2, :], SD[:, 0, :], S[:, 11, :], ALU.add).then_inc(fout_done, 1)
                        TT(S[:, 3, :], S[:, 11, :], SD[:, 0, :], ALU.subtract).then_inc(fout_done, 1)

            modulation(0)
            inverse_root(0, S[:, 9, :], NC)
            operand(0, ctxs, ctxs, S[:, 9, :], gainc, chi, clo, 0, 0, 1)
            inverse_root(1, S[:, 9, :], NT)
            dve.wait_ge(filt_out, 8 * 16)
            operand(1, x, y, S[:, 9, :], gain[:, 0, 0, :], hhi, hlo, 0, 0, 0)

            prep(2, 2, 0)
            for t in range(QKV_UNITS + 2):
                if t < QKV_UNITS:
                    prep(t + AHEAD, (t + AHEAD) % 4, (t + AHEAD) % 2)
                if t < NKV:
                    dve.wait_ge(evac_done, t + 1)
                    for half in range(2):
                        ps = SCD[t][:, half, 0:3 * P].rearrange("p (a b) -> p a b", a=3)
                        TT(vlo[:, 3 * half:3 * half + 3, t, :], ps, f(vhi[:, 3 * half:3 * half + 3, t, :]),
                           ALU.subtract).then_inc(vlo_done, 1)
                for n, (_, ps, w, r, key, hi, lo) in jobs_of(t - 2):
                    if r is not None:
                        dve.wait_ge(rope_in, 16)
                        dve.wait_ge(job_rot, r + 1)
                        dve.wait_ge(job_qn, n + 1)
                        TT(S[:, n % 4, :], B3[:, :], araw[:, 1, 0:NT], ALU.mult).then_inc(job_sin, 1)
                        dve.wait_ge(job_sin, r + 1)
                        dve.wait_ge(job_cos, r + 1)
                        full = S[:, 10 + r % 2, :]
                        TT(full, full, S[:, n % 4, :], ALU.add).then_inc(job_full, 1)
                    else:
                        full = S[:, 8 + n % 2, 0:w]
                        dve.wait_ge(job_qn, n + 1)
                        dve.sem_inc(job_full, 1)
                    dve.wait_ge(job_hi, n + 1)
                    TT(lo, full, f(hi), ALU.subtract).then_inc(job_lo, 1)
                for n, (_, ps, w, r, key, hi, lo) in jobs_of(t - 1):
                    dve.wait_ge(job_sd, n + 1)
                    own(nc.vector.reciprocal(S[:, 6 + n % 2, 0:w], S[:, 6 + n % 2, 0:w]))
                    dve.wait_ge(evac_done, t)
                    if n >= 2:
                        dve.wait_ge(job_lo, n - 1)
                    g = col[:, C_KG:C_KG + 1] if key else qg[:, 0:1]
                    STT(S[:, 8 + n % 2, 0:w], S[:, n % 4, 0:w], g, S[:, 6 + n % 2, 0:w], ALU.mult,
                        ALU.mult).then_inc(job_qn, 1)

            for k in range(KC):
                TS(S[:, 4 + k // 4, k % 4 * P:(k % 4 + 1) * P], ident, ce[:, k, 0:1], None,
                   ALU.mult).then_inc(cdiag_done, 1)

            def o_lo(m):
                dve.wait_ge(ohi_done, m + 1)
                cols_ = slice((m % 2) * 2 * P, (m % 2 + 1) * 2 * P)
                TT(hlo[:, m // 2, cols_], (B2, B3)[m % 2][:, 0:2 * P], f(hhi[:, m // 2, cols_]), ALU.subtract).then_inc(olo_done, 1)

            for n in range(NQ + 5):
                m = n - 2
                if 0 <= m < NQ:
                    dve.wait_ge(exp_done, m + 1)
                    if m >= 2:
                        dve.wait_ge(p_done, m - 1)
                    own(nc.vector.reciprocal(rinv[:, m % 2:m % 2 + 1], rsum[:, m % 2:m % 2 + 1]))
                    TS(PROB[m % 2], PROB[m % 2], rinv[:, m % 2:m % 2 + 1], None, ALU.mult).then_inc(p_done, 1)
                m = n - 3
                if 0 <= m < NQ:
                    dve.wait_ge(phi_done, m + 1)
                    for half in range(2):
                        at = slice(3 * half, 3 * half + 3)
                        TT(plo[:, m // 2 % 2, at, (m % 2) * P:(m % 2 + 1) * P],
                           AB[:, half, 0:3 * P].rearrange("p (b c) -> p b c", b=3),
                           f(phi[:, m // 2 % 2, at, (m % 2) * P:(m % 2 + 1) * P]), ALU.subtract).then_inc(plo_done, 1)
                if n < NQ:
                    dve.wait_ge(score_done, n + 1)
                    if n >= 2:
                        dve.wait_ge(exp_done, n - 1)
                    nc.vector.tensor_reduce(out=nmax[:, n % 2:n % 2 + 1], in_=SCORE[n % 2], op=ALU.max,
                                            axis=AX.X, negate=True).then_inc(nmax_done, 1)
                if n >= 6 and n % 2 == 0:
                    o_lo((n - 6) // 2)
            modulation(1)
            for third in range(3):
                at = slice(2 * third, 2 * third + 2)
                dve.wait_ge(thi_done, 2 + third)
                TT(t2lo[:, at, :], S[:, 8:10, :], f(t2hi[:, at, :]), ALU.subtract).then_inc(tlo_done, 1)

            def preps(u0, groups):
                with dve.Fori(0, groups) as i:
                    for s in range(4):
                        prep(u0 + 4 * i + s + AHEAD, (s + AHEAD) % 4, (s + AHEAD) % 2)

            def boundary(b):
                nb = 2 * b + NORMS_BEFORE
                lg, ng, lo_, no_, ls, ts = BOUND[b]
                inverse_root(nb, S[:, 8, :], NT)
                for j in range(KC):
                    own(STT(y[:, j, :], y[:, j, :], gcol(lg, ng, j), S[:, 8, :], ALU.mult, ALU.mult))
                    TT(x[:, j, :], x[:, j, :], y[:, j, :], ALU.add).then_inc(x_done, 1)
                if b == 3:
                    return
                inverse_root(nb + 1, S[:, 9, :], NT)
                dve.wait_ge(x_done, KC * (b + 1))
                operand(b + 2, x, y, S[:, 9, :], gain[:, lo_, no_, :], hhi, hlo, ls, ts, 0)

            def quarter(l, q, last=False):
                u0 = (U_MLP0, U_MLP1)[l] + 16 * q
                c0 = l * 32 + 8 * q

                def modulate(s):
                    if l == 0 and s < ADA_QUARTER:
                        dve.wait_ge(arow_in[s % ADA_RING], 16 * (8 + 3 * q + s // ADA_RING + 1))
                        slot = arow_slot(48, s % ADA_RING)
                        nc.vector.tensor_tensor_reduce(slot, slot, crow1[:, :], 1.0, 0.0, ALU.mult, ALU.add,
                                                       asum[:, s:s + 1]).then_inc(asum1_done, 1)

                for j in range(8):
                    prep(u0 + j + AHEAD, (j + AHEAD) % 4, (j + AHEAD) % 2)
                    dve.wait_ge(ghi_done, c0 + j + 1)
                    TT(glo[:, j, :], S[:, 10 + j % 2, :], f(ghi[:, j, :]), ALU.subtract).then_inc(g_done, 1)
                    modulate(j)
                for j in range(8):
                    u = u0 + 8 + j
                    if not last or u + AHEAD < UNITS:
                        prep(u + AHEAD, (j + AHEAD) % 4, (j + AHEAD) % 2)
                    dve.wait_ge(evac_done, u + 1)
                    if j == 0:
                        dve.wait_ge(y_zero, l + 1)
                        if not isinstance(c0, int) or c0:
                            dve.wait_ge(y_done, c0)
                    TT(y[:, j, :], y[:, j, :], S[:, 8 + j % 2, :], ALU.add).then_inc(y_done, 1)
                    modulate(8 + j)
                if l == 0:
                    dve.wait_ge(asum1_done, ADA_QUARTER * (q + 1))
                    at = 48 + ADA_QUARTER * q
                    TT(mods[:, 0, bass.ds(at, ADA_QUARTER)], asum[:, :],
                       col[:, bass.ds(C_AB + at, ADA_QUARTER)], ALU.add).then_inc(bias_done, 1)
                    dve.wait_ge(bias_done, q + 1)

            preps(U_OUT0, OUT_UNITS // 4)
            boundary(0)
            dve.wait_ge(crow_done, 2)
            quarter(0, 0)
            with dve.Fori(1, QUARTERS) as q:
                quarter(0, q)
            modulation(2)
            boundary(1)

            def hy_prep(n):
                u = U_HY + n + AHEAD
                prep(u, u % 4, u % 2)

            def hy_unit(n):
                dve.wait_ge(evac_done, U_HY + n + 1)
                dst = y[:, n, :] if n < KC else es[:, 1, :]
                own(STT(dst[:, 1:NT], es[:, 0, 0:NT - 1], col[:, C_CW + n:C_CW + n + 1], dst[:, 1:NT],
                        ALU.mult, ALU.add))
                ins = STT(dst[:, 0:NT - 1], es[:, 0, 1:NT], col[:, C_CW + 48 + n:C_CW + 49 + n], dst[:, 0:NT - 1],
                          ALU.mult, ALU.add)
                if n >= KC:
                    own(ins)
                    ins = TT(y[:, n % KC, :], y[:, n % KC, :], dst, ALU.mult)
                ins.then_inc(tap_done, 1)

            def spectrum_a(m):
                dve.wait_ge(odd_done, 2 * m + 2)
                if m:
                    dve.wait_ge(spec_lo, 4 * m)
                c, c_, s, s_, e2, e3 = S[:, 8, :], S[:, 9, :], S[:, 10, :], S[:, 11, :], es[:, 2, :], es[:, 3, :]
                own(TT(c, SC[:, 0, :], c_, ALU.add))
                own(TT(c_, SC[:, 0, :], c_, ALU.subtract))
                own(TT(s_, s, SD[:, 0, :], ALU.subtract))
                TT(s, SD[:, 0, :], s, ALU.add).then_inc(spec_free, 1)
                dve.wait_ge(filt_in, 16 * (m + 1))
                dve.wait_ge(spec_free, m + 1)
                own(TT(e2, c, FP, ALU.mult))
                own(TT(e3, s, FQ, ALU.mult))
                own(TT(e2, e2, e3, ALU.subtract))
                own(TT(c, c, FQ, ALU.mult))
                own(TT(s, s, FP, ALU.mult))
                own(TT(c, c, s, ALU.add))

            def spectrum_b(m):
                c, c_, s, s_, e2, e3 = S[:, 8, :], S[:, 9, :], S[:, 10, :], S[:, 11, :], es[:, 2, :], es[:, 3, :]
                own(TT(e3, c_, FP_, ALU.mult))
                own(TT(s, s_, FQ_, ALU.mult))
                own(TT(e3, e3, s, ALU.subtract))
                own(TT(c_, c_, FQ_, ALU.mult))
                TT(s_, s_, FP_, ALU.mult).then_inc(filt_used, 1)
                dve.wait_ge(filt_used, m + 1)
                own(TT(c_, c_, s_, ALU.add))
                TT(SPEC[0], e2, e3, ALU.add).then_inc(spec_full, 1)
                dve.wait_ge(spec_full, 4 * m + 1)
                TT(SPEC[1], e2, e3, ALU.subtract).then_inc(spec_full, 1)
                TT(SPEC[2], c, c_, ALU.add).then_inc(spec_full, 1)
                dve.wait_ge(spec_full, 4 * m + 3)
                TT(SPEC[3], c, c_, ALU.subtract).then_inc(spec_full, 1)
                for e in range(4):
                    dve.wait_ge(spec_hi, 4 * m + e + 1)
                    TT(glo[:, 2 * e + m % 2, :], SPEC[e], f(ghi[:, 2 * e + m % 2, :]),
                       ALU.subtract).then_inc(spec_lo, 1)

            for n in range(4):
                hy_prep(n)
                hy_unit(n)
            def z_los(k):
                for tt in range(4):
                    dve.wait_ge(zhi_done, 4 * k + tt + 1)
                    TT(zlo[:, tt, :], SCD[tt // 2][:, tt % 2, :], f(zhi[:, tt, :]), ALU.subtract).then_inc(zlo_done, 1)

            def conv(k, i):
                j = 4 * STAGES[k][1] + i
                dve.wait_ge(inv_done, 4 * k + i + 1)
                dve.wait_ge(skip_done, 4 * k + i + 1)
                v = y[:, j, :].rearrange("p (m two) -> p two m", two=2)
                STT(v, (B2, B3)[i % 2][:, :].rearrange("p (two m) -> p two m", two=2), 1.0 / 512, v,
                    ALU.mult, ALU.add).then_inc(conv_done, 1)

            for k in range(5):
                if k < 4:
                    z_los(k)
                if k:
                    conv(k - 1, 0)
                    conv(k - 1, 1)
                if k < 4:
                    spectrum_a(2 * k)
                if k:
                    conv(k - 1, 2)
                    conv(k - 1, 3)
                    dve.wait_ge(conv_done, 4 * k)
                n = 4 * (k + 1)
                for s in range(4):
                    hy_prep(n + s)
                    if k < 4 and s < 3:
                        (spectrum_b, spectrum_a, spectrum_b)[s](2 * k + (s + 1) // 2)
                    hy_unit(n + s)
            for j in range(KC):
                dve.wait_ge(z3_hi, j + 1)
                TT(glo[:, j, :], y[:, j, :], f(ghi[:, j, :]), ALU.subtract).then_inc(z3_lo, 1)
            preps(U_OUT1, OUT_UNITS // 4)
            boundary(2)
            with dve.Fori(0, QUARTERS - 1) as q:
                quarter(1, q)
            quarter(1, QUARTERS - 1, last=True)
            boundary(3)

        @block.tensor
        def _(pe):
            mm = nc.tensor.matmul

            def mm3(o, lh, ll, rh, rl, first, last):
                mm(o, lh, rh, start=first, stop=False)
                mm(o, lh, rl, start=False, stop=False)
                return mm(o, ll, rh, start=False, stop=last)

            def unit_ready(u):
                pe.wait_ge(hi_done, u + 1)
                pe.wait_ge(lo_done, u + 1)
                if not isinstance(u, int) or u >= 2:
                    pe.wait_ge(evac_done, u - 1)

            def unit(u, s, o, hi, lo, chunk_ready=None):
                unit_ready(u)
                for k in range(KC):
                    if chunk_ready:
                        chunk_ready(k)
                    w = slice(k * P, (k + 1) * P)
                    ins = mm3(o, whi[:, s, w], wlo[:, s, w], hi[:, k, :], lo[:, k, :], k == 0, k == KC - 1)
                return ins

            def ada(a):
                pe.wait_ge(ada_in[a % 2], 16 * (a // 2 + 1))
                for k in range(KC):
                    ins = mm(B3[:, 2 * a:2 * a + 2], araw[:, a % 2, k * P:(k + 1) * P], ce[:, k, :],
                             start=k == 0, stop=k == KC - 1)
                ins.then_inc(ada_done, 1)

            def add_squares(b, nb, j, w):
                pe.wait_ge(sq_done, b * KC + j + 1)
                if j == 0 and nb:
                    pe.wait_ge(sd_done, nb)
                mm(B2[:, 0:w], ones, S[:, 10 + j % 2, 0:w], start=j == 0, stop=j == KC - 1).then_inc(ss_done, 1)

            pe.wait_ge(small_in, 96)
            mm(B2[0:FH, :], S[0:NFEAT, 10, 0:FH], S[0:NFEAT, 6, :], start=True, stop=True).then_inc(fmlp_done, 1)
            pe.wait_ge(sin_done, 1)
            mm(B2[0:FH, :], S[0:FH, 10, FH:2 * FH], S[0:FH, 7, :], start=True, stop=True).then_inc(fmlp_done, 1)
            pe.wait_ge(sin_done, 2)
            pe.wait_ge(w3_in, 16)
            pe.wait_ge(silu_done, 1)
            for q in range(5):
                for n in range(4 * q, min(4 * q + 4, 16)):
                    tt = n % 4
                    if n:
                        pe.wait_ge(gen_used, n)
                    for d in range(2):
                        ins = mm(AB[:, d, :], S[0:FH, 8, tt * P:(tt + 1) * P],
                                 fs[0:FH, (2 * (q % 2) + d) * 2 + q // 2, :], start=True, stop=True)
                    ins.then_inc(gen_done, 1)
                    ada(n)
                if q >= 1:
                    hi, lo = FPAIR[(q - 1) % 2]
                    pe.wait_ge(eo_lo, 8 * q)
                    pe.wait_ge(tlo_done, 1)
                    for ft in range(2):
                        m = 2 * (q - 1) + ft
                        if m:
                            pe.wait_ge(fout_done, 4 * m)
                        for kind, bank in ((CE, SC[:, 0, :]), (CO, SC[:, 1, :]), (SE, SD[:, 0, :]), (SO, SD[:, 1, :])):
                            at = (4 if kind in (SE, SO) else 0) + (2 if kind in (CO, SO) else 0)
                            for kt in range(2):
                                w = slice(kt * 256 + ft * P, kt * 256 + (ft + 1) * P)
                                ins = mm3(bank, thi[:, kind, w], tlo[:, kind, w], hi[:, at + kt, :],
                                          lo[:, at + kt, :], kt == 0, kt == 1)
                        ins.then_inc(fdft_done, 1)

            for j in range(KC):
                add_squares(0, 0, j, NC)
            for j in range(KC):
                add_squares(1, 1, j, NT)

            for t in range(QKV_UNITS + 2):
                if t < NKV:
                    unit_ready(t)
                    for kt in range(KT):
                        th, tl = (hhi, hlo) if kt < NT // P else (chi, clo)
                        at = (kt if kt < NT // P else kt - NT // P) * P
                        for k in range(KC):
                            if kt == 0:
                                pe.wait_ge(h_done, KC + k + 1)
                            w = slice(k * P, (k + 1) * P)
                            ins = mm3(SCD[t][:, kt // 3, kt % 3 * P:(kt % 3 + 1) * P], th[:, k, at:at + P],
                                      tl[:, k, at:at + P], whi[:, t % 4, w], wlo[:, t % 4, w], k == 0, k == KC - 1)
                    ins.then_inc(unit_done, 1)
                elif t < 2 * NKV:
                    g = t - NKV
                    pe.wait_ge(vlo_done, 2 * g + 2)
                    unit(t, t % 4, SCD[g][:, 0, :], hhi, hlo)
                    unit(t, t % 4, SCD[g][:, 1, 0:NC], chi, clo).then_inc(unit_done, 1)
                elif t < QKV_UNITS:
                    unit(t, t % 4, AB[:, t % 2, :], hhi, hlo).then_inc(unit_done, 1)
                for n, (_, ps, w, r, key, hi, lo) in jobs_of(t - 2):
                    if r is not None:
                        pe.wait_ge(job_qn, n + 1)
                        if r:
                            pe.wait_ge(job_sin, r)
                        mm(B3[:, :], rotm, S[:, 8 + n % 2, :], start=True, stop=True).then_inc(job_rot, 1)
                for n, (_, ps, w, r, key, hi, lo) in jobs_of(t - 1):
                    pe.wait_ge(job_sq, n + 1)
                    if n:
                        pe.wait_ge(job_sd, n)
                    mm(B2[:, 0:w], ones, S[:, 4 + n % 2, 0:w], start=True, stop=True).then_inc(job_ss, 1)

            def prob_values(m):
                pe.wait_ge(plo_done, 4 * m + 4)
                if m >= 2:
                    pe.wait_ge(olo_done, m - 1)
                g = m // 2 // GROUP
                for kt in range(KT):
                    ins = mm3((B2, B3)[m % 2][:, 0:2 * P], vhi[:, kt, g, :], vlo[:, kt, g, :],
                              phi[:, m % 2, kt, :], plo[:, m % 2, kt, :], kt == 0, kt == KT - 1)
                ins.then_inc(pv_done, 1)

            for n in range(NQ + 4):
                m = n - 3
                if 0 <= m < NQ:
                    pe.wait_ge(p_done, m + 1)
                    if m == 0:
                        pe.wait_ge(crow_done, 1)
                    else:
                        pe.wait_ge(plo_done, 2 * m)
                    for kt in range(KT):
                        ins = nc.tensor.transpose(AB[:, kt // 3, kt % 3 * P:(kt % 3 + 1) * P],
                                                  PROB[m % 2][:, kt * P:(kt + 1) * P], ident)
                    ins.then_inc(pt_done, 1)
                if n < NQ:
                    h, qt = divmod(n, QT)
                    g = h // GROUP
                    pe.wait_ge(job_lo, len(JOBS) - NH + h + 1)
                    if n >= 2:
                        pe.wait_ge(exp_done, n - 1)
                    w = slice(qt * P, (qt + 1) * P)
                    mm3(SCD[n % 2][:, 0, :], ghi[:, h, w], glo[:, h, w], khi[:, g, 0:NT], klo[:, g, 0:NT], True, True)
                    mm3(SCD[n % 2][:, 1, 0:NC], ghi[:, h, w], glo[:, h, w], khi[:, g, NT:NK], klo[:, g, NT:NK],
                        True, True).then_inc(score_done, 1)
                if n == 1:
                    pe.wait_ge(cdiag_done, KC)
                    mm(AB[:, 0, :], ones, S[:, 4, :], start=True, stop=True)
                    mm(AB[:, 1, :], ones, S[:, 5, :], start=True, stop=True).then_inc(csum_done, 1)
                if n >= 5 and n % 2 == 1:
                    prob_values((n - 5) // 2)

            def boundary(b):
                nb = 2 * b + NORMS_BEFORE
                pe.wait_ge(ysq_done, KC * (b + 1))
                pe.wait_ge(sd_done, nb)
                mm(B2[:, :], ones, S[:, 11, :], start=True, stop=True).then_inc(yss_done, 1)
                if b == 3:
                    return
                for j in range(KC):
                    add_squares(b + 2, nb + 1, j, NT)

            def out_units(u0, hi, lo, ready):
                with pe.Fori(0, OUT_UNITS // 4) as i:
                    for s in range(4):
                        unit(u0 + 4 * i + s, s, AB[:, s % 2, :], hi, lo,
                             ready if s == 0 else None).then_inc(unit_done, 1)

            def quarter(l, q):
                u0 = (U_MLP0, U_MLP1)[l] + 16 * q
                c0 = l * 32 + 8 * q
                for j in range(8):
                    unit(u0 + j, j % 4, AB[:, j % 2, :], hhi, hlo,
                         (lambda k: pe.wait_ge(h_done, (2 + 2 * l) * KC + k + 1)) if j == 0 else None
                         ).then_inc(unit_done, 1)
                for j in range(8):
                    unit(u0 + 8 + j, j % 4, AB[:, j % 2, :], ghi, glo,
                         (lambda k: pe.wait_ge(g_done, c0 + k + 1)) if j == 0 else None).then_inc(unit_done, 1)

            pe.wait_ge(plo_done, 2 * NQ)
            out_units(U_OUT0, hhi, hlo, lambda k: pe.wait_ge(olo_done, NQ // 2))
            boundary(0)
            with pe.Fori(0, QUARTERS) as q:
                quarter(0, q)
            boundary(1)

            def hy_unit(n):
                u = U_HY + n
                unit(u, u % 4, AB[:, n % 2, :], hhi, hlo,
                     (lambda k: pe.wait_ge(h_done, 3 * KC + k + 1)) if n == 0 else None).then_inc(unit_done, 1)

            for n in range(4):
                hy_unit(n)
            def transposes(k):
                pe.wait_ge(tap_done, 4 * (k + 1))
                if k:
                    pe.wait_ge(spec_free, 2 * k)
                for tt in range(4):
                    for i in range(4):
                        at = tt // 2 + 256 * (tt % 2)
                        ins = nc.tensor.transpose(SCD[tt // 2][:, tt % 2, i * P:(i + 1) * P],
                                                  y[:, 4 * STAGES[k][1] + i, at:at + 255:2], ident)
                    ins.then_inc(zt_done, 1)

            def forward(k, ft):
                if ft == 0:
                    pe.wait_ge(zlo_done, 4 * k + 4)
                    pe.wait_ge(tlo_done, 4)
                else:
                    pe.wait_ge(spec_free, 2 * k + 1)
                for kind, bank in ((CE, SC[:, 0, :]), (CO, SC[:, 1, :]), (SE, SD[:, 0, :]), (SO, SD[:, 1, :])):
                    at = 2 if kind in (CO, SO) else 0
                    for kt in range(2):
                        w = slice(kt * 256 + ft * P, kt * 256 + (ft + 1) * P)
                        ins = mm3(bank, t2hi[:, kind, w], t2lo[:, kind, w], zhi[:, at + kt, :],
                                  zlo[:, at + kt, :], kt == 0, kt == 1)
                ins.then_inc(dft_done, 1)

            def inverse(k, i):
                if i == 0:
                    pe.wait_ge(spec_lo, 8 * k + 8)
                if 4 * k + i >= 2:
                    pe.wait_ge(conv_done, 4 * k + i - 1)
                bank = (B2, B3)[i % 2]
                w = slice(i * P, (i + 1) * P)
                for half, terms in enumerate((((0, CEI), (3, SEI)), ((1, CO), (2, SO)))):
                    for a, (e, kind) in enumerate(terms):
                        for ft in range(2):
                            r = slice(ft * 256, (ft + 1) * 256)
                            ins = mm3(bank[:, half * 256:(half + 1) * 256], ghi[:, 2 * e + ft, w],
                                      glo[:, 2 * e + ft, w], t2hi[:, kind, r], t2lo[:, kind, r],
                                      a == 0 and ft == 0, a == 1 and ft == 1)
                ins.then_inc(inv_done, 1)

            for k in range(5):
                if k < 4:
                    transposes(k)
                if k:
                    inverse(k - 1, 0)
                    inverse(k - 1, 1)
                if k < 4:
                    forward(k, 0)
                if k:
                    inverse(k - 1, 2)
                    inverse(k - 1, 3)
                n = 4 * (k + 1)
                hy_unit(n)
                if k < 4:
                    forward(k, 1)
                for s in range(1, 4):
                    hy_unit(n + s)
            out_units(U_OUT1, ghi, glo, lambda k: pe.wait_ge(z3_lo, k + 1))
            boundary(2)
            with pe.Fori(0, QUARTERS) as q:
                quarter(1, q)
            boundary(3)


def even_first(n):
    return np.concatenate([np.arange(0, n, 2), np.arange(1, n, 2)])


def shape_tables():
    f32 = np.float32
    q = P // 4
    rot = np.zeros((P, P), f32)
    for o in range(P):
        quarter, r = divmod(o, q)
        rot[(quarter ^ 1) * q + r, o] = -1.0 if quarter % 2 == 0 else 1.0
    consts = np.stack([np.eye(P, dtype=f32), np.ones((P, P), f32), rot], axis=1)
    t = np.arange(NT)
    nf = HD // 4
    inv = (f32(10000.0) ** (-np.arange(nf, dtype=f32) / f32(nf))).astype(f32)
    ar = (t // GRID_W).astype(f32)[None] * inv[:, None]
    ac = (t % GRID_W).astype(f32)[None] * inv[:, None]
    ang = np.concatenate([ar, ar, ac, ac], axis=0)
    ropes = np.stack([np.cos(ang), np.sin(ang)], axis=1).astype(f32)
    tl = np.linspace(0.0, 1.0, NT, dtype=f32)
    w = (f32(2.0 * math.pi) * np.arange(NT, dtype=f32) / f32(NT)).astype(f32)
    bands = np.linspace(1e-4, 15, 16, dtype=f32)
    bw = (bands[:, None] * w[None]).astype(f32)
    feats = np.concatenate([tl[None], np.cos(bw), -np.sin(bw)], axis=0).astype(f32)
    deltas = np.abs(np.linspace(math.log(1e-2) / 0.3, math.log(1e-2) / 1.5, D, dtype=f32))
    window = np.exp(-tl[:, None] * deltas[None]).astype(f32)
    order = even_first(NT)
    window = window[order].reshape(4, P, 2, NT).transpose(2, 0, 1, 3)
    k = np.arange(256)[None]
    m = np.arange(256)[:, None]
    even = np.pi * (2 * k + 1) * (2 * m) / 1024.0
    odd = np.pi * (2 * k + 1) * (2 * m + 1) / 1024.0
    kinds = [np.cos(even), np.cos(odd), np.sin(even), np.sin(odd), np.cos(even).T, np.sin(even).T]
    tables = np.stack([a.astype(f32).reshape(2, P, 256).transpose(1, 0, 2).reshape(P, 512) for a in kinds], axis=1)
    return consts, ropes, np.ascontiguousarray(feats[:, order]), np.ascontiguousarray(window), tables


def units_of(w):
    n = w.shape[1] // P
    return w.reshape(KC, P, n, P).transpose(2, 1, 0, 3).reshape(n, P, D)


def kernel(**inputs):
    import concourse.bacc as bacc
    from concourse.bass_utils import run_bass_kernel_spmd

    a = {k: np.asarray(v) for k, v in inputs.items()}
    f32 = np.float32

    def mlp_units(l):
        w1, w2 = a["mlp_w1"][l], a["mlp_w2"][l]
        parts = []
        for q in range(QUARTERS):
            parts += [units_of(w1[:, q * D:(q + 1) * D]), units_of(w2[q * D:(q + 1) * D])]
        return parts

    win = units_of(a["ga_w_in"][0])
    wpack = np.concatenate([win[10:12], win[8:10], win[0:8], units_of(a["ga_w_out"][0])] + mlp_units(0)
                           + [units_of(a["hy_w_in"][0]), units_of(a["hy_w_out"][0])] + mlp_units(1))
    arows = [a["ada_w"][l].T.reshape(48, P, D) for l in range(2)]
    apack = np.concatenate([units_of(a["ada_w"][0][:, 0:16 * P]), arows[0][16:], arows[1]])

    def chunks(v):
        return v.reshape(-1, P).T

    cols = np.zeros((P, NCOLS), f32)
    cols[:, C_G:C_G + 64] = chunks(a["norm_g"])
    cols[:, C_AB:C_AB + 96] = chunks(a["ada_b"])
    cols[:, C_QG:C_QG + 1] = chunks(a["ga_q_gain"])
    cols[:, C_KG:C_KG + 1] = chunks(a["ga_k_gain"])
    cols[:, C_CW:C_CW + 72] = chunks(a["hy_conv_w"])
    cols[:, C_CB:C_CB + 24] = chunks(a["hy_conv_b"])
    cols[:, C_SK:C_SK + 16] = chunks(a["hy_skip"])
    cols[0:FH, C_F] = a["hy_f_b1"][0]
    cols[0:FH, C_F + 1] = a["hy_f_b2"][0]
    cols[0:FH, C_F + 2:C_F + 4] = a["hy_f_freq"][0].T
    consts, ropes, feats, window, tables = shape_tables()
    cT = np.stack([a["c"][0], a["c_ctx"]], axis=-1).reshape(KC, P, 2).transpose(1, 0, 2)
    arrays = {
        "xT": a["x"][0].T.reshape(KC, P, NT).transpose(1, 0, 2),
        "ctxT": a["ctx"][0].T.reshape(KC, P, NC).transpose(1, 0, 2),
        "cT": cT, "cols": cols, "wpack": wpack, "apack": apack,
        "fw1": a["hy_f_w1"][0], "fw2": a["hy_f_w2"][0], "fw3": a["hy_f_w3"][0].reshape(FH, 8, NT),
        "featsT": feats, "decay": window, "tables": tables, "consts": consts, "ropes": ropes,
    }
    arrays = {k: np.ascontiguousarray(v) for k, v in arrays.items()}
    nc = bacc.Bacc("TRN2", target_bir_lowering=False, num_devices=1)
    args = [nc.dram_tensor(f"in_{k}", v.shape, F32, kind="ExternalInput").ap() for k, v in arrays.items()]
    args.append(nc.dram_tensor("spectra", [8, P, 4, NT], F32, kind="Internal").ap())
    args.append(nc.dram_tensor("outT", [KC, P, NT], F32, kind="ExternalOutput").ap())
    build(nc, *args)
    r = run_bass_kernel_spmd(nc, [{f"in_{k}": v for k, v in arrays.items()}], core_ids=[0])
    o = r.results[0]["outT"]
    return np.ascontiguousarray(o.reshape(D, NT).T)[None]
```

```python
import math
from contextlib import ExitStack

import concourse.bass as bass
import concourse.mybir as mybir
import numpy as np

F32 = mybir.dt.float32
F32R = mybir.dt.float32r
ALU = mybir.AluOpType
ACT = mybir.ActivationFunctionType
AX = mybir.AxisListType

P = 128
D = 1024
KC = D // P
NT = 512
NC = 256
NK = NT + NC
KT = NK // P
HD = 128
NH = 8
NKV = 2
GROUP = NH // NKV
QT = NT // P
EPS = 1e-6
FH = 64
NFEAT = 33
GRID_W = 64
QUARTERS = 4
QKV_ORDER = (0, 1, 2, 3, 8, 9, 4, 5, 6, 7, 10, 11)
QKV_UNITS = len(QKV_ORDER)
UNIT_Q = [QKV_ORDER.index(h) for h in range(NH)]
UNIT_K = [QKV_ORDER.index(NH + g) for g in range(NKV)]
UNIT_V = [QKV_ORDER.index(NH + NKV + g) for g in range(NKV)]
OUT_UNITS = 8
MLP_UNITS = QUARTERS * 16
HY_UNITS = 24
U_QKV = 0
U_OUT0 = U_QKV + QKV_UNITS
U_MLP0 = U_OUT0 + OUT_UNITS
U_HY = U_MLP0 + MLP_UNITS
U_OUT1 = U_HY + HY_UNITS
U_MLP1 = U_OUT1 + OUT_UNITS
UNITS = U_MLP1 + MLP_UNITS
AHEAD = 3
ADA_START = [0, 16, 48, 96]
ADA_RING = 4
ADA_QUARTER = 48 // QUARTERS
C_G, C_AB, C_QG, C_KG = 0, 64, 160, 161
C_CW, C_CB, C_SK, C_F = 162, 234, 258, 274
NCOLS = 280
CE, CO, SE, SO, CEI, SEI = range(6)
TWO_PI_A = 6.28125
TWO_PI_B = float(np.float32(2 * math.pi - 6.28125))
TWO_PI_C = float(np.float32(2 * math.pi - 6.28125 - TWO_PI_B))
MAGIC = 12582912.0


def build(nc, xT, ctxT, cT, cols, wpack, apack, fw1, fw2, fw3, featsT, decay, tables, consts, ropes, fdram, out):
    with ExitStack() as ctx:
        def sb(name, shape, dt=F32, stack=ctx):
            return stack.enter_context(nc.sbuf_tensor(name, shape, dt))

        def sem(name):
            return ctx.enter_context(nc.semaphore(name))

        raw = sb("raw", [P, 2, D])
        with ExitStack() as area:
            afirst = sb("afirst", [P, 4, D], F32, area)
            crows = sb("crows", [P, 2, D], F32, area)
            cdiag = sb("cdiag", [P, 2, D], F32, area)
        whi = sb("whi", [P, 4, D], F32R)
        wlo = sb("wlo", [P, 4, D], F32R)
        araw = sb("araw", [P, 2, D])
        x = sb("x", [P, KC, NT])
        hhi = sb("hhi", [P, KC, NT], F32R)
        hlo = sb("hlo", [P, KC, NT], F32R)
        ghi = sb("ghi", [P, KC, NT], F32R)
        glo = sb("glo", [P, KC, NT], F32R)
        S = sb("scratch", [P, 12, NT])
        cst = sb("consts", [P, 3, P])
        col = sb("cols", [P, NCOLS])
        cs = sb("cs", [P, KC, 2])
        ce = sb("ce", [P, KC, 2])
        mods = sb("mods", [P, 96 + 16])
        gain = sb("gain", [P, 2, 4, KC])
        gainc = sb("gainc", [P, KC])
        nmax = sb("nmax", [P, 2])
        rsum = sb("rsum", [P, 2])
        rinv = sb("rinv", [P, 2])
        asum = sb("asum", [P, ADA_QUARTER])
        qg = sb("qg", [P, 1])
        epst = sb("eps", [P, 1])
        tap2 = sb("tap2", [P, 2, NT])
        ident, ones, rotm = (cst[:, n, :] for n in range(3))
        y = S[:, 0:KC, :]
        with ExitStack() as area:
            thi = sb("thi", [P, 6, NT], F32R, area)
            tlo = sb("tlo", [P, 6, NT], F32R, area)
            fs = sb("fs", [P, 12, NT], F32, area)
        with ExitStack() as area:
            khi = sb("khi", [P, NKV, NK], F32R, area)
            klo = sb("klo", [P, NKV, NK], F32R, area)
            vhi = sb("vhi", [P, KT, NKV, HD], F32R, area)
            vlo = sb("vlo", [P, KT, NKV, HD], F32R, area)
            phi = sb("phi", [P, 2, KT, 2 * P], F32R, area)
            plo = sb("plo", [P, 2, KT, 2 * P], F32R, area)
        with ExitStack() as area:
            sb("below", [P, 4 * NKV * NK], F32, area)
            chi = sb("chi", [P, KC, NC], F32R, area)
            clo = sb("clo", [P, KC, NC], F32R, area)
            ctxs = sb("ctxs", [P, KC, NC], F32, area)
        with ExitStack() as area:
            sb("below3", [P, 4 * NKV * NK + 2 * KC * NC], F32, area)
            vt = sb("vt", [P, NKV, NK], F32, area)
        with ExitStack() as area:
            t2hi = sb("t2hi", [P, 6, NT], F32R, area)
            t2lo = sb("t2lo", [P, 6, NT], F32R, area)
            zhi = sb("zhi", [P, 4, NT], F32R, area)
            zlo = sb("zlo", [P, 4, NT], F32R, area)
            es = sb("es", [P, 4, NT], F32, area)
        with ExitStack() as area:
            sb("below2", [P, 12 * NT], F32, area)
            amore = sb("amore", [P, ADA_RING - 2, D], F32, area)
            crow1 = sb("crow1", [P, D], F32, area)

        AB = ctx.enter_context(nc.psum_tensor("bank01", [P, 2, NT], F32))
        B2 = ctx.enter_context(nc.psum_tensor("bank2", [P, NT], F32))
        B3 = ctx.enter_context(nc.psum_tensor("bank3", [P, NT], F32))
        SC = ctx.enter_context(nc.psum_tensor("bank45", [P, 2, NT], F32))
        SD = ctx.enter_context(nc.psum_tensor("bank67", [P, 2, NT], F32))
        SCD = (SC, SD)

        small_in = sem("small_in")
        x_in = sem("x_in")
        table_in = sem("table_in")
        w3_in = sem("w3_in")
        decay_in = [sem(f"decay_in{n}") for n in range(2)]
        ctx_in = sem("ctx_in")
        rope_in = sem("rope_in")
        table2_in = sem("table2_in")
        filt_in = sem("filt_in")
        filt_out = sem("filt_out")
        raw_in = [sem(f"raw_in{n}") for n in range(2)]
        arow_in = [sem(f"arow_in{n}") for n in range(ADA_RING)]
        ysq_done = sem("ysq_done")
        yss_done = sem("yss_done")
        x_out = sem("x_out")
        hi_done = sem("hi_done")
        lo_done = sem("lo_done")
        unit_done = sem("unit_done")
        evac_done = sem("evac_done")
        eps_set = sem("eps_set")
        silu_e = sem("silu_e")
        silu_done = sem("silu_done")
        adal_done = sem("adal_done")
        mod_done = sem("mod_done")
        cdiag_done = sem("cdiag_done")
        csum_done = sem("csum_done")
        crow_done = sem("crow_done")
        amul_done = sem("amul_done")
        asum_done = sem("asum_done")
        asum1_done = sem("asum1_done")
        bias_done = sem("bias_done")
        sin_arg = sem("sin_arg")
        sin_done = sem("sin_done")
        fmlp_done = sem("fmlp_done")
        thi_done = sem("thi_done")
        tlo_done = sem("tlo_done")
        gen_done = sem("gen_done")
        gen_used = sem("gen_used")
        w3_done = sem("w3_done")
        row0_done = sem("row0_done")
        eo_hi = sem("eo_hi")
        eo_lo = sem("eo_lo")
        fdft_done = sem("fdft_done")
        fodd_done = sem("fodd_done")
        fout_done = sem("fout_done")
        xsq_done = sem("xsq_done")
        xss_done = sem("xss_done")
        csq_done = sem("csq_done")
        css_done = sem("css_done")
        sq_done = sem("sq_done")
        pair_done = sem("pair_done")
        ss_done = sem("ss_done")
        sd_done = sem("sd_done")
        rs_done = sem("rs_done")
        scaled_done = sem("scaled_done")
        x_done = sem("x_done")
        ht_done = sem("ht_done")
        hhi_done = sem("hhi_done")
        h_done = sem("h_done")
        vt_done = sem("vt_done")
        vhi_done = sem("vhi_done")
        vlo_done = sem("vlo_done")
        job_sq = sem("job_sq")
        job_ss = sem("job_ss")
        job_sd = sem("job_sd")
        job_qn = sem("job_qn")
        job_rot = sem("job_rot")
        job_cos = sem("job_cos")
        job_sin = sem("job_sin")
        job_full = sem("job_full")
        job_hi = sem("job_hi")
        job_lo = sem("job_lo")
        score_done = sem("score_done")
        nmax_done = sem("nmax_done")
        exp_done = sem("exp_done")
        p_done = sem("p_done")
        pt_done = sem("pt_done")
        phi_done = sem("phi_done")
        plo_done = sem("plo_done")
        pv_done = sem("pv_done")
        ohi_done = sem("ohi_done")
        olo_done = sem("olo_done")
        g_full = sem("g_full")
        ghi_done = sem("ghi_done")
        g_done = sem("g_done")
        y_done = sem("y_done")
        y_zero = sem("y_zero")
        centre_done = sem("centre_done")
        tap_done = sem("tap_done")
        zt_done = sem("zt_done")
        zhi_done = sem("zhi_done")
        zlo_done = sem("zlo_done")
        dft_done = sem("dft_done")
        odd_done = sem("odd_done")
        spec_free = sem("spec_free")
        filt_used = sem("filt_used")
        mirror_done = sem("mirror_done")
        spec_full = sem("spec_full")
        spec_hi = sem("spec_hi")
        spec_lo = sem("spec_lo")
        inv_done = sem("inv_done")
        skip_done = sem("skip_done")
        conv_done = sem("conv_done")
        z3_hi = sem("z3_hi")
        z3_lo = sem("z3_lo")
        own_act = sem("own_act")
        own_dve = sem("own_dve")
        own_pool = sem("own_pool")

        block = ctx.enter_context(nc.Block())

        FPAIR = ((hhi, hlo), (ghi, glo))
        FE = (fs[:, 8, :], fs[:, 9, :])
        FO = (fs[:, 10, :], S[:, 4, :])
        DEC = (fs[:, 11, :], S[:, 9, :])
        GEN = (AB[:, 0, :], AB[:, 1, :], B2[:, :], B3[:, :])
        JOBS, turn = [], 0
        for u in range(QKV_UNITS):
            if u in UNIT_Q:
                h = UNIT_Q.index(u)
                JOBS.append((u, AB[:, u % 2, :], NT, turn, False, ghi[:, h, :], glo[:, h, :]))
            elif u in UNIT_K:
                g = UNIT_K.index(u)
                JOBS.append((u, SCD[g][:, 0, :], NT, turn, True, khi[:, g, 0:NT], klo[:, g, 0:NT]))
                JOBS.append((u, SCD[g][:, 1, 0:NC], NC, None, True, khi[:, g, NT:NK], klo[:, g, NT:NK]))
            turn += 1
        ROPE = [n for n, job in enumerate(JOBS) if job[3] is not None]

        SCORE = [b[:, :, :].rearrange("p a b -> p (a b)")[:, 0:NK] for b in SCD]
        CSQ = fs[:, 0:4, :].rearrange("p a (b n) -> p (a b) n", b=2)
        CRS = tap2[:, 0, 0:NC]
        CTX_STEPS = {1: range(3), 2: range(3, 6), 3: range(6, KC)}
        XH = [S[:, 4 + j % 4, :] for j in range(KC)]
        YC = [y[:, j, :] for j in range(KC)]
        PROB = [S[:, 2 * n:2 * n + 2, :].rearrange("p a b -> p (a b)")[:, 0:NK] for n in range(2)]
        FP, FP_, FQ, FQ_ = (araw[:, n // 2, n % 2 * NT:(n % 2 + 1) * NT] for n in range(4))
        UNIT_RAW = (es[:, 0, :], tap2[:, 0, :])
        UNIT_TAPS = (es[:, 1, :], tap2[:, 1, :])
        SPEC = (S[:, 10, :], es[:, 2, :], S[:, 11, :], S[:, 8, :])
        XC, XC_, XS, XS_ = (S[:, 8 + n, :] for n in range(4))

        def jobs_of(t):
            return [(n, job) for n, job in enumerate(JOBS) if job[0] == t]

        def split_first(t):
            return any(len(jobs_of(s)) > 1 for s in (t, t - 1, t - 2))

        NQ = NH * QT
        STAGES = [(0, 0), (0, 1), (1, 0), (1, 1)]
        BOUND = [(0, 1, 0, 2, 0, 24), (0, 3, 1, 0, 1, 0), (1, 1, 1, 2, 1, 24), (1, 3, None, None, None, None)]
        NORMS_BEFORE = 2
        FCOL = {n: C_F + n for n in range(4)}

        def f(ap):
            return ap.bitcast(F32)

        crow = S[:, 6:8, :].rearrange("p a b -> p (a b)")

        def arow_slot(a, k):
            if a < ADA_START[1]:
                return afirst[:, k, :]
            if k < 2:
                return araw[:, k, :]
            if a < 48:
                return S[:, 4 + 2 * k:6 + 2 * k, :].rearrange("p a b -> p (a b)")
            return amore[:, k - 2, :]

        def gcol(l, n, j):
            return gain[:, l, n, j:j + 1]

        def shift(l, t, j, v=0):
            return mods[:, 96 * v + 48 * l + t + j:96 * v + 48 * l + t + j + 1]

        class Own:

            def __init__(self, eng, s):
                self.eng, self.s, self.n = eng, s, 0

            def __call__(self, ins):
                self.wait(self.mark(ins))

            def mark(self, ins):
                self.n += 1
                ins.then_inc(self.s, 1)
                return self.n

            def wait(self, n):
                self.eng.wait_ge(self.s, n)

        def complex_product(own, op, t, c, s, fp, fq):
            m = own.mark(op(t, c, fp, ALU.mult))
            own.wait(m)
            m = own.mark(op(c, c, fq, ALU.mult))
            n = own.mark(op(fp, s, fp, ALU.mult))
            own.wait(m)
            m = own.mark(op(fq, s, fq, ALU.mult))
            own.wait(n)
            last = op(c, c, fp, ALU.add)
            return m, last

        @block.sync
        def _(sp):
            sp.dma_start(cst[:, :, :], consts).then_inc(small_in, 16)
            sp.dma_start(col[:, :], cols).then_inc(small_in, 16)
            sp.dma_start(cs[:, :, :], cT).then_inc(small_in, 16)
            sp.dma_start(S[0:NFEAT, 6, :], featsT).then_inc(small_in, 16)
            sp.dma_start(S[0:NFEAT, 10, 0:FH], fw1).then_inc(small_in, 16)
            sp.dma_start(S[0:FH, 10, FH:2 * FH], fw2).then_inc(small_in, 16)
            sp.dma_start(fs[0:FH, 0:8, :], fw3).then_inc(w3_in, 16)
            sp.dma_start(S[:, 0:6, :], tables).then_inc(table_in, 16)

            def load_decay(n):
                q, tt = divmod(n, 4)
                if n >= 2:
                    sp.wait_ge(gen_used, 2 * n - 2)
                sp.dma_start(DEC[n % 2], decay[q // 2, tt]).then_inc(decay_in[n % 2], 16)

            def load_ada(a):
                if ADA_RING <= a < 16:
                    sp.wait_ge(adal_done, a - ADA_RING + 1)
                sp.dma_start(arow_slot(a, a % ADA_RING), apack[a]).then_inc(arow_in[a % ADA_RING], 16)

            def load_unit(u, s):
                sp.wait_ge(hi_done, u - 1)
                sp.wait_ge(lo_done, u - 1)
                sp.dma_start(raw[:, s, :], wpack[u]).then_inc(raw_in[s], 16)

            load_decay(0)
            for a in range(ADA_RING):
                load_ada(a)
            sp.wait_ge(sin_done, 2)
            load_decay(1)
            sp.dma_start(x[:, :, :], xT).then_inc(x_in, 16)
            for q in range(5):
                for ft in range(2):
                    for n in (4 * q + 2 * ft + 2, 4 * q + 2 * ft + 3):
                        if n < 16:
                            load_decay(n)
                        if n + 2 < 16:
                            load_ada(n + 2)
                    if q == 0:
                        sp.dma_start(raw[:, ft, :], wpack[ft]).then_inc(raw_in[ft], 16)
                    else:
                        m = 2 * (q - 1) + ft
                        if m == 5:
                            sp.wait_ge(eo_lo, 32)
                            sp.dma_start(ctxs[:, :, :], ctxT).then_inc(ctx_in, 16)
                        if m == 7:
                            load_unit(2, 0)
                            load_unit(3, 1)
                        sp.wait_ge(fout_done, 4 * m + 4)
                        sp.dma_start(fdram[m], S[:, 0:4, :]).then_inc(filt_out, 16)

            def load_units(u0, u1):
                if u0 % 2:
                    load_unit(u0, 1)
                    u0 += 1
                with sp.Fori(0, (u1 - u0) // 2) as i:
                    for s in range(2):
                        load_unit(u0 + 2 * i + s, s)
                if u1 % 2:
                    load_unit(u1 - 1, 0)

            load_units(4, U_OUT0 + 5)
            sp.wait_ge(job_sin, len(ROPE))
            sp.wait_ge(job_cos, len(ROPE))
            sp.wait_ge(job_lo, len(JOBS))
            for a in range(16, 48):
                if a >= 16 + ADA_RING:
                    sp.wait_ge(asum_done, a - ADA_RING + 1)
                sp.dma_start(arow_slot(a, a % ADA_RING), apack[a]).then_inc(arow_in[a % ADA_RING], 16)
            load_units(U_OUT0 + 5, U_MLP0 + 5)
            sp.wait_ge(asum_done, 48)
            sp.wait_ge(olo_done, NQ // 2)
            for k in range(ADA_RING):
                sp.dma_start(arow_slot(48, k), apack[48 + k]).then_inc(arow_in[k], 16)

            def load_quarter(q, last=False):
                for s in range(16):
                    load_unit(U_MLP0 + 5 + 16 * q + s, (s + 1) % 2)
                    if s < ADA_QUARTER - (ADA_RING if last else 0):
                        sp.wait_ge(asum1_done, ADA_QUARTER * q + s + 1)
                        sp.dma_start(arow_slot(48, s % ADA_RING),
                                     apack[48 + ADA_RING + ADA_QUARTER * q + s]).then_inc(arow_in[s % ADA_RING], 16)

            with sp.Fori(0, QUARTERS - 1) as q:
                load_quarter(q)
            load_quarter(QUARTERS - 1, last=True)
            load_units(U_HY + 5, UNITS)
            for j in range(KC):
                sp.wait_ge(x_done, 3 * KC + j + 1)
                sp.dma_start(out[j], x[:, j, :]).then_inc(x_out, 16)
            sp.wait_ge(filt_out, 8 * 16)
            sp.wait_ge(x_out, KC * 16)

        @block.gpsimd
        def _(pool):
            nc.gpsimd.memset(epst[:, :], EPS).then_inc(eps_set, 1)
            pool.dma_start(araw[:, :, 0:NT], ropes).then_inc(rope_in, 16)

            def x_squares(j):
                dst = S[:, 6 + (j == 0), :]
                ins = nc.gpsimd.tensor_tensor(dst, x[:, j, :], x[:, j, :], ALU.mult)
                if j:
                    own(ins)
                    ins = nc.gpsimd.tensor_tensor(S[:, 7, :], S[:, 7, :], S[:, 6, :], ALU.add)
                ins.then_inc(xsq_done, 1)
                pool.wait_ge(xsq_done, j + 1)

            own = Own(pool, own_pool)
            pool.wait_ge(crow_done, 4)
            for a in range(16):
                pool.wait_ge(arow_in[a % ADA_RING], 16 * (a // ADA_RING + 1))
                if a >= 2:
                    pool.wait_ge(asum_done, a - 1)
                nc.gpsimd.tensor_tensor(cdiag[:, a % 2, :], arow_slot(a, a % ADA_RING), crows[:, 1, :],
                                        ALU.mult).then_inc(amul_done, 1)
                if a == 7:
                    pool.wait_ge(x_in, 16)
                    pool.wait_ge(fmlp_done, 2)
                if a >= 8:
                    x_squares(a - 8)
            for m in (6, 7):
                pool.wait_ge(fodd_done, 12 + 4 * (m - 5))
                pool.wait_ge(filt_out, 16 * m)
                for n, (a, b, op) in enumerate(((tap2[:, 0, :], S[:, 10, :], ALU.add),
                                                (tap2[:, 0, :], S[:, 10, :], ALU.subtract),
                                                (tap2[:, 1, :], S[:, 11, :], ALU.add),
                                                (S[:, 11, :], tap2[:, 1, :], ALU.subtract))):
                    nc.gpsimd.tensor_tensor(S[:, n, :], a, b, op).then_inc(fout_done, 1)
            pool.wait_ge(rope_in, 16)
            PT = nc.gpsimd.tensor_tensor

            def lo_part(u):
                pool.wait_ge(hi_done, u + 1)
                PT(wlo[:, u % 4, :], raw[:, u % 2, :], f(whi[:, u % 4, :]), ALU.subtract).then_inc(lo_done, 1)

            pool.wait_ge(lo_done, AHEAD)
            for t in range(QKV_UNITS):
                lo_part(t + AHEAD)
                for n, job in jobs_of(t - 1):
                    if job[3] is not None:
                        r = job[3]
                        pool.wait_ge(job_qn, n + 1)
                        if r >= 2:
                            pool.wait_ge(job_lo, ROPE[r - 2] + 1)
                        PT(S[:, 10 + r % 2, :], S[:, 8 + n % 2, :], araw[:, 0, 0:NT], ALU.mult).then_inc(job_cos, 1)
            pool.wait_ge(crow_done, 5)
            for a in range(16, 48):
                pool.wait_ge(arow_in[a % ADA_RING], 16 * (a // ADA_RING + 1))
                slot = arow_slot(a, a % ADA_RING)
                nc.gpsimd.tensor_tensor(slot, slot, crow, ALU.mult).then_inc(amul_done, 1)

            def y_squares(b):
                for j in range(KC):
                    if b == 0 and j in (0, 2, 4):
                        third = j // 2
                        if third:
                            pool.wait_ge(tlo_done, third + 1)
                        else:
                            pool.wait_ge(asum_done, 48)
                        pool.dma_start(S[:, 8:10, :], tables[:, 2 * third:2 * third + 2, :]).then_inc(table2_in, 16)
                    if b % 2 == 0:
                        pool.wait_ge(evac_done, (U_OUT0, U_OUT1)[b // 2] + j + 1)
                    else:
                        pool.wait_ge(y_done, b // 2 * 32 + 24 + j + 1)
                    dst = S[:, 10 + (j == 0), :]
                    ins = nc.gpsimd.tensor_tensor(dst, y[:, j, :], y[:, j, :], ALU.mult)
                    if 0 < j < KC - 1:
                        own(ins)
                        ins = nc.gpsimd.tensor_tensor(S[:, 11, :], S[:, 11, :], S[:, 10, :], ALU.add)
                    ins.then_inc(ysq_done, 1)
                    pool.wait_ge(ysq_done, b * KC + j + 1)

            def x_pairs(b):
                for i in range(KC // 2):
                    pool.wait_ge(sq_done, b * KC + 2 * i + 2)
                    nc.gpsimd.tensor_tensor(y[:, 2 * i, :], y[:, 2 * i, :], y[:, 2 * i + 1, :],
                                            ALU.add).then_inc(pair_done, 1)

            y_squares(0)
            x_pairs(0)
            pool.wait_ge(h_done, 3 * KC)
            nc.gpsimd.memset(y, 0.0).then_inc(y_zero, 1)
            pool.wait_ge(g_done, 32)
            y_squares(1)
            x_pairs(1)
            pool.wait_ge(asum1_done, 48)
            def load_spectrum(m):
                o, c = STAGES[m // 2]
                if m:
                    pool.wait_ge(filt_used, m)
                else:
                    pool.wait_ge(filt_out, 8 * 16)
                pool.dma_start(araw[:, :, :].rearrange("p a (b n) -> p (a b) n", b=2),
                               fdram[2 * (2 * c + o) + m % 2]).then_inc(filt_in, 16)

            def hy_prep(n):
                lo_part(U_HY + n + AHEAD)

            def mirrored(m):
                pool.wait_ge(filt_in, 16 * (m + 1))
                pool.wait_ge(spec_free, m + 1)
                e3 = es[:, 3, :]
                n, last = complex_product(own, PT, e3, XC_, XS_, FP_, FQ_)
                last.then_inc(mirror_done, 1)
                own.wait(n)
                PT(e3, e3, FQ_, ALU.subtract).then_inc(mirror_done, 1)
                pool.wait_ge(mirror_done, 2 * m + 2)

            load_spectrum(0)
            pool.wait_ge(lo_done, U_HY + AHEAD)
            for n in range(4):
                hy_prep(n)
            for k in range(5):
                hy_prep(4 * (k + 1))
                if k < 4:
                    mirrored(2 * k)
                    load_spectrum(2 * k + 1)
                    mirrored(2 * k + 1)
                    if k < 3:
                        load_spectrum(2 * k + 2)
                for s in range(1, 4):
                    hy_prep(4 * (k + 1) + s)
            y_squares(2)
            x_pairs(2)
            pool.wait_ge(h_done, 5 * KC)
            nc.gpsimd.memset(y, 0.0).then_inc(y_zero, 1)
            pool.wait_ge(g_done, 64)
            y_squares(3)

        @block.scalar
        def _(act):
            own = Own(act, own_act)
            A = nc.scalar.activation

            def prep(u, s, r):
                act.wait_ge(raw_in[r], (u - r) * 8 + 16)
                if not isinstance(u, int) or u >= 4:
                    act.wait_ge(unit_done, u - 3)
                A(whi[:, s, :], raw[:, r, :], ACT.Copy).then_inc(hi_done, 1)

            def operand_hi(k, hi, l, t, v, buf, js):
                for j in js:
                    act.wait_ge(ht_done, k * KC + j + 1)
                    A(hi[:, j, :], buf[j], ACT.Identity, bias=shift(l, t, j, v)).then_inc(hhi_done, 1)

            act.wait_ge(small_in, 96)
            A(ce[:, :, :], cs[:, :, :], ACT.Exp, scale=-1.0).then_inc(silu_e, 1)
            for k in range(2):
                act.wait_ge(sin_arg, k + 1)
                A(S[0:FH, 7 + k, :], S[0:FH, 9, :], ACT.Sin).then_inc(sin_done, 1)
                if k == 0:
                    for v in range(2):
                        act.wait_ge(csum_done, 2 * v + 2)
                        A(crows[:, v, :], SCD[v][:, :, :].rearrange("p a b -> p (a b)"), ACT.Copy).then_inc(crow_done, 2)
                    act.wait_ge(table_in, 16)
                    A(thi[:, :, :], S[:, 0:6, :], ACT.Copy).then_inc(thi_done, 1)

            def filter_his(n):
                q, tt = divmod(n, 4)
                hi = FPAIR[q % 2][0]
                if q >= 2:
                    act.wait_ge(fdft_done, 2 * (q - 1))
                if tt == 0:
                    act.wait_ge(row0_done, q + 1)
                else:
                    act.wait_ge(gen_used, 2 * n + 1)
                A(hi[:, tt, :], FE[n % 2], ACT.Copy).then_inc(eo_hi, 1)
                act.wait_ge(gen_used, 2 * n + 2)
                A(hi[:, 4 + tt, :], FO[n % 2], ACT.Copy).then_inc(eo_hi, 1)
                act.wait_ge(amul_done, n + 1)
                A(cdiag[:, n % 2, :], cdiag[:, n % 2, :], ACT.Copy,
                  accum_out=mods[:, 96 + n:97 + n]).then_inc(asum_done, 1)

            def filter_odds(m):
                act.wait_ge(fdft_done, m + 1)
                if m:
                    act.wait_ge(fout_done, 4 * m)
                A(S[:, 10, :], SC[:, 1, :], ACT.Copy).then_inc(fodd_done, 1)
                A(S[:, 11, :], SD[:, 1, :], ACT.Copy).then_inc(fodd_done, 1)
                if m >= 6:
                    A(tap2[:, 0, :], SC[:, 0, :], ACT.Copy).then_inc(fodd_done, 1)
                    A(tap2[:, 1, :], SD[:, 0, :], ACT.Copy).then_inc(fodd_done, 1)

            for q in range(4):
                for ft in range(2):
                    filter_his(4 * q + 2 * ft)
                    filter_his(4 * q + 2 * ft + 1)
                    if q:
                        filter_odds(2 * (q - 1) + ft)

            act.wait_ge(eps_set, 1)
            act.wait_ge(xss_done, 1)
            A(S[:, 9, :], B2[:, :], ACT.Sqrt, scale=1.0 / D, bias=epst[:, 0:1]).then_inc(sd_done, 1)
            act.wait_ge(fdft_done, 6)
            operand_hi(0, hhi, 0, 0, 0, XH, range(2))
            filter_odds(6)
            operand_hi(0, hhi, 0, 0, 0, XH, range(2, KC))
            prep(0, 0, 0)
            prep(1, 1, 1)
            act.wait_ge(ctx_in, 16)
            act.wait_ge(gen_done, 32)
            A(CSQ, ctxs[:, :, :], ACT.Square).then_inc(csq_done, 1)
            filter_odds(7)
            def value_his(t):
                for n, (_, ps, w, r, key, hi, lo) in jobs_of(t):
                    act.wait_ge(job_full, n + 1)
                    A(hi, S[:, 10 + r % 2, :] if r is not None else S[:, 8 + n % 2, 0:w], ACT.Copy).then_inc(job_hi, 1)

            prep(2, 2, 0)
            for t in range(QKV_UNITS + 2):
                if t < QKV_UNITS:
                    prep(t + AHEAD, (t + AHEAD) % 4, (t + AHEAD) % 2)
                if t == 1:
                    act.wait_ge(css_done, KC)
                    A(CRS, B2[:, 0:NC], ACT.Sqrt, scale=1.0 / D, bias=epst[:, 0:1]).then_inc(sd_done, 1)
                if t in CTX_STEPS:
                    operand_hi(1, chi, 0, 0, 1, [ctxs[:, j, :] for j in range(KC)], CTX_STEPS[t])
                for n, (_, ps, w, r, key, hi, lo) in jobs_of(t - 1):
                    act.wait_ge(job_ss, n + 1)
                    if n >= 2:
                        act.wait_ge(job_qn, n - 1)
                    A(S[:, 6 + n % 2, 0:w], B2[:, 0:w], ACT.Sqrt, scale=1.0 / HD, bias=epst[:, 0:1]).then_inc(job_sd, 1)
                if split_first(t):
                    value_his(t - 2)
                if t < QKV_UNITS:
                    act.wait_ge(unit_done, t + 1)
                if t in UNIT_V:
                    g = UNIT_V.index(t)
                    A(vt[:, g, :], SCORE[g], ACT.Copy).then_inc(evac_done, 1)
                for i, (n, (_, ps, w, r, key, hi, lo)) in enumerate(jobs_of(t)):
                    if n >= 2:
                        act.wait_ge(job_ss, n - 1)
                    A(S[:, 4 + n % 2, 0:w], ps, ACT.Square).then_inc(job_sq, 1)
                    if n == 0:
                        act.wait_ge(filt_out, 8 * 16)
                    if n >= 4:
                        act.wait_ge(job_lo, n - 3)
                    ins = A(S[:, n % 4, 0:w], ps, ACT.Copy)
                    if i + 1 < len(jobs_of(t)):
                        own(ins)
                    else:
                        ins.then_inc(evac_done, 1)
                if not split_first(t):
                    value_his(t - 2)
                if t - 1 in UNIT_V:
                    g = UNIT_V.index(t - 1)
                    act.wait_ge(vt_done, g + 1)
                    A(vhi[:, :, g, :].rearrange("p (a b) c -> p a b c", a=2),
                      AB[:, :, 0:3 * P].rearrange("p a (b c) -> p a b c", b=3), ACT.Copy).then_inc(vhi_done, 1)

            for n in range(NQ + 5):
                if n >= 6 and n % 2 == 0:
                    m = (n - 6) // 2
                    act.wait_ge(pv_done, m + 1)
                    A(hhi[:, m // 2, (m % 2) * 2 * P:(m % 2 + 1) * 2 * P], (B2, B3)[m % 2][:, 0:2 * P],
                      ACT.Copy).then_inc(ohi_done, 1)
                m = n - 3
                if 0 <= m < NQ:
                    act.wait_ge(pt_done, m + 1)
                    if m >= 4:
                        act.wait_ge(pv_done, m // 2 - 1)
                    A(phi[:, m // 2 % 2, :, (m % 2) * P:(m % 2 + 1) * P].rearrange("p (a b) c -> p a b c", a=2),
                      AB[:, :, 0:3 * P].rearrange("p a (b c) -> p a b c", b=3), ACT.Copy).then_inc(phi_done, 1)
                m = n - 1
                if 0 <= m < NQ:
                    act.wait_ge(nmax_done, m + 1)
                    if m >= 2:
                        act.wait_ge(pt_done, m - 1)
                    A(PROB[m % 2], SCORE[m % 2], ACT.Exp, bias=nmax[:, m % 2:m % 2 + 1],
                      accum_out=rsum[:, m % 2:m % 2 + 1]).then_inc(exp_done, 1)
                if n == 1:
                    act.wait_ge(csum_done, 5)
                    A(crow, AB[:, :, :].rearrange("p a b -> p (a b)"), ACT.Copy).then_inc(crow_done, 1)
                a = n - 4
                if 0 <= a < 32:
                    act.wait_ge(amul_done, a + 17)
                    slot = arow_slot(16, a % ADA_RING)
                    A(slot, slot, ACT.Copy, accum_out=mods[:, 16 + a:17 + a]).then_inc(asum_done, 1)

            act.wait_ge(olo_done, NQ // 2)
            A(crow1[:, :], crow, ACT.Copy).then_inc(crow_done, 1)
            act.wait_ge(crow_done, 6)
            def out_units(u0):
                for j in range(OUT_UNITS):
                    u = u0 + j
                    prep(u + AHEAD, (j + AHEAD) % 4, (j + AHEAD) % 2)
                    act.wait_ge(unit_done, u + 1)
                    A(y[:, j, :], AB[:, j % 2, :], ACT.Copy).then_inc(evac_done, 1)
                    if u0 == U_OUT0 and j in (1, 3, 5):
                        third = j // 2
                        act.wait_ge(table2_in, 16 * (third + 1))
                        A(t2hi[:, 2 * third:2 * third + 2, :], S[:, 8:10, :], ACT.Copy).then_inc(thi_done, 1)

            def boundary(b):
                nb = 2 * b + NORMS_BEFORE
                act.wait_ge(yss_done, b + 1)
                act.wait_ge(tlo_done, 4)
                A(S[:, 8, :], B2[:, :], ACT.Sqrt, scale=1.0 / D, bias=epst[:, 0:1]).then_inc(sd_done, 1)
                if b == 3:
                    return
                for j in range(KC):
                    act.wait_ge(x_done, b * KC + j + 1)
                    A(y[:, j, :], x[:, j, :], ACT.Square).then_inc(sq_done, 1)
                act.wait_ge(ss_done, KC // 2 * (b + 1))
                A(S[:, 9, :], B2[:, :], ACT.Sqrt, scale=1.0 / D, bias=epst[:, 0:1]).then_inc(sd_done, 1)
                operand_hi(b + 2, hhi, BOUND[b][4], BOUND[b][5], 0, YC, range(KC))

            def quarter(l, q, last=False):
                u0 = (U_MLP0, U_MLP1)[l] + 16 * q
                c0 = l * 32 + 8 * q
                for j in range(8):
                    prep(u0 + j + AHEAD, (j + AHEAD) % 4, (j + AHEAD) % 2)
                    act.wait_ge(unit_done, u0 + j + 1)
                    if j < 2:
                        if not isinstance(c0, int) or c0:
                            act.wait_ge(y_done, c0)
                            act.wait_ge(g_done, c0)
                    else:
                        act.wait_ge(g_done, c0 + j - 1)
                    A(S[:, 8 + j % 2, :], AB[:, j % 2, :], ACT.Relu).then_inc(evac_done, 1)
                    act.wait_ge(evac_done, u0 + j + 1)
                    A(S[:, 10 + j % 2, :], S[:, 8 + j % 2, :], ACT.Square).then_inc(g_full, 1)
                    act.wait_ge(g_full, c0 + j + 1)
                    A(ghi[:, j, :], S[:, 10 + j % 2, :], ACT.Copy).then_inc(ghi_done, 1)
                for j in range(8):
                    u = u0 + 8 + j
                    if not last or u + AHEAD < UNITS:
                        prep(u + AHEAD, (j + AHEAD) % 4, (j + AHEAD) % 2)
                    act.wait_ge(unit_done, u + 1)
                    if j >= 2:
                        act.wait_ge(y_done, c0 + j - 1)
                    A(S[:, 8 + j % 2, :], AB[:, j % 2, :], ACT.Copy).then_inc(evac_done, 1)

            out_units(U_OUT0)
            boundary(0)
            quarter(0, 0)
            with act.Fori(1, QUARTERS) as q:
                quarter(0, q)
            boundary(1)

            def hy_unit(n):
                u = U_HY + n
                act.wait_ge(unit_done, u + 1)
                if n >= 2:
                    act.wait_ge(tap_done, n - 1)
                A(UNIT_RAW[n % 2], AB[:, n % 2, :], ACT.Copy).then_inc(evac_done, 1)
                act.wait_ge(evac_done, u + 1)
                centre = y[:, n, :] if n < KC else UNIT_TAPS[n % 2]
                A(centre, UNIT_RAW[n % 2], ACT.Identity, scale=col[:, C_CW + 24 + n:C_CW + 25 + n],
                  bias=col[:, C_CB + n:C_CB + n + 1]).then_inc(centre_done, 1)

            def hy_prep(n):
                u = U_HY + n + AHEAD
                prep(u, u % 4, u % 2)

            for n in range(4):
                hy_prep(n)
                hy_unit(n)
            def z_hi(k):
                for tt in range(4):
                    act.wait_ge(zt_done, 4 * k + tt + 1)
                    A(zhi[:, tt, :], SCD[tt // 2][:, tt % 2, :], ACT.Copy).then_inc(zhi_done, 1)

            def skip(k):
                o, c = STAGES[k]
                for j in range(4 * c, 4 * c + 4):
                    A(y[:, j, :], y[:, j, :], ACT.Copy,
                      scale=col[:, C_SK + 8 * o + j:C_SK + 8 * o + j + 1]).then_inc(skip_done, 1)

            def odd_halves(m):
                act.wait_ge(dft_done, m + 1)
                if m:
                    act.wait_ge(spec_lo, 4 * m)
                A(S[:, 9, :], SC[:, 1, :], ACT.Copy).then_inc(odd_done, 1)
                A(S[:, 10, :], SD[:, 1, :], ACT.Copy).then_inc(odd_done, 1)

            def spectrum_hi(m):
                if m % 2 == 0 and m:
                    act.wait_ge(inv_done, 2 * m)
                for i, e in enumerate((0, 2, 1, 3)):
                    act.wait_ge(spec_full, 4 * m + i + 1)
                    A(ghi[:, 2 * e + m % 2, :], SPEC[e], ACT.Copy).then_inc(spec_hi, 1)

            for k in range(4):
                z_hi(k)
                n = 4 * (k + 1)
                if k:
                    hy_prep(n - 1)
                hy_prep(n)
                skip(k)
                if k == 0:
                    hy_unit(n)
                odd_halves(2 * k)
                if k == 0:
                    hy_prep(n + 1)
                    hy_unit(n + 1)
                spectrum_hi(2 * k)
                odd_halves(2 * k + 1)
                if k:
                    hy_unit(n)
                    hy_prep(n + 1)
                    hy_unit(n + 1)
                hy_prep(n + 2)
                if k:
                    spectrum_hi(2 * k + 1)
                hy_unit(n + 2)
                hy_unit(n + 3)
                if k == 0:
                    spectrum_hi(1)
            hy_prep(19)

            def z3_his(j):
                A(ghi[:, j, :], y[:, j, :], ACT.Copy).then_inc(z3_hi, 1)

            for i in range(4):
                hy_prep(20 + i)
                hy_unit(20 + i)
                if i == 0:
                    act.wait_ge(inv_done, 16)
                act.wait_ge(tap_done, 21 + i)
                z3_his(i)
                z3_his(4 + i)
            act.wait_ge(z3_lo, KC)
            out_units(U_OUT1)
            boundary(2)
            with act.Fori(0, QUARTERS - 1) as q:
                quarter(1, q)
            quarter(1, QUARTERS - 1, last=True)
            boundary(3)

        @block.vector
        def _(dve):
            own = Own(dve, own_dve)
            TT = nc.vector.tensor_tensor
            STT = nc.vector.scalar_tensor_tensor
            TS = nc.vector.tensor_scalar

            def prep(u, s, r):
                dve.wait_ge(hi_done, u + 1)
                TT(wlo[:, s, :], raw[:, r, :], f(whi[:, s, :]), ALU.subtract).then_inc(lo_done, 1)

            def inverse_root(nb, dst, w):
                dve.wait_ge(sd_done, nb + 1)
                nc.vector.reciprocal(dst[:, 0:w], dst[:, 0:w]).then_inc(rs_done, 1)
                dve.wait_ge(rs_done, nb + 1)

            def operand(k, src, buf, rs, gains, hi, lo, l, t, v, js):
                w = hi.shape[2]

                def lo_part(j):
                    dve.wait_ge(hhi_done, k * KC + j + 1)
                    STT(lo[:, j, :], buf[j], shift(l, t, j, v), f(hi[:, j, :]), ALU.add,
                        ALU.subtract).then_inc(h_done, 1)

                for j in js:
                    if k == 0 and j >= 4:
                        dve.wait_ge(h_done, j - 3)
                    STT(buf[j], src[:, j, :], gains[:, j:j + 1], rs[:, 0:w], ALU.mult,
                        ALU.mult).then_inc(ht_done, 1)
                    if j > js[0]:
                        lo_part(j - 1)
                lo_part(js[-1])

            def modulation(b):
                a, a1 = ADA_START[b], ADA_START[b + 1]
                l = a // 48
                bias = col[:, C_AB + a:C_AB + a1]
                if b == 0:
                    dve.wait_ge(asum_done, 16)
                    dve.wait_ge(adal_done, 16)
                    for v in range(2):
                        own(TT(mods[:, 96 * v:96 * v + 16], mods[:, 96 * v:96 * v + 16], bias, ALU.add))
                elif b == 1:
                    dve.wait_ge(asum_done, 48)
                    own(TT(mods[:, a:a1], mods[:, a:a1], bias, ALU.add))

                def scaled(dst, m, g, v=0):
                    at = 96 * v + 48 * l + 8 * m
                    return STT(dst, mods[:, at:at + 8], 1.0, col[:, C_G + 8 * g:C_G + 8 * g + 8], ALU.add, ALU.mult)

                def gated(dst, m, g):
                    at = 48 * l + 8 * m
                    return TT(dst, mods[:, at:at + 8], col[:, C_G + 8 * g:C_G + 8 * g + 8], ALU.mult)

                if b == 0:
                    own(scaled(gainc[:, :], 1, 0, 1))
                if b != 1:
                    last = scaled(gain[:, l, 0, :], 1, 4 * l)
                if b:
                    if b == 2:
                        own(last)
                    own(gated(gain[:, l, 1, :], 2, 4 * l + 1))
                    own(scaled(gain[:, l, 2, :], 4, 4 * l + 2))
                    last = gated(gain[:, l, 3, :], 5, 4 * l + 3)
                last.then_inc(mod_done, 1)
                dve.wait_ge(mod_done, b + 1)

            dve.wait_ge(silu_e, 1)
            own(nc.vector.tensor_scalar_add(ce[:, :, :], ce[:, :, :], 1.0))
            own(nc.vector.reciprocal(ce[:, :, :], ce[:, :, :]))
            TT(ce[:, :, :], ce[:, :, :], cs[:, :, :], ALU.mult).then_inc(silu_done, 1)
            dve.wait_ge(silu_done, 1)
            for v in range(2):
                for k in range(KC):
                    TS(cdiag[:, v, k * P:(k + 1) * P], ident, ce[:, k, v:v + 1], None, ALU.mult).then_inc(cdiag_done, 1)
            nc.vector.tensor_scalar_mul(qg[:, :], col[:, C_QG:C_QG + 1], HD ** -0.5)

            dve.wait_ge(w3_in, 16)
            w3 = fs[0:FH, 0:8, :].rearrange("p (o d c) n -> p o d c n", o=2, d=2)
            for o in range(2):
                TT(w3[:, o, 0], w3[:, o, 0], w3[:, o, 1], ALU.add).then_inc(w3_done, 1)
            for o in range(2):
                dve.wait_ge(w3_done, o + 1)
                STT(w3[:, o, 1], w3[:, o, 1], -2.0, w3[:, o, 0], ALU.mult, ALU.add).then_inc(w3_done, 1)

            arg, turns = S[0:FH, 9, :], S[0:FH, 11, :]
            for k in range(2):
                dve.wait_ge(fmlp_done, k + 1)
                if k:
                    dve.wait_ge(sin_done, 1)
                own(TS(arg, B2[0:FH, :], col[0:FH, FCOL[k]:FCOL[k] + 1], col[0:FH, FCOL[2 + k]:FCOL[2 + k] + 1],
                       ALU.add, ALU.mult))
                own(TS(turns, arg, 1.0 / (2 * math.pi), MAGIC, ALU.mult, ALU.add))
                own(nc.vector.tensor_scalar_add(turns, turns, -MAGIC))
                for part in (TWO_PI_A, TWO_PI_B, TWO_PI_C):
                    own(STT(arg, turns, -part, arg, ALU.mult, ALU.add))
                TS(arg, arg, 3.1415925, -3.1415925, ALU.min, ALU.max).then_inc(sin_arg, 1)
            dve.wait_ge(thi_done, 1)
            TT(tlo[:, :, :], S[:, 0:6, :], f(thi[:, :, :]), ALU.subtract).then_inc(tlo_done, 1)
            dve.wait_ge(tlo_done, 1)

            def filter_tile(n):
                tt = n % 4
                dve.wait_ge(decay_in[n % 2], 16 * (n // 2 + 1))
                for d, dst in enumerate((FE[n % 2], FO[n % 2])):
                    dve.wait_ge(gen_done, 2 * n + d + 1)
                    if n >= 2:
                        dve.wait_ge(eo_lo, 2 * n - 3 + d)
                    TT(dst, GEN[(2 * n + d) % 4], DEC[n % 2], ALU.mult).then_inc(gen_used, 1)
                if tt == 0:
                    dve.wait_ge(gen_used, 2 * n + 2)
                    e0 = FE[n % 2][0:1, :]
                    own(TT(e0, e0, FO[n % 2][0:1, :], ALU.add))
                    nc.vector.tensor_scalar_mul(e0, e0, 0.5).then_inc(row0_done, 1)
                    dve.wait_ge(row0_done, n // 4 + 1)

            def modulate_latent(a):
                dve.wait_ge(amul_done, a + 1)
                dve.wait_ge(arow_in[a % ADA_RING], 16 * (a // ADA_RING + 1))
                slot = arow_slot(a, a % ADA_RING)
                nc.vector.tensor_tensor_reduce(slot, slot, crows[:, 0, :], 1.0, 0.0, ALU.mult, ALU.add,
                                               mods[:, a:a + 1]).then_inc(adal_done, 1)

            def filter_los(n):
                q, tt = divmod(n, 4)
                hi, lo = FPAIR[q % 2]
                dve.wait_ge(eo_hi, 2 * n + 1)
                TT(lo[:, tt, :], FE[n % 2], f(hi[:, tt, :]), ALU.subtract).then_inc(eo_lo, 1)
                dve.wait_ge(eo_hi, 2 * n + 2)
                TT(lo[:, 4 + tt, :], FO[n % 2], f(hi[:, 4 + tt, :]), ALU.subtract).then_inc(eo_lo, 1)

            def filter_outs(m):
                dve.wait_ge(fodd_done, 2 * m + 2)
                if m:
                    dve.wait_ge(filt_out, 16 * m)
                TT(S[:, 0, :], SC[:, 0, :], S[:, 10, :], ALU.add).then_inc(fout_done, 1)
                TT(S[:, 1, :], SC[:, 0, :], S[:, 10, :], ALU.subtract).then_inc(fout_done, 1)
                TT(S[:, 2, :], SD[:, 0, :], S[:, 11, :], ALU.add).then_inc(fout_done, 1)
                TT(S[:, 3, :], S[:, 11, :], SD[:, 0, :], ALU.subtract).then_inc(fout_done, 1)

            for q in range(4):
                for ft in range(2):
                    n = 4 * q + 2 * ft
                    filter_tile(n)
                    filter_tile(n + 1)
                    filter_los(n)
                    modulate_latent(n)
                    filter_los(n + 1)
                    modulate_latent(n + 1)
                    if q:
                        filter_outs(2 * (q - 1) + ft)

            modulation(0)
            inverse_root(0, S[:, 9, :], NT)
            operand(0, x, XH, S[:, 9, :], gain[:, 0, 0, :], hhi, hlo, 0, 0, 0, range(KC))
            prep(0, 0, 0)
            prep(1, 1, 1)

            def value_lo(n, full, hi, lo):
                dve.wait_ge(job_hi, n + 1)
                TT(lo, full, f(hi), ALU.subtract).then_inc(job_lo, 1)

            prep(2, 2, 0)
            for t in range(QKV_UNITS + 2):
                if t == 1:
                    inverse_root(1, CRS, NC)
                if t in CTX_STEPS:
                    operand(1, ctxs, [ctxs[:, j, :] for j in range(KC)], CRS, gainc, chi, clo, 0, 0, 1, CTX_STEPS[t])
                for n, (_, ps, w, r, key, hi, lo) in jobs_of(t - 2):
                    if r is not None:
                        dve.wait_ge(rope_in, 16)
                        dve.wait_ge(job_rot, r + 1)
                        dve.wait_ge(job_qn, n + 1)
                        TT(S[:, n % 4, :], B3[:, :], araw[:, 1, 0:NT], ALU.mult).then_inc(job_sin, 1)
                        dve.wait_ge(job_sin, r + 1)
                        dve.wait_ge(job_cos, r + 1)
                        full = S[:, 10 + r % 2, :]
                        TT(full, full, S[:, n % 4, :], ALU.add).then_inc(job_full, 1)
                    else:
                        full = S[:, 8 + n % 2, 0:w]
                        dve.wait_ge(job_qn, n + 1)
                        dve.sem_inc(job_full, 1)
                    if split_first(t):
                        value_lo(n, full, hi, lo)
                for n, (_, ps, w, r, key, hi, lo) in jobs_of(t - 1):
                    dve.wait_ge(job_sd, n + 1)
                    own(nc.vector.reciprocal(S[:, 6 + n % 2, 0:w], S[:, 6 + n % 2, 0:w]))
                    dve.wait_ge(evac_done, t)
                    if n >= 2:
                        dve.wait_ge(job_lo, n - 1)
                    g = col[:, C_KG:C_KG + 1] if key else qg[:, 0:1]
                    STT(S[:, 8 + n % 2, 0:w], S[:, n % 4, 0:w], g, S[:, 6 + n % 2, 0:w], ALU.mult,
                        ALU.mult).then_inc(job_qn, 1)
                if not split_first(t):
                    for n, (_, ps, w, r, key, hi, lo) in jobs_of(t - 2):
                        value_lo(n, S[:, 10 + r % 2, :], hi, lo)
                if t - 1 in UNIT_V:
                    g = UNIT_V.index(t - 1)
                    dve.wait_ge(vhi_done, g + 1)
                    for half in range(2):
                        ps = AB[:, half, 0:3 * P].rearrange("p (a b) -> p a b", a=3)
                        TT(vlo[:, 3 * half:3 * half + 3, g, :], ps, f(vhi[:, 3 * half:3 * half + 3, g, :]),
                           ALU.subtract).then_inc(vlo_done, 1)

            for k in range(KC):
                TS(S[:, 4 + k // 4, k % 4 * P:(k % 4 + 1) * P], ident, ce[:, k, 0:1], None,
                   ALU.mult).then_inc(cdiag_done, 1)

            def o_lo(m):
                dve.wait_ge(ohi_done, m + 1)
                cols_ = slice((m % 2) * 2 * P, (m % 2 + 1) * 2 * P)
                TT(hlo[:, m // 2, cols_], (B2, B3)[m % 2][:, 0:2 * P], f(hhi[:, m // 2, cols_]), ALU.subtract).then_inc(olo_done, 1)

            for n in range(NQ + 5):
                m = n - 2
                if 0 <= m < NQ:
                    dve.wait_ge(exp_done, m + 1)
                    if m >= 2:
                        dve.wait_ge(p_done, m - 1)
                    own(nc.vector.reciprocal(rinv[:, m % 2:m % 2 + 1], rsum[:, m % 2:m % 2 + 1]))
                    TS(PROB[m % 2], PROB[m % 2], rinv[:, m % 2:m % 2 + 1], None, ALU.mult).then_inc(p_done, 1)
                m = n - 3
                if 0 <= m < NQ:
                    dve.wait_ge(phi_done, m + 1)
                    for half in range(2):
                        at = slice(3 * half, 3 * half + 3)
                        TT(plo[:, m // 2 % 2, at, (m % 2) * P:(m % 2 + 1) * P],
                           AB[:, half, 0:3 * P].rearrange("p (b c) -> p b c", b=3),
                           f(phi[:, m // 2 % 2, at, (m % 2) * P:(m % 2 + 1) * P]), ALU.subtract).then_inc(plo_done, 1)
                if n < NQ:
                    dve.wait_ge(score_done, n + 1)
                    if n >= 2:
                        dve.wait_ge(exp_done, n - 1)
                    nc.vector.tensor_reduce(out=nmax[:, n % 2:n % 2 + 1], in_=SCORE[n % 2], op=ALU.max,
                                            axis=AX.X, negate=True).then_inc(nmax_done, 1)
                if n >= 6 and n % 2 == 0:
                    o_lo((n - 6) // 2)
            modulation(1)

            def boundary(b):
                nb = 2 * b + NORMS_BEFORE
                lg, ng, lo_, no_, ls, ts = BOUND[b]
                inverse_root(nb, S[:, 8, :], NT)
                for j in range(KC + 1):
                    if j < KC:
                        STT(y[:, j, :], y[:, j, :], gcol(lg, ng, j), S[:, 8, :], ALU.mult,
                            ALU.mult).then_inc(scaled_done, 1)
                    if j:
                        dve.wait_ge(scaled_done, KC * b + j)
                        TT(x[:, j - 1, :], x[:, j - 1, :], y[:, j - 1, :], ALU.add).then_inc(x_done, 1)
                if b == 3:
                    return
                inverse_root(nb + 1, S[:, 9, :], NT)
                dve.wait_ge(x_done, KC * (b + 1))
                operand(b + 2, x, YC, S[:, 9, :], gain[:, lo_, no_, :], hhi, hlo, ls, ts, 0, range(KC))

            def quarter(l, q, last=False):
                u0 = (U_MLP0, U_MLP1)[l] + 16 * q
                c0 = l * 32 + 8 * q

                def modulate(s):
                    if l == 0 and s < ADA_QUARTER:
                        dve.wait_ge(arow_in[s % ADA_RING], 16 * (13 + 3 * q + s // ADA_RING))
                        slot = arow_slot(48, s % ADA_RING)
                        nc.vector.tensor_tensor_reduce(slot, slot, crow1[:, :], 1.0, 0.0, ALU.mult, ALU.add,
                                                       asum[:, s:s + 1]).then_inc(asum1_done, 1)

                for j in range(8):
                    prep(u0 + j + AHEAD, (j + AHEAD) % 4, (j + AHEAD) % 2)
                    dve.wait_ge(ghi_done, c0 + j + 1)
                    TT(glo[:, j, :], S[:, 10 + j % 2, :], f(ghi[:, j, :]), ALU.subtract).then_inc(g_done, 1)
                    modulate(j)
                for j in range(8):
                    u = u0 + 8 + j
                    if not last or u + AHEAD < UNITS:
                        prep(u + AHEAD, (j + AHEAD) % 4, (j + AHEAD) % 2)
                    dve.wait_ge(evac_done, u + 1)
                    if j == 0:
                        dve.wait_ge(y_zero, l + 1)
                        if not isinstance(c0, int) or c0:
                            dve.wait_ge(y_done, c0)
                    TT(y[:, j, :], y[:, j, :], S[:, 8 + j % 2, :], ALU.add).then_inc(y_done, 1)
                    modulate(8 + j)
                if l == 0:
                    dve.wait_ge(asum1_done, ADA_QUARTER * (q + 1))
                    at = 48 + ADA_QUARTER * q
                    TT(mods[:, bass.ds(at, ADA_QUARTER)], asum[:, :],
                       col[:, bass.ds(C_AB + at, ADA_QUARTER)], ALU.add).then_inc(bias_done, 1)
                    dve.wait_ge(bias_done, q + 1)

            dve.wait_ge(lo_done, U_OUT0 + AHEAD)
            for j in range(OUT_UNITS):
                prep(U_OUT0 + j + AHEAD, (j + AHEAD) % 4, (j + AHEAD) % 2)
                if j in (1, 3, 5):
                    third = j // 2
                    at = slice(2 * third, 2 * third + 2)
                    dve.wait_ge(thi_done, 2 + third)
                    TT(t2lo[:, at, :], S[:, 8:10, :], f(t2hi[:, at, :]), ALU.subtract).then_inc(tlo_done, 1)
            boundary(0)
            dve.wait_ge(crow_done, 6)
            quarter(0, 0)
            with dve.Fori(1, QUARTERS) as q:
                quarter(0, q)
            modulation(2)
            boundary(1)

            def hy_unit(n):
                dve.wait_ge(centre_done, n + 1)
                raw_unit = UNIT_RAW[n % 2]
                dst = y[:, n, :] if n < KC else UNIT_TAPS[n % 2]
                own(STT(dst[:, 1:NT], raw_unit[:, 0:NT - 1], col[:, C_CW + n:C_CW + n + 1], dst[:, 1:NT],
                        ALU.mult, ALU.add))
                ins = STT(dst[:, 0:NT - 1], raw_unit[:, 1:NT], col[:, C_CW + 48 + n:C_CW + 49 + n], dst[:, 0:NT - 1],
                          ALU.mult, ALU.add)
                if n >= KC:
                    own(ins)
                    ins = TT(y[:, n % KC, :], y[:, n % KC, :], dst, ALU.mult)
                ins.then_inc(tap_done, 1)

            def spectrum_sums(m):
                dve.wait_ge(odd_done, 2 * m + 2)
                if m:
                    dve.wait_ge(spec_lo, 4 * m)
                c = own.mark(TT(XC, SC[:, 0, :], XC_, ALU.add))
                s = own.mark(TT(XS_, XS, SD[:, 0, :], ALU.subtract))
                own.wait(c)
                c = own.mark(TT(XC_, SC[:, 0, :], XC_, ALU.subtract))
                own.wait(s)
                s = TT(XS, SD[:, 0, :], XS, ALU.add)
                own.wait(c)
                s.then_inc(spec_free, 1)

            def spectrum_products(m):
                dve.wait_ge(filt_in, 16 * (m + 1))
                dve.wait_ge(spec_free, m + 1)
                e2 = es[:, 2, :]
                n, last = complex_product(own, TT, e2, XC, XS, FP, FQ)
                k = own.mark(last)
                own.wait(n)
                TT(e2, e2, FQ, ALU.subtract).then_inc(filt_used, 1)
                own.wait(k)
                dve.wait_ge(filt_used, m + 1)

            def spectrum_ends(m):
                dve.wait_ge(mirror_done, 2 * m + 2)
                e2, e3 = es[:, 2, :], es[:, 3, :]
                TT(SPEC[0], e2, e3, ALU.add).then_inc(spec_full, 1)
                TT(SPEC[2], XC, XC_, ALU.add).then_inc(spec_full, 1)
                dve.wait_ge(spec_full, 4 * m + 1)
                TT(SPEC[1], e2, e3, ALU.subtract).then_inc(spec_full, 1)
                dve.wait_ge(spec_full, 4 * m + 2)
                TT(SPEC[3], XC, XC_, ALU.subtract).then_inc(spec_full, 1)
                for i, e in enumerate((0, 2, 1, 3)):
                    dve.wait_ge(spec_hi, 4 * m + i + 1)
                    TT(glo[:, 2 * e + m % 2, :], SPEC[e], f(ghi[:, 2 * e + m % 2, :]),
                       ALU.subtract).then_inc(spec_lo, 1)

            for n in range(4):
                hy_unit(n)
            def z_los(k):
                for tt in range(4):
                    dve.wait_ge(zhi_done, 4 * k + tt + 1)
                    TT(zlo[:, tt, :], SCD[tt // 2][:, tt % 2, :], f(zhi[:, tt, :]), ALU.subtract).then_inc(zlo_done, 1)

            def conv(k, i):
                j = 4 * STAGES[k][1] + i
                dve.wait_ge(inv_done, 4 * k + i + 1)
                dve.wait_ge(skip_done, 4 * k + i + 1)
                v = y[:, j, :].rearrange("p (m two) -> p two m", two=2)
                STT(v, (B2, B3)[i % 2][:, :].rearrange("p (two m) -> p two m", two=2), 1.0 / 512, v,
                    ALU.mult, ALU.add).then_inc(conv_done, 1)

            def z3_los(j):
                dve.wait_ge(z3_hi, 2 * (j % 4) + j // 4 + 1)
                TT(glo[:, j, :], y[:, j, :], f(ghi[:, j, :]), ALU.subtract).then_inc(z3_lo, 1)

            for k in range(5):
                if k < 4:
                    z_los(k)
                if k:
                    conv(k - 1, 0)
                if k == 0:
                    hy_unit(4)
                if k < 4:
                    spectrum_sums(2 * k)
                    spectrum_products(2 * k)
                if k == 0:
                    hy_unit(5)
                if k:
                    conv(k - 1, 1)
                    conv(k - 1, 2)
                    conv(k - 1, 3)
                    dve.wait_ge(conv_done, 4 * k)
                if k < 4:
                    spectrum_ends(2 * k)
                    spectrum_sums(2 * k + 1)
                n = 4 * (k + 1)
                for s in range(4):
                    if 0 < k < 4 and s == 2:
                        spectrum_ends(2 * k + 1)
                    if k or s >= 2:
                        hy_unit(n + s)
                    if k == 4:
                        z3_los(s)
                        z3_los(4 + s)
                    if k < 4 and s == 0:
                        spectrum_products(2 * k + 1)
                if k == 0:
                    spectrum_ends(1)
            dve.wait_ge(lo_done, U_OUT1 + AHEAD)
            with dve.Fori(0, OUT_UNITS // 4) as i:
                for s in range(4):
                    prep(U_OUT1 + 4 * i + s + AHEAD, (s + AHEAD) % 4, (s + AHEAD) % 2)
            boundary(2)
            with dve.Fori(0, QUARTERS - 1) as q:
                quarter(1, q)
            quarter(1, QUARTERS - 1, last=True)
            boundary(3)

        @block.tensor
        def _(pe):
            mm = nc.tensor.matmul

            def mm3(o, lh, ll, rh, rl, first, last):
                mm(o, lh, rh, start=first, stop=False)
                mm(o, lh, rl, start=False, stop=False)
                return mm(o, ll, rh, start=False, stop=last)

            def unit_ready(u):
                pe.wait_ge(hi_done, u + 1)
                pe.wait_ge(lo_done, u + 1)
                if not isinstance(u, int) or u >= 2:
                    pe.wait_ge(evac_done, u - 1)

            def unit(u, s, o, hi, lo, chunk_ready=None):
                unit_ready(u)
                for k in range(KC):
                    if chunk_ready:
                        chunk_ready(k)
                    w = slice(k * P, (k + 1) * P)
                    ins = mm3(o, whi[:, s, w], wlo[:, s, w], hi[:, k, :], lo[:, k, :], k == 0, k == KC - 1)
                return ins

            pe.wait_ge(small_in, 96)
            mm(B2[0:FH, :], S[0:NFEAT, 10, 0:FH], S[0:NFEAT, 6, :], start=True, stop=True).then_inc(fmlp_done, 1)
            for v in range(2):
                pe.wait_ge(cdiag_done, KC * (v + 1))
                for half in range(2):
                    mm(SCD[v][:, half, :], ones, cdiag[:, v, half * NT:(half + 1) * NT], start=True,
                       stop=True).then_inc(csum_done, 1)
            pe.wait_ge(sin_done, 1)
            mm(B2[0:FH, :], S[0:FH, 10, FH:2 * FH], S[0:FH, 7, :], start=True, stop=True).then_inc(fmlp_done, 1)
            pe.wait_ge(sin_done, 2)
            pe.wait_ge(w3_in, 16)
            pe.wait_ge(w3_done, 4)
            pe.wait_ge(silu_done, 1)

            def filter_tile(n):
                q, tt = divmod(n, 4)
                for d in range(2):
                    i = 2 * n + d
                    if i >= 4:
                        pe.wait_ge(gen_used, i - 3)
                    mm(GEN[i % 4], S[0:FH, 8, tt * P:(tt + 1) * P], fs[0:FH, (2 * (q % 2) + d) * 2 + q // 2, :],
                       start=True, stop=True).then_inc(gen_done, 1)

            def filter_dft(m):
                q, ft = divmod(m, 2)
                hi, lo = FPAIR[q % 2]
                pe.wait_ge(eo_lo, 8 * q + 8)
                pe.wait_ge(tlo_done, 1)
                if m == 7:
                    pe.wait_ge(fodd_done, 16)
                elif m:
                    pe.wait_ge(fout_done, 4 * m)
                else:
                    pe.wait_ge(crow_done, 4)
                for kind, bank in ((CE, SC[:, 0, :]), (CO, SC[:, 1, :]), (SE, SD[:, 0, :]), (SO, SD[:, 1, :])):
                    at = (4 if kind in (SE, SO) else 0) + (2 if kind in (CO, SO) else 0)
                    for kt in range(2):
                        w = slice(kt * 256 + ft * P, kt * 256 + (ft + 1) * P)
                        ins = mm3(bank, thi[:, kind, w], tlo[:, kind, w], hi[:, at + kt, :],
                                  lo[:, at + kt, :], kt == 0, kt == 1)
                ins.then_inc(fdft_done, 1)

            for q in range(4):
                for ft in range(2):
                    filter_tile(4 * q + 2 * ft)
                    filter_tile(4 * q + 2 * ft + 1)
                    if q:
                        filter_dft(2 * (q - 1) + ft)
            pe.wait_ge(gen_used, 32)
            pe.wait_ge(xsq_done, KC)
            mm(B2[:, :], ones, S[:, 7, :], start=True, stop=True).then_inc(xss_done, 1)
            filter_dft(6)
            filter_dft(7)

            for t in range(QKV_UNITS + 2):
                if t in UNIT_Q:
                    unit(t, t % 4, AB[:, t % 2, :], hhi, hlo,
                         (lambda k: pe.wait_ge(h_done, k + 1)) if t == 0 else None).then_inc(unit_done, 1)
                    if t == 0:
                        pe.wait_ge(csq_done, 1)
                        pe.wait_ge(sd_done, 1)
                        for j in range(KC):
                            mm(B2[:, 0:NC], ones, CSQ[:, j, :], start=j == 0, stop=j == KC - 1).then_inc(css_done, 1)
                elif t < QKV_UNITS:
                    first = t == UNIT_K[0]
                    if first:
                        pe.wait_ge(fodd_done, 20)
                    ps = SCD[(UNIT_K if t in UNIT_K else UNIT_V).index(t)]
                    unit(t, t % 4, ps[:, 0, :], hhi, hlo)
                    unit(t, t % 4, ps[:, 1, 0:NC], chi, clo,
                         (lambda k: pe.wait_ge(h_done, KC + k + 1)) if first else None).then_inc(unit_done, 1)
                if t - 1 in UNIT_V:
                    g = UNIT_V.index(t - 1)
                    pe.wait_ge(evac_done, t)
                    if g:
                        pe.wait_ge(vlo_done, 2 * g)
                    for kt in range(KT):
                        ins = nc.tensor.transpose(AB[:, kt // 3, kt % 3 * P:(kt % 3 + 1) * P],
                                                  vt[:, g, kt * P:(kt + 1) * P], ident)
                    ins.then_inc(vt_done, 1)
                for n, (_, ps, w, r, key, hi, lo) in jobs_of(t - 2):
                    if r is not None:
                        pe.wait_ge(job_qn, n + 1)
                        if r:
                            pe.wait_ge(job_sin, r)
                        mm(B3[:, :], rotm, S[:, 8 + n % 2, :], start=True, stop=True).then_inc(job_rot, 1)
                for n, (_, ps, w, r, key, hi, lo) in jobs_of(t - 1):
                    pe.wait_ge(job_sq, n + 1)
                    if n:
                        pe.wait_ge(job_sd, n)
                    else:
                        pe.wait_ge(sd_done, 2)
                    mm(B2[:, 0:w], ones, S[:, 4 + n % 2, 0:w], start=True, stop=True).then_inc(job_ss, 1)

            def prob_values(m):
                pe.wait_ge(plo_done, 4 * m + 4)
                if m >= 2:
                    pe.wait_ge(olo_done, m - 1)
                g = m // 2 // GROUP
                for kt in range(KT):
                    ins = mm3((B2, B3)[m % 2][:, 0:2 * P], vhi[:, kt, g, :], vlo[:, kt, g, :],
                              phi[:, m % 2, kt, :], plo[:, m % 2, kt, :], kt == 0, kt == KT - 1)
                ins.then_inc(pv_done, 1)

            for n in range(NQ + 4):
                m = n - 3
                if 0 <= m < NQ:
                    pe.wait_ge(p_done, m + 1)
                    if m == 0:
                        pe.wait_ge(crow_done, 5)
                    else:
                        pe.wait_ge(plo_done, 2 * m)
                    for kt in range(KT):
                        ins = nc.tensor.transpose(AB[:, kt // 3, kt % 3 * P:(kt % 3 + 1) * P],
                                                  PROB[m % 2][:, kt * P:(kt + 1) * P], ident)
                    ins.then_inc(pt_done, 1)
                if n < NQ:
                    h, qt = divmod(n, QT)
                    g = h // GROUP
                    if n == 0:
                        pe.wait_ge(job_lo, len(JOBS))
                    if n >= 2:
                        pe.wait_ge(exp_done, n - 1)
                    w = slice(qt * P, (qt + 1) * P)
                    mm3(SCD[n % 2][:, 0, :], ghi[:, h, w], glo[:, h, w], khi[:, g, 0:NT], klo[:, g, 0:NT], True, True)
                    mm3(SCD[n % 2][:, 1, 0:NC], ghi[:, h, w], glo[:, h, w], khi[:, g, NT:NK], klo[:, g, NT:NK],
                        True, True).then_inc(score_done, 1)
                if n == 1:
                    pe.wait_ge(cdiag_done, 3 * KC)
                    pe.wait_ge(vlo_done, 2 * NKV)
                    mm(AB[:, 0, :], ones, S[:, 4, :], start=True, stop=True)
                    mm(AB[:, 1, :], ones, S[:, 5, :], start=True, stop=True).then_inc(csum_done, 1)
                if n >= 5 and n % 2 == 1:
                    prob_values((n - 5) // 2)

            def boundary(b):
                nb = 2 * b + NORMS_BEFORE
                pe.wait_ge(ysq_done, KC * (b + 1) - 1)
                pe.wait_ge(sd_done, nb)
                mm(B2[:, :], ones, S[:, 11, :], start=True, stop=False)
                pe.wait_ge(ysq_done, KC * (b + 1))
                mm(B2[:, :], ones, S[:, 10, :], start=False, stop=True).then_inc(yss_done, 1)
                if b == 3:
                    return
                pe.wait_ge(sd_done, nb + 1)
                for i in range(KC // 2):
                    pe.wait_ge(pair_done, KC // 2 * b + i + 1)
                    mm(B2[:, :], ones, y[:, 2 * i, :], start=i == 0, stop=i == KC // 2 - 1).then_inc(ss_done, 1)

            def out_units(u0, hi, lo, ready):
                with pe.Fori(0, OUT_UNITS // 4) as i:
                    for s in range(4):
                        unit(u0 + 4 * i + s, s, AB[:, s % 2, :], hi, lo,
                             ready if s == 0 else None).then_inc(unit_done, 1)

            def quarter(l, q):
                u0 = (U_MLP0, U_MLP1)[l] + 16 * q
                c0 = l * 32 + 8 * q
                for j in range(8):
                    unit(u0 + j, j % 4, AB[:, j % 2, :], hhi, hlo,
                         (lambda k: pe.wait_ge(h_done, (2 + 2 * l) * KC + k + 1)) if j == 0 else None
                         ).then_inc(unit_done, 1)
                for j in range(8):
                    unit(u0 + 8 + j, j % 4, AB[:, j % 2, :], ghi, glo,
                         (lambda k: pe.wait_ge(g_done, c0 + k + 1)) if j == 0 else None).then_inc(unit_done, 1)

            pe.wait_ge(plo_done, 2 * NQ)
            out_units(U_OUT0, hhi, hlo, lambda k: pe.wait_ge(olo_done, NQ // 2))
            boundary(0)
            with pe.Fori(0, QUARTERS) as q:
                quarter(0, q)
            boundary(1)

            def hy_unit(n):
                u = U_HY + n
                unit(u, u % 4, AB[:, n % 2, :], hhi, hlo,
                     (lambda k: pe.wait_ge(h_done, 3 * KC + k + 1)) if n == 0 else None).then_inc(unit_done, 1)

            for n in range(4):
                hy_unit(n)
            def transposes(k):
                if k:
                    pe.wait_ge(spec_free, 2 * k)
                for i in range(4):
                    pe.wait_ge(tap_done, 4 * k + i + 1)
                    for tt in range(4):
                        at = tt // 2 + 256 * (tt % 2)
                        ins = nc.tensor.transpose(SCD[tt // 2][:, tt % 2, i * P:(i + 1) * P],
                                                  y[:, 4 * STAGES[k][1] + i, at:at + 255:2], ident)
                        if i == 3:
                            ins.then_inc(zt_done, 1)

            def forward(k, ft):
                if ft == 0:
                    pe.wait_ge(zlo_done, 4 * k + 4)
                    pe.wait_ge(tlo_done, 4)
                else:
                    pe.wait_ge(spec_free, 2 * k + 1)
                for kind, bank in ((CE, SC[:, 0, :]), (CO, SC[:, 1, :]), (SE, SD[:, 0, :]), (SO, SD[:, 1, :])):
                    at = 2 if kind in (CO, SO) else 0
                    for kt in range(2):
                        w = slice(kt * 256 + ft * P, kt * 256 + (ft + 1) * P)
                        ins = mm3(bank, t2hi[:, kind, w], t2lo[:, kind, w], zhi[:, at + kt, :],
                                  zlo[:, at + kt, :], kt == 0, kt == 1)
                ins.then_inc(dft_done, 1)

            def inverse(k, i):
                if i == 0:
                    pe.wait_ge(spec_lo, 8 * k + 8)
                if 4 * k + i >= 2:
                    pe.wait_ge(conv_done, 4 * k + i - 1)
                bank = (B2, B3)[i % 2]
                w = slice(i * P, (i + 1) * P)
                for half, terms in enumerate((((0, CEI), (3, SEI)), ((1, CO), (2, SO)))):
                    for a, (e, kind) in enumerate(terms):
                        for ft in range(2):
                            r = slice(ft * 256, (ft + 1) * 256)
                            ins = mm3(bank[:, half * 256:(half + 1) * 256], ghi[:, 2 * e + ft, w],
                                      glo[:, 2 * e + ft, w], t2hi[:, kind, r], t2lo[:, kind, r],
                                      a == 0 and ft == 0, a == 1 and ft == 1)
                ins.then_inc(inv_done, 1)

            for k in range(5):
                if k < 4:
                    transposes(k)
                n = 4 * (k + 1)
                if k in (0, 4):
                    hy_unit(n)
                if k:
                    inverse(k - 1, 0)
                if k < 4:
                    forward(k, 0)
                if k:
                    inverse(k - 1, 1)
                    inverse(k - 1, 2)
                else:
                    hy_unit(n + 1)
                if k < 4:
                    forward(k, 1)
                if k:
                    inverse(k - 1, 3)
                for s in range(2 if k == 0 else k == 4, 4):
                    hy_unit(n + s)
            out_units(U_OUT1, ghi, glo, lambda k: pe.wait_ge(z3_lo, 2 * (k % 4) + k // 4 + 1))
            boundary(2)
            with pe.Fori(0, QUARTERS) as q:
                quarter(1, q)
            boundary(3)


def even_first(n):
    return np.concatenate([np.arange(0, n, 2), np.arange(1, n, 2)])


def shape_tables():
    f32 = np.float32
    q = P // 4
    rot = np.zeros((P, P), f32)
    for o in range(P):
        quarter, r = divmod(o, q)
        rot[(quarter ^ 1) * q + r, o] = -1.0 if quarter % 2 == 0 else 1.0
    consts = np.stack([np.eye(P, dtype=f32), np.ones((P, P), f32), rot], axis=1)
    t = np.arange(NT)
    nf = HD // 4
    inv = (f32(10000.0) ** (-np.arange(nf, dtype=f32) / f32(nf))).astype(f32)
    ar = (t // GRID_W).astype(f32)[None] * inv[:, None]
    ac = (t % GRID_W).astype(f32)[None] * inv[:, None]
    ang = np.concatenate([ar, ar, ac, ac], axis=0)
    ropes = np.stack([np.cos(ang), np.sin(ang)], axis=1).astype(f32)
    tl = np.linspace(0.0, 1.0, NT, dtype=f32)
    w = (f32(2.0 * math.pi) * np.arange(NT, dtype=f32) / f32(NT)).astype(f32)
    bands = np.linspace(1e-4, 15, 16, dtype=f32)
    bw = (bands[:, None] * w[None]).astype(f32)
    feats = np.concatenate([tl[None], np.cos(bw), -np.sin(bw)], axis=0).astype(f32)
    deltas = np.abs(np.linspace(math.log(1e-2) / 0.3, math.log(1e-2) / 1.5, D, dtype=f32))
    window = np.exp(-tl[:, None] * deltas[None]).astype(f32)
    order = even_first(NT)
    window = window[order].reshape(4, P, 2, NT).transpose(2, 0, 1, 3)
    k = np.arange(256)[None]
    m = np.arange(256)[:, None]
    even = np.pi * (2 * k + 1) * (2 * m) / 1024.0
    odd = np.pi * (2 * k + 1) * (2 * m + 1) / 1024.0
    kinds = [np.cos(even), np.cos(odd), np.sin(even), np.sin(odd), np.cos(even).T, np.sin(even).T]
    tables = np.stack([a.astype(f32).reshape(2, P, 256).transpose(1, 0, 2).reshape(P, 512) for a in kinds], axis=1)
    return consts, ropes, np.ascontiguousarray(feats[:, order]), np.ascontiguousarray(window), tables


def units_of(w):
    n = w.shape[1] // P
    return w.reshape(KC, P, n, P).transpose(2, 1, 0, 3).reshape(n, P, D)


def kernel(**inputs):
    import concourse.bacc as bacc
    from concourse.bass_utils import run_bass_kernel_spmd

    a = {k: np.asarray(v) for k, v in inputs.items()}
    f32 = np.float32

    def mlp_units(l):
        w1, w2 = a["mlp_w1"][l], a["mlp_w2"][l]
        parts = []
        for q in range(QUARTERS):
            parts += [units_of(w1[:, q * D:(q + 1) * D]), units_of(w2[q * D:(q + 1) * D])]
        return parts

    win = units_of(a["ga_w_in"][0])
    wpack = np.concatenate([win[list(QKV_ORDER)], units_of(a["ga_w_out"][0])] + mlp_units(0)
                           + [units_of(a["hy_w_in"][0]), units_of(a["hy_w_out"][0])] + mlp_units(1))
    apack = np.concatenate([a["ada_w"][l].T.reshape(48, P, D) for l in range(2)])

    def chunks(v):
        return v.reshape(-1, P).T

    cols = np.zeros((P, NCOLS), f32)
    cols[:, C_G:C_G + 64] = chunks(a["norm_g"])
    cols[:, C_AB:C_AB + 96] = chunks(a["ada_b"])
    cols[:, C_QG:C_QG + 1] = chunks(a["ga_q_gain"])
    cols[:, C_KG:C_KG + 1] = chunks(a["ga_k_gain"])
    cols[:, C_CW:C_CW + 72] = chunks(a["hy_conv_w"])
    cols[:, C_CB:C_CB + 24] = chunks(a["hy_conv_b"])
    cols[:, C_SK:C_SK + 16] = chunks(a["hy_skip"])
    cols[0:FH, C_F] = a["hy_f_b1"][0]
    cols[0:FH, C_F + 1] = a["hy_f_b2"][0]
    cols[0:FH, C_F + 2:C_F + 4] = a["hy_f_freq"][0].T
    consts, ropes, feats, window, tables = shape_tables()
    cT = np.stack([a["c"][0], a["c_ctx"]], axis=-1).reshape(KC, P, 2).transpose(1, 0, 2)
    arrays = {
        "xT": a["x"][0].T.reshape(KC, P, NT).transpose(1, 0, 2),
        "ctxT": a["ctx"][0].T.reshape(KC, P, NC).transpose(1, 0, 2),
        "cT": cT, "cols": cols, "wpack": wpack, "apack": apack,
        "fw1": a["hy_f_w1"][0], "fw2": a["hy_f_w2"][0], "fw3": a["hy_f_w3"][0].reshape(FH, 8, NT),
        "featsT": feats, "decay": window, "tables": tables, "consts": consts, "ropes": ropes,
    }
    arrays = {k: np.ascontiguousarray(v) for k, v in arrays.items()}
    nc = bacc.Bacc("TRN2", target_bir_lowering=False, num_devices=1)
    args = [nc.dram_tensor(f"in_{k}", v.shape, F32, kind="ExternalInput").ap() for k, v in arrays.items()]
    args.append(nc.dram_tensor("spectra", [8, P, 4, NT], F32, kind="Internal").ap())
    args.append(nc.dram_tensor("outT", [KC, P, NT], F32, kind="ExternalOutput").ap())
    build(nc, *args)
    r = run_bass_kernel_spmd(nc, [{f"in_{k}": v for k, v in arrays.items()}], core_ids=[0])
    o = r.results[0]["outT"]
    return np.ascontiguousarray(o.reshape(D, NT).T)[None]
```
